# Optimizing a Trainium2 kernel written in Bass

```python
import math
import jax, jax.numpy as jnp
from jax import lax
import numpy as np

D_MODEL = 1024
BATCH = 1
SEQ = 1024
DEPTH = 1

N_META = 16
MIX_WIDTH = D_MODEL
ATTN_WIDTH = MIX_WIDTH // 2
POOL_WIDTH = MIX_WIDTH - ATTN_WIDTH
ATTN_HEAD_DIM = 64
ATTN_HEADS = ATTN_WIDTH // (2 * ATTN_HEAD_DIM)
ATTN_VALUE_DIM = 2 * ATTN_HEAD_DIM
POOL_WINDOWS = (2, 4, 8, 16)
POOL_GROUPS = len(POOL_WINDOWS)
POOL_GROUP_DIM = POOL_WIDTH // POOL_GROUPS
IN_WIDTH = 3 * ATTN_WIDTH + POOL_WIDTH
N_EXPERTS = 16
EXPERT_CAPACITY_FACTOR = 2
D_FF = 2048
ROPE_THETA = 10000.0
Q_BLOCK = 128
EPS = 1e-6

kernel_name = "hymba_diffattn_pool_ecmoe_block"

def _rms(x, g):
    x32 = x.astype(jnp.float32)
    y = x32 * lax.rsqrt(jnp.mean(x32 * x32, axis=-1, keepdims=True) + EPS)
    return (y * g.astype(jnp.float32)).astype(x.dtype)

def _rope(x, pos):
    half = x.shape[-1] // 2
    freqs = ROPE_THETA ** (-jnp.arange(half, dtype=jnp.float32) / half)
    ang = pos[:, None] * freqs[None, :]
    cos = jnp.cos(ang).astype(x.dtype)
    sin = jnp.sin(ang).astype(x.dtype)
    x1, x2 = x[..., :half], x[..., half:]
    return jnp.concatenate([x1 * cos - x2 * sin, x1 * sin + x2 * cos], axis=-1)

def _diff_attention(q, k, v, lam, lam_init, subln_g):
    B, L = q.shape[0], q.shape[1]
    H, dh, dv = ATTN_HEADS, ATTN_HEAD_DIM, ATTN_VALUE_DIM
    pos = jnp.arange(L, dtype=jnp.float32)
    q = _rope(jnp.transpose(q, (0, 2, 3, 1, 4)), pos)
    k = _rope(jnp.transpose(k, (0, 2, 3, 1, 4)), pos)
    v = jnp.transpose(v, (0, 2, 1, 3))
    n_blk = -(-L // Q_BLOCK)
    Lp = n_blk * Q_BLOCK
    q = jnp.pad(q, ((0, 0), (0, 0), (0, 0), (0, Lp - L), (0, 0)))
    qb = jnp.moveaxis(q.reshape(B, H, 2, n_blk, Q_BLOCK, dh), 3, 0)
    scale = dh ** -0.5

    def one_block(qblk):
        s = jnp.einsum('bhmqd,bhmkd->bhmqk', qblk, k).astype(jnp.float32) * scale
        p = jax.nn.softmax(s, axis=-1)
        a = p[:, :, 0] - lam * p[:, :, 1]
        return jnp.einsum('bhqk,bhkd->bhqd', a.astype(v.dtype), v)

    o = lax.map(one_block, qb)
    o = jnp.moveaxis(o, 0, 2).reshape(B, H, Lp, dv)[:, :, :L]
    o = _rms(o, subln_g) * (1.0 - lam_init)
    return jnp.transpose(o, (0, 2, 1, 3)).reshape(B, L, H * dv)

def _pool_mixer(p, pool_w, pool_scale):
    B, L, _ = p.shape
    p32 = p.astype(jnp.float32)
    cs = jnp.concatenate([jnp.zeros((B, 1, POOL_WIDTH), jnp.float32), jnp.cumsum(p32, axis=1)], axis=1)
    t = jnp.arange(L)
    outs = []
    for g, w in enumerate(POOL_WINDOWS):
        lo = jnp.clip(t - w // 2, 0, L)
        hi = jnp.clip(t + w // 2, 0, L)
        c0, c1 = g * POOL_GROUP_DIM, (g + 1) * POOL_GROUP_DIM
        csg = cs[:, :, c0:c1]
        mean = (csg[:, hi] - csg[:, lo]) / (hi - lo).astype(jnp.float32)[None, :, None]
        outs.append(mean - p32[:, :, c0:c1])
    d = jnp.stack(outs, axis=2).astype(p.dtype)
    y = jnp.einsum('blgc,gcd->blgd', d, pool_w)
    return y.reshape(B, L, POOL_WIDTH) * pool_scale

def _expert_choice_ffn(h, w_router, w_gate, w_up, w_down):
    B, L, D = h.shape
    cap = EXPERT_CAPACITY_FACTOR * L // N_EXPERTS
    aff = jax.nn.softmax(jnp.einsum('bld,de->ble', h, w_router).astype(jnp.float32), axis=-1)
    gates, idx = lax.top_k(jnp.swapaxes(aff, 1, 2), cap)
    xg = jax.vmap(lambda hb, ib: hb[ib])(h, idx)
    a = jax.nn.silu(jnp.einsum('becd,edf->becf', xg, w_gate)) * jnp.einsum('becd,edf->becf', xg, w_up)
    y = jnp.einsum('becf,efd->becd', a, w_down) * gates[..., None].astype(h.dtype)
    return jax.vmap(lambda ib, yb: jnp.zeros((L, D), yb.dtype).at[ib.reshape(-1)].add(yb.reshape(-1, D)))(idx, y)

def setup_inputs(seed: int = 0) -> dict:
    key = jax.random.key(seed)
    ks = jax.random.split(key, 20)
    f32 = jnp.float32
    nrm = lambda k, shape, s: jax.random.normal(k, shape, f32) * s
    gain = lambda k, shape: 1.0 + 0.01 * jax.random.normal(k, shape, f32)
    return {
        "x": nrm(ks[0], (BATCH, SEQ, D_MODEL), 1.0),
        "meta_tokens": nrm(ks[1], (N_META, D_MODEL), 1.0),
        "ln1_g": gain(ks[2], (DEPTH, D_MODEL)),
        "w_in": nrm(ks[3], (DEPTH, D_MODEL, IN_WIDTH), D_MODEL ** -0.5),
        "q_norm_g": gain(ks[4], (DEPTH, ATTN_HEAD_DIM)),
        "k_norm_g": gain(ks[5], (DEPTH, ATTN_HEAD_DIM)),
        "lambda_q1": nrm(ks[6], (DEPTH, ATTN_HEAD_DIM), 0.1),
        "lambda_k1": nrm(ks[7], (DEPTH, ATTN_HEAD_DIM), 0.1),
        "lambda_q2": nrm(ks[8], (DEPTH, ATTN_HEAD_DIM), 0.1),
        "lambda_k2": nrm(ks[9], (DEPTH, ATTN_HEAD_DIM), 0.1),
        "subln_g": gain(ks[10], (DEPTH, ATTN_VALUE_DIM)),
        "pool_w": nrm(ks[11], (DEPTH, POOL_GROUPS, POOL_GROUP_DIM, POOL_GROUP_DIM), POOL_GROUP_DIM ** -0.5),
        "pool_scale": gain(ks[12], (DEPTH, POOL_WIDTH)),
        "w_out": nrm(ks[13], (DEPTH, MIX_WIDTH, D_MODEL), MIX_WIDTH ** -0.5),
        "ln2_g": gain(ks[14], (DEPTH, D_MODEL)),
        "w_router": nrm(ks[15], (DEPTH, D_MODEL, N_EXPERTS), D_MODEL ** -0.5),
        "w_gate": nrm(ks[16], (DEPTH, N_EXPERTS, D_MODEL, D_FF), D_MODEL ** -0.5),
        "w_up": nrm(ks[17], (DEPTH, N_EXPERTS, D_MODEL, D_FF), D_MODEL ** -0.5),
        "w_down": nrm(ks[18], (DEPTH, N_EXPERTS, D_FF, D_MODEL), D_FF ** -0.5),
    }

def reference(x, meta_tokens, ln1_g, w_in, q_norm_g, k_norm_g, lambda_q1, lambda_k1, lambda_q2, lambda_k2,
              subln_g, pool_w, pool_scale, w_out, ln2_g, w_router, w_gate, w_up, w_down):
    B = x.shape[0]
    meta = jnp.broadcast_to(meta_tokens[None].astype(x.dtype), (B, N_META, D_MODEL))
    h = jnp.concatenate([meta, x], axis=1)
    L = h.shape[1]
    for l in range(DEPTH):
        lam_init = 0.8 - 0.6 * math.exp(-0.3 * l)
        hn = _rms(h, ln1_g[l])
        proj = jnp.einsum('bld,dn->bln', hn, w_in[l])
        q = proj[..., :ATTN_WIDTH].reshape(B, L, ATTN_HEADS, 2, ATTN_HEAD_DIM)
        k = proj[..., ATTN_WIDTH:2 * ATTN_WIDTH].reshape(B, L, ATTN_HEADS, 2, ATTN_HEAD_DIM)
        v = proj[..., 2 * ATTN_WIDTH:3 * ATTN_WIDTH].reshape(B, L, ATTN_HEADS, ATTN_VALUE_DIM)
        p = proj[..., 3 * ATTN_WIDTH:]
        q = _rms(q, q_norm_g[l])
        k = _rms(k, k_norm_g[l])
        lam = (jnp.exp(jnp.sum(lambda_q1[l].astype(jnp.float32) * lambda_k1[l].astype(jnp.float32)))
               - jnp.exp(jnp.sum(lambda_q2[l].astype(jnp.float32) * lambda_k2[l].astype(jnp.float32)))
               + lam_init)
        attn = _diff_attention(q, k, v, lam, lam_init, subln_g[l])
        pool = _pool_mixer(p, pool_w[l], pool_scale[l])
        mix = jnp.concatenate([attn, pool], axis=-1)
        h = h + jnp.einsum('blm,md->bld', mix, w_out[l])
        h = h + _expert_choice_ffn(_rms(h, ln2_g[l]), w_router[l], w_gate[l], w_up[l], w_down[l])
    return h[:, N_META:]


_drawn_inputs = setup_inputs


def setup_inputs(seed=0):
    import zlib

    import numpy as np

    out = dict(_drawn_inputs(seed))
    spreads = {}
    factors = {'ln1_g': 4.781,
     'q_norm_g': 8.0,
     'k_norm_g': 7.616,
     'lambda_q1': 11.607,
     'lambda_k2': 22.328,
     'subln_g': 64.0,
     'pool_scale': 21.987,
     'ln2_g': 18.195}
    for name, (base, spread) in spreads.items():
        noise = np.random.default_rng([zlib.crc32(name.encode()), seed]).standard_normal(out[name].shape)
        drawn = base * np.exp(spread * noise) if base else spread * noise
        out[name] = __import__('jax').numpy.asarray(drawn.astype(out[name].dtype))
    for name, factor in factors.items():
        out[name] = (out[name] * factor).astype(out[name].dtype)
    return out
```

```python
from contextlib import ExitStack

import numpy as np
import concourse.bass as bass
from concourse import mybir

F32 = mybir.dt.float32
U32 = mybir.dt.uint32
I32 = mybir.dt.int32
ACT = mybir.ActivationFunctionType
ALU = mybir.AluOpType
AX = mybir.AxisListType

P = 128
D = 1024
SEQ = 1024
META = 16
L = SEQ + META
KD = D // P
NT = -(-L // P)
HEADS = 4
DH = 64
DV = 2 * DH
GROUPS = 4
WINDOWS = (2, 4, 8, 16)
E = 16
FF = 2048
CAP = 2 * L // E
CAPX = CAP - P
EPS = 1e-6
LAM_INIT = 0.2
SCALE = DH ** -0.5
ROWS = [min(P, L - P * t) for t in range(NT)]
OFF = (0, 348, 694)
WID = (348, 346, 346)
CHS, CHW = 346, 348
LS = 3 * CHW
KEY0 = [OFF[c] + P * j for c in range(3) for j in range(3)]
KEYS = [(P, P, WID[c] - 2 * P)[j] for c in range(3) for j in range(3)]
KPOS = [CHW * c + OFF[c] - CHS * c + P * j for c in range(3) for j in range(3)]
PADW = 8
LP = L + 2 * PADW
ROUNDS = -(-CAP // 8)
SLOT = 8 * 512
JB = FF // 512
C_ID, C_BLK, C_SWAP, C_ONE = 0, P, 2 * P, 3 * P
C_EDGE = 4 * P
C_COS = C_EDGE + GROUPS * 16
C_SIN = C_COS + L
C_END = C_SIN + L


def constants():
    c = np.zeros((P, C_END), np.float32)
    p = np.arange(P)
    c[p, C_ID + p] = 1.0
    c[:, C_BLK:C_BLK + P] = (p[:, None] // DH == p[None, :] // DH) / DH
    c[p, C_SWAP + (p ^ (DH // 2))] = 1.0
    c[:, C_ONE:C_ONE + P] = 1.0 / DV
    t = np.arange(L)
    for g, w in enumerate(WINDOWS):
        count = np.minimum(t + w // 2, L) - np.maximum(t - w // 2, 0)
        edge = (w / count).astype(np.float32)
        c[:, C_EDGE + 16 * g:C_EDGE + 16 * g + 8] = edge[:8]
        c[:, C_EDGE + 16 * g + 8:C_EDGE + 16 * g + 16] = edge[-8:]
    half = DH // 2
    freq = np.float32(10000.0) ** (-np.arange(half, dtype=np.float32) / np.float32(half))
    ang = t.astype(np.float32)[None, :] * freq[p % half][:, None]
    c[:, C_COS:C_COS + L] = np.cos(ang)
    c[:, C_SIN:C_SIN + L] = np.sin(ang) * np.where(p % DH < half, -1.0, 1.0)[:, None]
    return c


def block_kernel(nc, x, meta_tokens, ln1_g, w_in, q_norm_g, k_norm_g, lambda_q1, lambda_k1,
                 lambda_q2, lambda_k2, subln_g, pool_w, pool_scale, w_out, ln2_g, w_router,
                 w_gate, w_up, w_down, consts, out):
    sums = nc.dram_tensor("sums", [L, D], F32, kind="Internal").ap()
    table = nc.dram_tensor("table", [L, D], F32, kind="Internal").ap()

    ctx = ExitStack()
    with ctx:
        def sb(name, shape, dt=F32):
            return ctx.enter_context(nc.sbuf_tensor(name, shape, dt))

        def sem(name):
            return ctx.enter_context(nc.semaphore(name))

        ring = sb("ring", [P, 6 * SLOT])
        mix_r = sb("mix_r", [P, KD * L])
        qk_r = sb("qk_r", [P, 2 * HEADS * L])
        v_r = sb("v_r", [P, NT * HEADS * DV])
        trig_r = sb("trig_r", [P, 2 * L])
        tmp_r = sb("tmp_r", [P, 9 * CHW])

        def slot(s):
            return ring[:, s * SLOT:(s + 1) * SLOT]

        def cut(region, at, n, **how):
            part = region[:, at:at + n]
            return part.rearrange("p (a b) -> p a b", **how) if how else part

        def xt(t):
            return ring[:, 4 * SLOT + t * D:4 * SLOT + (t + 1) * D] if t < NT - 1 else v_r[:, 0:D]

        hT = mix_r[:, :].rearrange("p (k t) -> p k t", k=KD)
        w_in_sb = [slot(s).rearrange("p (k n) -> p k n", k=KD) for s in range(4)]
        qT = cut(qk_r, 0, HEADS * L, a=HEADS)
        kT = cut(qk_r, HEADS * L, HEADS * L, a=HEADS)
        v_sb = v_r[:, :].rearrange("p (t n) -> p t n", t=NT)
        cosT, sinT = trig_r[:, 0:L], trig_r[:, L:2 * L]
        sq = [tmp_r[:, i * CHW:(i + 1) * CHW] for i in (0, 1)]
        qg = [tmp_r[:, i * CHW:(i + 1) * CHW] for i in (2, 3, 4)]
        rt = [tmp_r[:, i * CHW:(i + 1) * CHW] for i in (5, 6)]
        ta, tb = (tmp_r[:, i * CHW:(i + 1) * CHW] for i in (7, 8))
        pbuf = cut(ring, 4 * SLOT, GROUPS * LP, a=GROUPS)
        lev = [ring[:, 4 * SLOT + (GROUPS + i) * LP:4 * SLOT + (GROUPS + i + 1) * LP] for i in (0, 1)]
        probs = ring[:, 2 * SLOT:2 * SLOT + 4 * LS].rearrange("p (b m t) -> p b m t", b=2, m=2)
        flat_probs = ring[:, 2 * SLOT:2 * SLOT + 4 * LS]
        aT = cut(ring, 2 * SLOT + 4 * LS, NT * 3 * P, a=NT)
        mixT = hT
        w_out_sb = [slot(s).rearrange("p (k n) -> p k n", k=KD) for s in (0, 1)]
        hx = [cut(qk_r, i * D, D) for i in (0, 1)]
        h2 = [cut(qk_r, (2 + i) * D, D) for i in (0, 1)]
        hn = [cut(qk_r, (4 + i) * D, D) for i in (0, 1)]
        hnT = [cut(qk_r, (6 + i) * D, D, a=KD) for i in (0, 1)]
        g2 = trig_r[:, 0:D]
        affT = trig_r[0:E, D:D + L]
        lgT = tmp_r[0:E, 0:NT * P]
        lg = cut(tmp_r, NT * P, NT * E, a=NT)
        mv, mif, mi = (tmp_r[0:E, at:at + 8 * ROUNDS] for at in (1500, 1700, 1900))
        mi = mi.bitcast(U32)
        xT = cut(mix_r, 0, KD * CAP, a=KD)
        yT = cut(mix_r, KD * CAP, KD * CAP, a=KD)
        aff = cut(mix_r, 2 * KD * CAP, 8 * CAP)
        act_T = aff.rearrange("p (b f c) -> p b f c", b=2, f=4)
        silu = [cut(mix_r, 3 * KD * CAP + i * CAP, CAP) for i in (0, 1)]
        xg, xgx = v_r[:, 0:D], v_r[0:CAPX, D:2 * D]
        y_sb, yx_sb = v_r[:, 2 * D:3 * D], v_r[0:CAPX, 3 * D:4 * D]

        cst = sb("cst", [P, C_COS])
        ident = cst[:, C_ID:C_ID + P]
        blk_mean = cst[:, C_BLK:C_BLK + P]
        swap = cst[:, C_SWAP:C_SWAP + P]
        dv_mean = cst[:, C_ONE:C_ONE + P]
        edge = cst[:, C_EDGE:C_COS].rearrange("p (g c) -> p g c", g=GROUPS)
        poolw = sb("poolw", [P, GROUPS, P])
        wr = sb("wr", [P, KD, E])
        g1 = sb("g1", [P, KD])
        gq = sb("gq", [P, 2])
        sg = sb("sg", [P, 2])
        psc = sb("psc", [P, GROUPS])
        lamv = sb("lamv", [P, 4, DH])
        lamj = sb("lamj", [P, DH])
        lam = sb("lam", [P, 5])
        eps = sb("eps", [P, 1])
        st = sb("st", [P, 4, NT])
        st2 = sb("st2", [P, 4, NT])
        mx = sb("mx", [P, 2, 2])
        nb = sb("nb", [P, 2, 2])
        zs = sb("zs", [P, 2, 4, 2])
        rl = sb("rl", [P, 2])
        sm = sb("sm", [P, 3, NT])
        idx = sb("idx", [P, 2, E], I32)
        gat = sb("gat", [P, 2, E])
        gidx = sb("gidx", [P, 2], I32)
        sidx = sb("sidx", [P, 2], I32)
        gcur = sb("gcur", [P, 2])

        PS = ctx.enter_context(nc.psum_tensor("PS", [P, 8, 512], F32))

        def two_banks(b, rows=P):
            return PS[0:rows, b:b + 2, :].rearrange("p b n -> p (b n)")

        s_cst, s_trig, s_par, s_lam, s_g2 = (sem(n) for n in ("s_cst", "s_trig", "s_par", "s_lam", "s_g2"))
        s_x = [sem(f"s_x{t}") for t in range(NT)]
        s_win = [sem(f"s_win{j}") for j in range(4)]
        s_wout = sem("s_wout")
        eps_set, pad_set = sem("eps_set"), sem("pad_set")
        ssq, var_ready, std_ready, xs_ready, xtr, hT_ready = (
            sem(n) for n in ("ssq", "var_ready", "std_ready", "xs_ready", "xtr", "hT_ready"))
        proj_done, proj_taken, ms_done, sw_done, rt_ready, qk_ready, sq_ready = (
            sem(n) for n in ("proj_done", "proj_taken", "ms_done", "sw_done", "rt_ready", "qk_ready",
                             "sq_ready"))
        dve_chain, pool_chain, pads_set, win_ready, pool_d = (
            sem(n) for n in ("dve_chain", "pool_chain", "pads_set", "win_ready", "pool_d"))
        lam_dot, lam_exp, lam_ready = sem("lam_dot"), sem("lam_exp"), sem("lam_ready")
        scores, nb_ready, exp_done, diff_ready, tr_done, tr_taken, b7_done, b7_taken = (
            sem(n) for n in ("scores", "nb_ready", "exp_done", "diff_ready", "tr_done", "tr_taken",
                             "b7_done", "b7_taken"))
        osq, oms, ort, o_ready = sem("osq"), sem("oms"), sem("ort"), sem("o_ready")
        s_hx = [sem("s_hx0"), sem("s_hx1")]
        wo_done, h2_ready, ssq2, var2, std2, hn_ready, hn_tr, hnT_ready, rout_done, lgT_ready = (
            sem(n) for n in ("wo_done", "h2_ready", "ssq2", "var2", "std2", "hn_ready", "hn_tr",
                             "hnT_ready", "rout_done", "lgT_ready"))
        s_sums, s_table = [sem("s_sums0"), sem("s_sums1")], [sem("s_table0"), sem("s_table1")]
        lg_tr, lg_sub, lg_exp, aff_ready, aff_tr, ids_ready, ids_tr, route_ready = (
            sem(n) for n in ("lg_tr", "lg_sub", "lg_exp", "aff_ready", "aff_tr", "ids_ready",
                             "ids_tr", "route_ready"))
        s_w = [sem(f"s_w{i}") for i in range(6)]
        gidx_set, s_gath, s_gathx, xg_tr, xT_ready = (
            sem(n) for n in ("gidx_set", "s_gath", "s_gathx", "xg_tr", "xT_ready"))
        gu_done, silu_ready, act_ready, down_done, yT_ready, y_tr, y_taken, gcur_set = (
            sem(n) for n in ("gu_done", "silu_ready", "act_ready", "down_done", "yT_ready", "y_tr",
                             "y_taken", "gcur_set"))
        sidx_set, s_scat, s_scatx, s_out = (sem(n) for n in ("sidx_set", "s_scat", "s_scatx", "s_out"))

        STEPS = HEADS * NT
        b7 = []
        pool_left = [(g, c) for g in range(GROUPS) for c in range(3)]
        for s in range(1, STEPS + 1):
            if (s - 1) % 3 == 2:
                b7.append((s, "pv", (s - 1) // 3))
            elif pool_left:
                b7.append((s, "pool", pool_left.pop(0)))
        assert not pool_left
        b7_of = {s: (n, kind, what) for n, (s, kind, what) in enumerate(b7)}
        pv_uses = [n for n, (_, kind, _) in enumerate(b7) if kind == "pv"]

        block = ctx.enter_context(nc.Block())

        @block.sync
        def _(sp):
            sp.dma_start(cst[:], consts[:, 0:C_COS]).then_inc(s_cst, 16)
            for t in range(NT):
                if t == 0:
                    sp.dma_start(xt(0)[0:META, :], meta_tokens).then_inc(s_x[0], 16)
                    sp.dma_start(xt(0)[META:P, :], x[0, 0:P - META, :]).then_inc(s_x[0], 16)
                else:
                    a = P * t - META
                    sp.dma_start(xt(t)[0:ROWS[t], :], x[0, a:a + ROWS[t], :]).then_inc(s_x[t], 16)
            with nc.allow_non_contiguous_dma(reason="small parameters"):
                sp.dma_start(g1[:], ln1_g.rearrange("o (k p) -> p (o k)", p=P)).then_inc(s_par, 16)
                for m in range(2):
                    at = slice(DH * m, DH * m + DH)
                    sp.dma_start(gq[at, 0:1], q_norm_g.rearrange("o p -> p o")).then_inc(s_par, 16)
                    sp.dma_start(gq[at, 1:2], k_norm_g.rearrange("o p -> p o")).then_inc(s_par, 16)
                sp.dma_start(sg[:, 0:1], subln_g.rearrange("o p -> p o")).then_inc(s_par, 16)
                sp.dma_start(psc[:], pool_scale.rearrange("o (g p) -> p (o g)", p=P)).then_inc(s_par, 16)
            for j in range(4):
                sp.dma_start(w_in_sb[j], w_in[0].rearrange("(k p) n -> p k n", p=P)[:, :, 512 * j:512 * j + 512]
                             ).then_inc(s_win[j], 16)
                if j == 0:
                    sp.dma_start(trig_r[:], consts[:, C_COS:C_END]).then_inc(s_trig, 16)
                if j == 1:
                    with nc.allow_non_contiguous_dma(reason="small parameters"):
                        for n, v in enumerate((lambda_q1, lambda_k1, lambda_q2, lambda_k2)):
                            sp.dma_start(lamv[:, n, :], v[0, :].partition_broadcast(P)).then_inc(s_lam, 16)
                        sp.dma_start(poolw[:], pool_w[0].rearrange("g c d -> c g d")).then_inc(s_par, 16)
                        sp.dma_start(wr[:], w_router[0].rearrange("(k p) e -> p k e", p=P)).then_inc(s_par, 16)
            sp.wait_ge(proj_done, 24)
            for half in range(2):
                sp.dma_start(w_out_sb[half], w_out[0].rearrange("(k p) n -> p k n", p=P)[:, :, 512 * half:512 * half + 512]
                             ).then_inc(s_wout, 16)
            sp.wait_ge(qk_ready, 24)
            sp.dma_start(g2, ln2_g[0, :].partition_broadcast(P)).then_inc(s_g2, 16)

            def load(e, j, kind):
                one = bass.ds(e, 1)
                s = 3 * (j % 2) + kind
                if kind < 2:
                    w = (w_gate, w_up)[kind][0].rearrange("e (k p) f -> e p k f", p=P)[one, :, :, 512 * j:512 * j + 512]
                    dst = slot(s).rearrange("p (k n) -> p k n", k=KD)
                    src = w.rearrange("e p k f -> p (e k) f")
                else:
                    w = w_down[0][one, 512 * j:512 * j + 512, :].rearrange("e (k p) n -> e p k n", p=P)
                    dst = slot(s).rearrange("p (k n) -> p k n", k=4)
                    src = w.rearrange("e p k n -> p (e k) n")
                sp.dma_start(dst, src).then_inc(s_w[s], 16)

            def load_expert(e, js=range(JB)):
                for j in js:
                    sp.wait_ge(gu_done, 16 * e + 4 * j - 4)
                    load(e, j, 0)
                    load(e, j, 1)
                    sp.wait_ge(down_done, 4 * e + j - 1)
                    load(e, j, 2)

            sp.wait_ge(b7_taken, [n for n, (_, k, _) in enumerate(b7) if k == "pool"][-1] + 1)
            sp.wait_ge(pool_d, GROUPS)
            load(0, 1, 1)
            load(0, 1, 2)
            sp.wait_ge(b7_done, len(b7))
            load(0, 0, 2)
            load(0, 1, 0)

            def load_hx(t):
                b = t % 2
                if t >= 2:
                    sp.wait_ge(h2_ready, t - 1)
                if t == 0:
                    sp.dma_start(hx[0][0:META, :], meta_tokens).then_inc(s_hx[0], 16)
                    sp.dma_start(hx[0][META:P, :], x[0, 0:P - META, :]).then_inc(s_hx[0], 16)
                else:
                    a = P * t - META
                    sp.dma_start(hx[b][0:ROWS[t], :], x[0, a:a + ROWS[t], :]).then_inc(s_hx[b], 16)

            load_hx(0)
            load_hx(1)
            for t in range(NT):
                R = ROWS[t]
                if t + 2 < NT:
                    load_hx(t + 2)
                sp.wait_ge(h2_ready, t + 1)
                sp.dma_start(sums[P * t:P * t + R, :], h2[t % 2][0:R, :]).then_inc(s_sums[t % 2], 16)
                sp.wait_ge(hn_ready, t + 1)
                sp.dma_start(table[P * t:P * t + R, :], hn[t % 2][0:R, :]).then_inc(s_table[t % 2], 16)
            sp.wait_ge(wo_done, NT)
            load(0, 0, 0)
            load(0, 0, 1)
            load_expert(0, (2, 3))
            with sp.Fori(1, E) as e:
                load_expert(e)
            sp.wait_ge(s_scat, 16 * E)
            sp.wait_ge(s_scatx, 16 * E)
            sp.dma_start(out[0], sums[META:L, :]).then_inc(s_out, 16)
            sp.wait_ge(s_out, 16)

        @block.gpsimd
        def _(pool):
            steps = [0]

            def link(ins):
                steps[0] += 1
                ins.then_inc(pool_chain, 1)
                pool.wait_ge(pool_chain, steps[0])

            pool.memset(eps[:], EPS).then_inc(eps_set, 1)
            pool.wait_ge(xtr, NT)
            for g in range(GROUPS):
                pool.memset(pbuf[:, g, 0:PADW], 0.0).then_inc(pads_set, 1)
                pool.memset(pbuf[:, g, PADW + L:LP], 0.0).then_inc(pads_set, 1)
            pool.wait_ge(pads_set, 2 * GROUPS)
            n = 0
            for g in range(GROUPS):
                pool.wait_ge(proj_taken, 33 + 3 * (g + 1))
                src = pbuf[:, g, :]
                for lv in range(g + 1):
                    reach = 2 ** g - 2 ** lv if lv else 2 ** g - 1
                    lo, hi = PADW - reach, PADW + L + reach
                    a, b = (1, 0) if lv == 0 else (2 ** (lv - 1), 2 ** (lv - 1))
                    if lv == 0 and g:
                        pool.wait_ge(pool_d, g)
                    dst = lev[n % 2]
                    ins = pool.tensor_tensor(dst[:, lo:hi], src[:, lo - a:hi - a], src[:, lo + b:hi + b], ALU.add)
                    if lv < g:
                        link(ins)
                    src = dst
                    n += 1
                ins.then_inc(win_ready, 1)

            def gather(e):
                pool.tensor_copy(gidx[:, 0:1], idx[:, 0, bass.ds(e, 1)]).then_inc(gidx_set, 1)
                pool.tensor_copy(gidx[0:CAPX, 1:2], idx[0:CAPX, 1, bass.ds(e, 1)]).then_inc(gidx_set, 1)
                pool.wait_ge(gidx_set, 2)
                pool.indirect_dma_start(xg, None, table, bass.IndirectOffsetOnAxis(ap=gidx[:, 0:1], axis=0)
                                        ).then_inc(s_gath, 16)
                pool.indirect_dma_start(xgx, None, table, bass.IndirectOffsetOnAxis(ap=gidx[0:CAPX, 1:2], axis=0)
                                        ).then_inc(s_gathx, 16)
                pool.sem_clear(gidx_set)

            def scatter(e, first):
                if not first:
                    pool.wait_ge(s_scat, 16 * e)
                    pool.wait_ge(s_scatx, 16 * e)
                pool.wait_ge(y_taken, 3 * e + 3)
                pool.tensor_copy(sidx[:, 0:1], idx[:, 0, bass.ds(e, 1)]).then_inc(sidx_set, 1)
                pool.tensor_copy(sidx[0:CAPX, 1:2], idx[0:CAPX, 1, bass.ds(e, 1)]).then_inc(sidx_set, 1)
                pool.wait_ge(sidx_set, 2)
                pool.indirect_dma_start(sums, bass.IndirectOffsetOnAxis(ap=sidx[:, 0:1], axis=0), y_sb, None,
                                        compute_op=ALU.add).then_inc(s_scat, 16)
                pool.indirect_dma_start(sums, bass.IndirectOffsetOnAxis(ap=sidx[0:CAPX, 1:2], axis=0), yx_sb, None,
                                        compute_op=ALU.add).then_inc(s_scatx, 16)
                pool.sem_clear(sidx_set)

            for s in (*s_table, *s_sums):
                pool.wait_ge(s, 16 * (NT // 2 + (s in (s_table[0], s_sums[0]))))
            pool.wait_ge(route_ready, 4)
            gather(0)
            pool.wait_ge(xg_tr, 1)
            gather(1)
            pool.wait_ge(xg_tr, 2)
            gather(2)
            scatter(0, True)
            with pool.Fori(2, E - 1) as e:
                pool.wait_ge(xg_tr, e + 1)
                gather(e + 1)
                scatter(e - 1, False)
            scatter(E - 2, False)
            scatter(E - 1, False)
            pool.wait_ge(s_scat, 16 * E)
            pool.wait_ge(s_scatx, 16 * E)

        @block.scalar
        def _(act):
            act.wait_ge(eps_set, 1)
            def root1(t):
                R = ROWS[t]
                act.wait_ge(var_ready, t + 1)
                act.activation(st[0:R, 2, t:t + 1], st[0:R, 1, t:t + 1], ACT.Sqrt).then_inc(std_ready, 1)

            for t in range(NT):
                R = ROWS[t]
                act.wait_ge(s_x[t], 32 if t == 0 else 16)
                act.activation(two_banks(4 + 2 * (t % 2), R), xt(t)[0:R, :], ACT.Square,
                               accum_out=st[0:R, 0, t:t + 1]).then_inc(ssq, 1)
                if t:
                    root1(t - 1)
            root1(NT - 1)

            def rope_root(i):
                act.wait_ge(ms_done, i + 1)
                if i >= 2:
                    act.wait_ge(qk_ready, i - 1)
                W = WID[i % 3]
                act.activation(rt[i % 2][:, 0:W], PS[:, 4 + i % 2, 0:W], ACT.Sqrt, bias=eps[:, 0:1]).then_inc(rt_ready, 1)

            act.wait_ge(s_par, 16 * 9)
            for i in range(24):
                n, W = i // 3, WID[i % 3]
                act.wait_ge(proj_done, i + 1)
                if i >= 2:
                    act.wait_ge(ms_done, i - 1)
                act.activation(sq[i % 2][:, 0:W], PS[:, i % 4, 0:W], ACT.Square).then_inc(sq_ready, 1)
                if i >= 3:
                    act.wait_ge(qk_ready, i - 2)
                    act.wait_ge(sw_done, i - 2)
                act.activation(qg[i % 3][:, 0:W], PS[:, i % 4, 0:W], ACT.Identity, scale=gq[:, n % 2:n % 2 + 1]
                               ).then_inc(proj_taken, 1)
                if i:
                    rope_root(i - 1)
            rope_root(23)
            for t in range(NT):
                i, R = 24 + t, KEYS[t]
                act.wait_ge(proj_done, i + 1)
                if t == 0:
                    act.wait_ge(xtr, NT)
                act.activation(v_sb[0:R, t, :], PS[0:R, i % 4, :], ACT.Copy).then_inc(proj_taken, 1)
            for n in range(12):
                i, g, c = 33 + n, n // 3, n % 3
                act.wait_ge(proj_done, i + 1)
                act.activation(pbuf[:, g, PADW + OFF[c]:PADW + OFF[c] + WID[c]], PS[:, i % 4, 0:WID[c]], ACT.Copy
                               ).then_inc(proj_taken, 1)
            act.wait_ge(lam_dot, 2)
            act.activation(lam[:, 2:4], lam[:, 0:2], ACT.Exp).then_inc(lam_exp, 1)

            def exps(s, m):
                R = ROWS[s % NT]
                act.wait_ge(nb_ready, 2 * s + m + 1)
                if s >= 2 and m == 0:
                    act.wait_ge(tr_done, 3 * (s - 1))
                p = probs[0:R, s % 2, m, :]
                act.activation(p.rearrange("p (c t) -> p c t", c=3), PS[0:R, 3 * m:3 * m + 3, 0:CHW], ACT.Exp, bias=nb[0:R, s % 2, m:m + 1],
                               scale=SCALE, accum_out=zs[0:R, s % 2, 0, m:m + 1]).then_inc(exp_done, 1)

            def take_transposes(s):
                R, q = ROWS[s % NT], s % NT
                for b in range(3):
                    act.wait_ge(tr_done, 3 * s + b + 1)
                    if b == 0 and q % 3 == 0 and s >= 3:
                        act.wait_ge(b7_done, pv_uses[s // 3 - 1] + 1)
                    act.activation(aT[:, 3 * b:3 * b + 3, (q % 3) * P:(q % 3) * P + R],
                                   PS[:, 6, 0:3 * P].rearrange("p (n r) -> p n r", n=3)[:, :, 0:R], ACT.Copy).then_inc(tr_taken, 1)

            def take_b7(s):
                if s not in b7_of:
                    return
                n, kind, what = b7_of[s]
                act.wait_ge(b7_done, n + 1)
                if kind == "pv":
                    h, q3 = what // 3, what % 3
                    N = sum(ROWS[3 * q3:3 * q3 + 3])
                    act.activation(mixT[:, h, 3 * P * q3:3 * P * q3 + N], PS[:, 7, 0:N], ACT.Copy).then_inc(b7_taken, 1)
                else:
                    g, c = what
                    act.activation(mixT[:, HEADS + g, OFF[c]:OFF[c] + WID[c]], PS[:, 7, 0:WID[c]], ACT.Identity,
                                   scale=psc[:, g:g + 1]).then_inc(b7_taken, 1)

            for s in range(STEPS + 1):
                if s < STEPS:
                    exps(s, 0)
                if s:
                    take_transposes(s - 1)
                if s < STEPS:
                    exps(s, 1)
                take_b7(s)

            def o_root(j):
                act.wait_ge(oms, j + 1)
                if j >= 2:
                    act.wait_ge(o_ready, j - 1)
                W = WID[j % 3]
                act.activation(rt[j % 2][:, 0:W], PS[:, j % 2, 0:W], ACT.Sqrt, bias=eps[:, 0:1]).then_inc(ort, 1)

            act.wait_ge(b7_taken, len(b7))
            for j in range(12):
                h, c = j // 3, j % 3
                if j >= 2:
                    act.wait_ge(oms, j - 1)
                act.activation(sq[j % 2][:, 0:WID[c]], mixT[:, h, OFF[c]:OFF[c] + WID[c]], ACT.Square).then_inc(osq, 1)
                if j:
                    o_root(j - 1)
            o_root(11)

            def take_hn(t):
                R = ROWS[t]
                act.wait_ge(hn_tr, t + 1)
                if t >= 2:
                    act.wait_ge(rout_done, t - 1)
                act.activation(hnT[t % 2][:, :, 0:R], two_banks(4).rearrange("p (k r) -> p k r", k=KD)[:, :, 0:R],
                               ACT.Copy).then_inc(hnT_ready, 1)
                act.wait_ge(rout_done, t + 1)
                act.activation(lgT[:, P * t:P * t + R], PS[0:E, 6, 0:R], ACT.Copy).then_inc(lgT_ready, 1)

            for t in range(NT):
                R, b = ROWS[t], t % 2
                act.wait_ge(h2_ready, t + 1)
                if t >= 2:
                    act.wait_ge(s_table[b], 16 * (t // 2))
                    act.wait_ge(hn_tr, t - 1)
                act.activation(hn[b][0:R, :], h2[b][0:R, :], ACT.Square, accum_out=st2[0:R, 0, t:t + 1]).then_inc(ssq2, 1)
                act.wait_ge(var2, t + 1)
                act.activation(st2[0:R, 2, t:t + 1], st2[0:R, 1, t:t + 1], ACT.Sqrt).then_inc(std2, 1)
                if t:
                    take_hn(t - 1)
            take_hn(NT - 1)
            act.wait_ge(lg_sub, 1)
            act.activation(lg, lg, ACT.Exp).then_inc(lg_exp, 1)

            def silus(e, j):
                for f in range(4):
                    n = 16 * e + 4 * j + f
                    act.wait_ge(gu_done, n + 1)
                    act.activation(silu[f % 2], PS[:, f % 2, 0:CAP], ACT.Silu).then_inc(silu_ready, 1)

            def take_y(e):
                act.wait_ge(y_tr, 3 * e + 1)
                act.wait_ge(gcur_set, 2 * e + 2)
                act.activation(y_sb, two_banks(5), ACT.Identity, scale=gcur[:, 0:1]).then_inc(y_taken, 1)
                for b in range(2):
                    act.wait_ge(y_tr, 3 * e + 2 + b)
                    act.activation(yx_sb[:, 512 * b:512 * b + 512], PS[0:CAPX, 7, :], ACT.Identity,
                                   scale=gcur[0:CAPX, 1:2]).then_inc(y_taken, 1)

            def expert(e, first=False):
                silus(e, 0)
                silus(e, 1)
                if not first:
                    take_y(e - 1)
                silus(e, 2)
                silus(e, 3)

            expert(0, first=True)
            with act.Fori(1, E) as e:
                expert(e)
            take_y(E - 1)

        @block.vector
        def _(dve):
            steps = [0]

            def link(ins):
                steps[0] += 1
                ins.then_inc(dve_chain, 1)
                dve.wait_ge(dve_chain, steps[0])

            def scale_rows(t):
                R = ROWS[t]
                dve.wait_ge(std_ready, t + 1)
                link(dve.reciprocal(st[0:R, 3, t:t + 1], st[0:R, 2, t:t + 1]))
                dve.tensor_scalar(xt(t)[0:R, :], xt(t)[0:R, :], st[0:R, 3, t:t + 1], None, ALU.mult).then_inc(xs_ready, 1)

            def take_xt(t):
                R = ROWS[t]
                dve.wait_ge(xtr, t + 1)
                for b in range(2):
                    gain = g1[:, 4 * b:4 * b + 4].unsqueeze(2).broadcast_to([P, 4, R])
                    dve.tensor_tensor(hT[:, 4 * b:4 * b + 4, P * t:P * t + R],
                                      PS[:, 2 * (t % 2) + b, :].rearrange("p (k r) -> p k r", k=4)[:, :, 0:R],
                                      gain, ALU.mult).then_inc(hT_ready, 1)

            for t in range(NT + 2):
                if t < NT:
                    R = ROWS[t]
                    dve.wait_ge(ssq, t + 1)
                    dve.tensor_scalar(st[0:R, 1, t:t + 1], st[0:R, 0, t:t + 1], 1.0 / D, EPS, ALU.mult, ALU.add
                                      ).then_inc(var_ready, 1)
                if 1 <= t <= NT:
                    scale_rows(t - 1)
                if t == 2:
                    dve.wait_ge(s_par, 16 * 9)
                if t >= 2:
                    take_xt(t - 2)

            dve.wait_ge(s_lam, 64)
            for m in range(2):
                ins = dve.tensor_tensor_reduce(lamj[:], lamv[:, 2 * m, :], lamv[:, 2 * m + 1, :], 1.0, 0.0,
                                               ALU.mult, ALU.add, lam[:, m:m + 1])
                ins.then_inc(lam_dot, 1)
                dve.wait_ge(lam_dot, m + 1)
            dve.tensor_scalar(sg[:, 1:2], sg[:, 0:1], 1.0 - LAM_INIT, None, ALU.mult)

            dve.wait_ge(s_trig, 16)
            for i in range(24):
                n, c = i // 3, i % 3
                W = WID[c]
                at = slice(OFF[c], OFF[c] + W)
                dst = (qT, kT)[n % 2][:, n // 2, at]
                dve.wait_ge(rt_ready, i + 1)
                link(dve.reciprocal(rt[i % 2][:, 0:W], rt[i % 2][:, 0:W]))
                dve.tensor_tensor(ta[:, 0:W], qg[i % 3][:, 0:W], cosT[:, at], ALU.mult)
                dve.wait_ge(sw_done, i + 1)
                link(dve.tensor_tensor(tb[:, 0:W], PS[:, 6 + i % 2, 0:W], sinT[:, at], ALU.mult))
                link(dve.tensor_tensor(ta[:, 0:W], ta[:, 0:W], tb[:, 0:W], ALU.add))
                dve.tensor_tensor(dst, ta[:, 0:W], rt[i % 2][:, 0:W], ALU.mult).then_inc(qk_ready, 1)

            dve.wait_ge(lam_exp, 1)
            link(dve.tensor_tensor(lam[:, 4:5], lam[:, 2:3], lam[:, 3:4], ALU.subtract))
            link(dve.tensor_scalar(lam[:, 4:5], lam[:, 4:5], LAM_INIT, None, ALU.add))

            def pool_diff(g):
                w = WINDOWS[g]
                s = lev[(sum(range(g + 2)) - 1) % 2]
                dve.wait_ge(win_ready, g + 1)
                for a, b in ((PADW, 0), (PADW + L - 8, 8)):
                    link(dve.tensor_tensor(s[:, a:a + 8], s[:, a:a + 8], edge[:, g, b:b + 8], ALU.mult))
                dve.scalar_tensor_tensor(out=pbuf[:, g, PADW:PADW + L], in0=s[:, PADW:PADW + L], scalar=1.0 / w,
                                         in1=pbuf[:, g, PADW:PADW + L], op0=ALU.mult, op1=ALU.subtract
                                         ).then_inc(pool_d, 1)

            def maxes(s, m):
                R, b = ROWS[s % NT], s % 2
                dve.wait_ge(scores, 2 * s + m + 1)
                link(dve.tensor_reduce(mx[0:R, b, m:m + 1], PS[0:R, 3 * m:3 * m + 3, 0:CHW], AX.XY, ALU.max))
                dve.tensor_scalar(nb[0:R, b, m:m + 1], mx[0:R, b, m:m + 1], -SCALE, None, ALU.mult).then_inc(nb_ready, 1)

            def difference(s):
                R, b = ROWS[s % NT], s % 2
                dve.wait_ge(exp_done, 2 * s + 2)
                p = probs[0:R, b, :, :]
                twice = p.rearrange("p m (c t) -> p m c t", c=3)[:, :, 1:3, 0:2]
                link(dve.tensor_reduce(zs[0:R, b, 1, :], twice, AX.XY, ALU.add))
                link(dve.tensor_tensor(zs[0:R, b, 2, :], zs[0:R, b, 0, :], zs[0:R, b, 1, :], ALU.subtract))
                link(dve.reciprocal(zs[0:R, b, 3, :], zs[0:R, b, 2, :]))
                link(dve.tensor_tensor(rl[0:R, b:b + 1], zs[0:R, b, 3, 1:2], lam[0:R, 4:5], ALU.mult))
                link(dve.tensor_scalar(probs[0:R, b, 1, :], probs[0:R, b, 1, :], rl[0:R, b:b + 1], None, ALU.mult))
                dve.scalar_tensor_tensor(out=probs[0:R, b, 0, :], in0=probs[0:R, b, 0, :],
                                         scalar=zs[0:R, b, 3, 0:1], in1=probs[0:R, b, 1, :],
                                         op0=ALU.mult, op1=ALU.subtract).then_inc(diff_ready, 1)

            for s in range(STEPS + 1):
                if s < STEPS:
                    maxes(s, 0)
                if s:
                    difference(s - 1)
                if s < STEPS:
                    maxes(s, 1)
                if s < GROUPS:
                    pool_diff(s)

            for j in range(12):
                h, c = j // 3, j % 3
                W = WID[c]
                part = mixT[:, h, OFF[c]:OFF[c] + W]
                dve.wait_ge(ort, j + 1)
                link(dve.reciprocal(rt[j % 2][:, 0:W], rt[j % 2][:, 0:W]))
                dve.scalar_tensor_tensor(out=part, in0=part, scalar=sg[:, 1:2], in1=rt[j % 2][:, 0:W],
                                         op0=ALU.mult, op1=ALU.mult).then_inc(o_ready, 1)

            dve.memset(lgT[:, L:NT * P], 0.0).then_inc(pad_set, 1)
            dve.wait_ge(s_g2, 16)
            for t in range(NT):
                R, b = ROWS[t], t % 2
                dve.wait_ge(wo_done, t + 1)
                dve.wait_ge(s_hx[b], 16 * (t // 2 + 1 + (b == 0)))
                if t >= 2:
                    dve.wait_ge(s_sums[b], 16 * (t // 2))
                dve.tensor_tensor(h2[b][0:R, :], two_banks(2 * b, R), hx[b][0:R, :], ALU.add).then_inc(h2_ready, 1)
                dve.wait_ge(ssq2, t + 1)
                dve.tensor_scalar(st2[0:R, 1, t:t + 1], st2[0:R, 0, t:t + 1], 1.0 / D, EPS, ALU.mult, ALU.add
                                  ).then_inc(var2, 1)
                dve.wait_ge(std2, t + 1)
                link(dve.reciprocal(st2[0:R, 3, t:t + 1], st2[0:R, 2, t:t + 1]))
                dve.scalar_tensor_tensor(out=hn[b][0:R, :], in0=h2[b][0:R, :], scalar=st2[0:R, 3, t:t + 1],
                                         in1=g2[0:R, :], op0=ALU.mult, op1=ALU.mult).then_inc(hn_ready, 1)

            dve.wait_ge(lg_tr, 1)
            lp = PS[:, 7, 0:NT * E].rearrange("p (t e) -> p t e", t=NT)
            link(dve.tensor_reduce(sm[:, 0, :], lp, AX.X, ALU.max))
            dve.tensor_tensor(lg, lp, sm[:, 0, :].unsqueeze(2).broadcast_to([P, NT, E]), ALU.subtract).then_inc(lg_sub, 1)
            dve.wait_ge(lg_exp, 1)
            link(dve.tensor_reduce(sm[:, 1, :], lg, AX.X, ALU.add))
            link(dve.reciprocal(sm[:, 2, :], sm[:, 1, :]))
            dve.tensor_tensor(lg, lg, sm[:, 2, :].unsqueeze(2).broadcast_to([P, NT, E]), ALU.mult).then_inc(aff_ready, 1)
            dve.wait_ge(aff_tr, 1)
            link(dve.tensor_copy(affT, PS[0:E, 0:3, :].rearrange("p b n -> p (b n)")[:, 0:L]))
            for r in range(ROUNDS):
                best = mv[:, 8 * r:8 * r + 8]
                link(dve.max(best, affT))
                link(dve.max_index(mi[:, 8 * r:8 * r + 8], best, affT))
                if r < ROUNDS - 1:
                    link(dve.match_replace(affT, best, affT, -1.0))
            dve.tensor_copy(mif, mi).then_inc(ids_ready, 1)
            dve.wait_ge(ids_tr, 1)
            for n, (dst, rows) in enumerate(((idx[:, 0, :], P), (gat[:, 0, :], P), (idx[0:CAPX, 1, :], CAPX),
                                             (gat[0:CAPX, 1, :], CAPX))):
                dve.tensor_copy(dst, PS[0:rows, 4, n * E:(n + 1) * E]).then_inc(route_ready, 1)

            def take_x(e, first):
                dve.wait_ge(xg_tr, e + 1)
                if not first:
                    dve.wait_ge(gu_done, 16 * e)
                for b in range(3):
                    n = min(3, KD - 3 * b)
                    dve.tensor_copy(xT[:, 3 * b:3 * b + n, :],
                                    PS[:, 5 + b, 0:n * CAP].rearrange("p (k c) -> p k c", k=n)).then_inc(xT_ready, 1)

            def acts(e, j, wait_down=True):
                if wait_down:
                    dve.wait_ge(down_done, 4 * e + j - 1)
                for f in range(4):
                    dve.wait_ge(silu_ready, 16 * e + 4 * j + f + 1)
                    dve.tensor_tensor(act_T[:, j % 2, f, :], silu[f % 2], PS[:, f % 2, CAP:2 * CAP], ALU.mult
                                      ).then_inc(act_ready, 1)

            def take_yT(e, first):
                dve.wait_ge(down_done, 4 * e + 4)
                if not first:
                    dve.wait_ge(y_tr, 3 * e)
                for b in range(3):
                    n = min(3, KD - 3 * b)
                    dve.tensor_copy(yT[:, 3 * b:3 * b + n, :],
                                    PS[:, 2 + b, 0:n * CAP].rearrange("p (k c) -> p k c", k=n)).then_inc(yT_ready, 1)
                if not first:
                    dve.wait_ge(s_scat, 16 * e)
                    dve.wait_ge(s_scatx, 16 * e)
                dve.tensor_copy(gcur[:, 0:1], gat[:, 0, bass.ds(e, 1)]).then_inc(gcur_set, 1)
                dve.tensor_copy(gcur[0:CAPX, 1:2], gat[0:CAPX, 1, bass.ds(e, 1)]).then_inc(gcur_set, 1)

            dve.wait_ge(route_ready, 4)
            take_x(0, True)
            acts(0, 0, False)
            acts(0, 1, False)
            acts(0, 2)
            acts(0, 3)
            take_x(1, False)
            acts(1, 0)
            take_yT(0, True)
            acts(1, 1)
            acts(1, 2)
            acts(1, 3)
            take_x(2, False)
            with dve.Fori(2, E - 1) as e:
                acts(e, 0)
                take_yT(e - 1, False)
                acts(e, 1)
                acts(e, 2)
                acts(e, 3)
                take_x(e + 1, False)
            acts(E - 1, 0)
            take_yT(E - 2, False)
            acts(E - 1, 1)
            acts(E - 1, 2)
            acts(E - 1, 3)
            take_yT(E - 1, False)

        @block.tensor
        def _(pe):
            pe.wait_ge(s_cst, 16)
            for t in range(NT):
                R = ROWS[t]
                pe.wait_ge(xs_ready, t + 1)
                if t >= 2:
                    pe.wait_ge(hT_ready, 2 * (t - 1))
                for k in range(KD):
                    ins = pe.transpose(PS[:, 2 * (t % 2) + k // 4, (k % 4) * P:(k % 4) * P + R],
                                       xt(t)[0:R, k * P:(k + 1) * P], ident[0:R, 0:R])
                ins.then_inc(xtr, 1)

            def stats(i):
                W = WID[i % 3]
                pe.wait_ge(sq_ready, i + 1)
                if i >= 2:
                    pe.wait_ge(rt_ready, i - 1)
                pe.matmul(PS[:, 4 + i % 2, 0:W], blk_mean, sq[i % 2][:, 0:W], start=True, stop=True).then_inc(ms_done, 1)
                pe.wait_ge(proj_taken, i + 1)
                if i >= 2:
                    pe.wait_ge(qk_ready, i - 1)
                pe.matmul(PS[:, 6 + i % 2, 0:W], swap, qg[i % 3][:, 0:W], start=True, stop=True).then_inc(sw_done, 1)

            pe.wait_ge(hT_ready, 2 * NT)
            for i in range(24):
                n, c = i // 3, i % 3
                if i < 6 and i % 3 == 0:
                    pe.wait_ge(s_win[n % 2], 16)
                if i >= 4:
                    pe.wait_ge(proj_taken, i - 3)
                for k in range(KD):
                    ins = pe.matmul(PS[:, i % 4, 0:WID[c]], w_in_sb[n % 2][:, k, P * (n // 2):P * (n // 2) + P],
                                    hT[:, k, OFF[c]:OFF[c] + WID[c]], start=k == 0, stop=k == KD - 1)
                ins.then_inc(proj_done, 1)
                if i:
                    stats(i - 1)
            for t in range(NT):
                i, R = 24 + t, KEYS[t]
                if t == 0:
                    pe.wait_ge(s_win[2], 16)
                pe.wait_ge(proj_taken, i - 3)
                for k in range(KD):
                    ins = pe.matmul(PS[0:R, i % 4, :], hT[:, k, KEY0[t]:KEY0[t] + R], w_in_sb[2][:, k, :],
                                    start=k == 0, stop=k == KD - 1)
                ins.then_inc(proj_done, 1)
                if t == 0:
                    stats(23)
            pe.wait_ge(s_win[3], 16)
            for n in range(12):
                i, g, c = 33 + n, n // 3, n % 3
                pe.wait_ge(proj_taken, i - 3)
                if n == 0:
                    pe.wait_ge(pads_set, 2 * GROUPS)
                for k in range(KD):
                    ins = pe.matmul(PS[:, i % 4, 0:WID[c]], w_in_sb[3][:, k, P * g:P * g + P],
                                    hT[:, k, OFF[c]:OFF[c] + WID[c]], start=k == 0, stop=k == KD - 1)
                ins.then_inc(proj_done, 1)

            def score(s, m):
                h, q = s // NT, s % NT
                R = ROWS[q]
                if s:
                    pe.wait_ge(exp_done, 2 * (s - 1) + m + 1)
                at = slice(DH * m, DH * m + DH)
                for c in range(3):
                    ins = pe.matmul(PS[0:R, 3 * m + c, 0:CHW], qT[at, h, P * q:P * q + R],
                                    kT[at, h, CHS * c:CHS * c + CHW], start=True, stop=True)
                ins.then_inc(scores, 1)

            def transposes(s):
                R = ROWS[s % NT]
                pe.wait_ge(diff_ready, s + 1)
                for b in range(3):
                    if s or b:
                        pe.wait_ge(tr_taken, 3 * s + b)
                    for kt in range(3 * b, 3 * b + 3):
                        at = 2 * LS * (s % 2) + KPOS[kt]
                        ins = pe.transpose(PS[:, 6, (kt % 3) * P:(kt % 3) * P + R],
                                           flat_probs[0:R, at:at + P], ident[0:R, 0:R])
                    ins.then_inc(tr_done, 1)

            def use_b7(s):
                if s not in b7_of:
                    return
                n, kind, what = b7_of[s]
                if n:
                    pe.wait_ge(b7_taken, n)
                if kind == "pv":
                    h, q3 = what // 3, what % 3
                    N = sum(ROWS[3 * q3:3 * q3 + 3])
                    pe.wait_ge(tr_taken, 3 * s)
                    for kt in range(NT):
                        KR = KEYS[kt]
                        ins = pe.matmul(PS[:, 7, 0:N], v_sb[0:KR, kt, DV * h:DV * h + DV], aT[0:KR, kt, 0:N],
                                        start=kt == 0, stop=kt == NT - 1)
                else:
                    g, c = what
                    pe.wait_ge(pool_d, g + 1)
                    ins = pe.matmul(PS[:, 7, 0:WID[c]], poolw[:, g, :], pbuf[:, g, PADW + OFF[c]:PADW + OFF[c] + WID[c]],
                                    start=True, stop=True)
                ins.then_inc(b7_done, 1)

            pe.wait_ge(proj_taken, 45)
            pe.wait_ge(qk_ready, 24)
            for s in range(STEPS + 1):
                if s < STEPS:
                    score(s, 0)
                    score(s, 1)
                if s:
                    transposes(s - 1)
                use_b7(s)

            for j in range(12):
                W = WID[j % 3]
                pe.wait_ge(osq, j + 1)
                if j >= 2:
                    pe.wait_ge(ort, j - 1)
                pe.matmul(PS[:, j % 2, 0:W], dv_mean, sq[j % 2][:, 0:W], start=True, stop=True).then_inc(oms, 1)

            def router(t):
                R = ROWS[t]
                pe.wait_ge(hn_ready, t + 1)
                if t:
                    pe.wait_ge(hnT_ready, t)
                for k in range(KD):
                    ins = pe.transpose(PS[:, 4 + k // 4, (k % 4) * P:(k % 4) * P + R],
                                       hn[t % 2][0:R, k * P:(k + 1) * P], ident[0:R, 0:R])
                ins.then_inc(hn_tr, 1)
                pe.wait_ge(hnT_ready, t + 1)
                if t:
                    pe.wait_ge(lgT_ready, t)
                for k in range(KD):
                    ins = pe.matmul(PS[0:E, 6, 0:R], wr[:, k, :], hnT[t % 2][:, k, 0:R], start=k == 0, stop=k == KD - 1)
                ins.then_inc(rout_done, 1)

            pe.wait_ge(s_wout, 32)
            pe.wait_ge(o_ready, 12)
            for t in range(NT):
                R = ROWS[t]
                if t >= 2:
                    pe.wait_ge(h2_ready, t - 1)
                for half in range(2):
                    for k in range(KD):
                        ins = pe.matmul(PS[0:R, 2 * (t % 2) + half, :], mixT[:, k, P * t:P * t + R],
                                        w_out_sb[half][:, k, :], start=k == 0, stop=k == KD - 1)
                ins.then_inc(wo_done, 1)
                if t:
                    router(t - 1)
            router(NT - 1)
            pe.wait_ge(lgT_ready, NT)
            pe.wait_ge(pad_set, 1)
            for t in range(NT):
                ins = pe.transpose(PS[:, 7, t * E:(t + 1) * E], lgT[:, P * t:P * t + P], ident[0:E, 0:E])
            ins.then_inc(lg_tr, 1)
            pe.wait_ge(h2_ready, NT)
            pe.wait_ge(aff_ready, 1)
            for t in range(NT):
                ins = pe.transpose(PS[0:E, t // 4, (t % 4) * P:(t % 4) * P + P], lg[:, t, :], ident)
            ins.then_inc(aff_tr, 1)
            pe.wait_ge(ids_ready, 1)
            for n, (src, at, rows) in enumerate(((mif, 0, P), (mv, 0, P), (mif, P, CAPX), (mv, P, CAPX))):
                ins = pe.transpose(PS[0:rows, 4, n * E:(n + 1) * E], src[:, at:at + rows], ident[0:E, 0:E])
            ins.then_inc(ids_tr, 1)

            def x_transposes(e, first):
                pe.wait_ge(s_gath, 16 * e + 16)
                pe.wait_ge(s_gathx, 16 * e + 16)
                if not first:
                    pe.wait_ge(y_taken, 3 * e - 3)
                for k in range(KD):
                    at = (k % 3) * CAP
                    pe.transpose(PS[:, 5 + k // 3, at:at + P], xg[:, k * P:(k + 1) * P], ident)
                    ins = pe.transpose(PS[:, 5 + k // 3, at + P:at + CAP], xgx[:, k * P:(k + 1) * P],
                                       ident[0:CAPX, 0:CAPX])
                ins.then_inc(xg_tr, 1)

            def gate_up(e, j, lag=True):
                base = 3 * (j % 2)
                if j == 0:
                    pe.wait_ge(xT_ready, 3 * e + 3)
                pe.wait_ge(s_w[base], 16 * (2 * e + j // 2 + 1))
                pe.wait_ge(s_w[base + 1], 16 * (2 * e + j // 2 + 1))
                for f in range(4):
                    if lag or f >= 2:
                        pe.wait_ge(act_ready, 16 * e + 4 * j + f - 1)
                    for n in range(2):
                        w = slot(base + n).rearrange("p (k n) -> p k n", k=KD)
                        for k in range(KD):
                            ins = pe.matmul(PS[:, f % 2, n * CAP:(n + 1) * CAP], w[:, k, f * P:(f + 1) * P],
                                            xT[:, k, :], start=k == 0, stop=k == KD - 1)
                    ins.then_inc(gu_done, 1)

            def down(e, j, first=False):
                base = 3 * (j % 2)
                if j == 0 and not first:
                    pe.wait_ge(yT_ready, 3 * e)
                pe.wait_ge(s_w[base + 2], 16 * (2 * e + j // 2 + 1))
                pe.wait_ge(act_ready, 16 * e + 4 * j + 4)
                w = slot(base + 2).rearrange("p (k n) -> p k n", k=4)
                for d in range(KD):
                    for f in range(4):
                        ins = pe.matmul(PS[:, 2 + d // 3, (d % 3) * CAP:(d % 3 + 1) * CAP], w[:, f, d * P:(d + 1) * P],
                                        act_T[:, j % 2, f, :], start=j == 0 and f == 0 and d % 3 == 0,
                                        stop=j == JB - 1 and f == 3, skip_group_check=True)
                ins.then_inc(down_done, 1)

            def y_transposes(e, last=False):
                pe.wait_ge(yT_ready, 3 * e + 3)
                if not last:
                    pe.wait_ge(xT_ready, 3 * e + 6)
                for d in range(KD):
                    ins = pe.transpose(PS[:, 5 + d // 4, (d % 4) * P:(d % 4) * P + P], yT[:, d, 0:P], ident)
                ins.then_inc(y_tr, 1)
                for b in range(2):
                    if b:
                        pe.wait_ge(y_taken, 3 * e + 2)
                    for d in range(4 * b, 4 * b + 4):
                        ins = pe.transpose(PS[0:CAPX, 7, (d % 4) * P:(d % 4) * P + P], yT[:, d, P:CAP], ident)
                    ins.then_inc(y_tr, 1)

            x_transposes(0, True)
            gate_up(0, 0, lag=False)
            gate_up(0, 1)
            down(0, 0, first=True)
            gate_up(0, 2)
            down(0, 1)
            x_transposes(1, True)
            gate_up(0, 3)
            down(0, 2)

            def expert(e, last=False):
                gate_up(e, 0)
                down(e - 1, 3)
                gate_up(e, 1)
                y_transposes(e - 1)
                down(e, 0)
                gate_up(e, 2)
                down(e, 1)
                if not last:
                    x_transposes(e + 1, False)
                gate_up(e, 3)
                down(e, 2)

            with pe.Fori(1, E - 1) as e:
                expert(e)
            expert(E - 1, last=True)
            down(E - 1, 3)
            y_transposes(E - 1, last=True)


_INS = ["x", "meta_tokens", "ln1_g", "w_in", "q_norm_g", "k_norm_g", "lambda_q1", "lambda_k1", "lambda_q2",
        "lambda_k2", "subln_g", "pool_w", "pool_scale", "w_out", "ln2_g", "w_router", "w_gate", "w_up", "w_down"]


def kernel(**inputs):
    import numpy as _np
    import concourse.bacc as _bacc
    from concourse import mybir as _mybir
    from concourse.bass_utils import run_bass_kernel_spmd as _run

    nc = _bacc.Bacc("TRN2", target_bir_lowering=False, num_devices=1)
    arrays = {f"in_{n}": _np.ascontiguousarray(inputs[n]) for n in _INS}
    arrays["in_consts"] = constants()
    args = [nc.dram_tensor(n, a.shape, _mybir.dt.from_np(a.dtype), kind="ExternalInput").ap()
            for n, a in arrays.items()]
    out = nc.dram_tensor("out_0", (1, SEQ, D), _mybir.dt.float32, kind="ExternalOutput").ap()
    block_kernel(nc, *args, out)
    r = _run(nc, [arrays], core_ids=[0])
    return r.results[0]["out_0"]
```

```python
from contextlib import ExitStack

import numpy as np
import concourse.bass as bass
from concourse import mybir

F32 = mybir.dt.float32
F32R = mybir.dt.float32r
BF16 = mybir.dt.bfloat16
U32 = mybir.dt.uint32
I32 = mybir.dt.int32
ACT = mybir.ActivationFunctionType
ALU = mybir.AluOpType
AX = mybir.AxisListType

P = 128
D = 1024
SEQ = 1024
META = 16
L = SEQ + META
KD = D // P
NT = -(-L // P)
HEADS = 4
DH = 64
DV = 2 * DH
GROUPS = 4
WINDOWS = (2, 4, 8, 16)
E = 16
FF = 2048
CAP = 2 * L // E
CAPX = CAP - P
EPS = 1e-6
LAM_INIT = 0.2
SCALE = DH ** -0.5
ROWS = [min(P, L - P * t) for t in range(NT)]
OFF = (0, 348, 694)
WID = (348, 346, 346)
CHS, CHW = 346, 348
LS = 3 * CHW
KEY0 = [OFF[c] + P * j for c in range(3) for j in range(3)]
KEYS = [(P, P, WID[c] - 2 * P)[j] for c in range(3) for j in range(3)]
KPOS = [CHW * c + OFF[c] - CHS * c + P * j for c in range(3) for j in range(3)]
PADW = 8
LP = L + 2 * PADW
ROUNDS = -(-CAP // 8)
SLOT = 8 * 512
FT = FF // P
RAW, CUT = 4, 3
CG, CD = FF // 256, D // 256
CH = CG + CD
TILES = 2 * CH
SMALL = 204160
G0 = NT
Q0 = G0 + 3 * GROUPS
ITEMS = Q0 + 6 * HEADS
C_ID, C_BLK, C_SWAP, C_ONE = 0, P, 2 * P, 3 * P
C_EDGE = 4 * P
C_COS = C_EDGE + GROUPS * 16
C_SIN = C_COS + L
C_END = C_SIN + L


def constants():
    c = np.zeros((P, C_END), np.float32)
    p = np.arange(P)
    c[p, C_ID + p] = 1.0
    c[:, C_BLK:C_BLK + P] = (p[:, None] // DH == p[None, :] // DH) / DH
    c[p, C_SWAP + (p ^ (DH // 2))] = 1.0
    c[:, C_ONE:C_ONE + P] = 1.0 / DV
    t = np.arange(L)
    for g, w in enumerate(WINDOWS):
        count = np.minimum(t + w // 2, L) - np.maximum(t - w // 2, 0)
        edge = (w / count).astype(np.float32)
        c[:, C_EDGE + 16 * g:C_EDGE + 16 * g + 8] = edge[:8]
        c[:, C_EDGE + 16 * g + 8:C_EDGE + 16 * g + 16] = edge[-8:]
    half = DH // 2
    freq = np.float32(10000.0) ** (-np.arange(half, dtype=np.float32) / np.float32(half))
    ang = t.astype(np.float32)[None, :] * freq[p % half][:, None]
    c[:, C_COS:C_COS + L] = np.cos(ang)
    c[:, C_SIN:C_SIN + L] = np.sin(ang) * np.where(p % DH < half, -1.0, 1.0)[:, None]
    return c


def block_kernel(nc, x, meta_tokens, ln1_g, w_in, q_norm_g, k_norm_g, lambda_q1, lambda_k1,
                 lambda_q2, lambda_k2, subln_g, pool_w, pool_scale, w_out, ln2_g, w_router,
                 w_gate, w_up, w_down, consts, out):
    sums = nc.dram_tensor("sums", [L, D], F32, kind="Internal").ap()
    table = nc.dram_tensor("table", [L, D], F32, kind="Internal").ap()
    parts = nc.dram_tensor("parts", [2 * HEADS, 2, P, L], F32, kind="Internal").ap()

    ctx = ExitStack()
    with ctx:
        def sem(name):
            return ctx.enter_context(nc.semaphore(name))

        base = -(-nc.sbuf_base // 64) * 64

        def at(name, offset, shape, dt=F32):
            return nc.alloc_sbuf_tensor_at(name, [P] + shape, dt, offset=base + offset)

        ring = at("ring", 0, [4 * SLOT + 2 * 192])
        px_r = at("px_r", 66304, [8 * D + 224])
        mix_r = at("mix_r", 99968, [KD * L])
        v_hi = at("v_hi", 133248, [NT, HEADS * DV], F32R)
        v_lo = at("v_lo", 151680, [NT, HEADS * DV], F32R)
        trig_r = at("trig_r", 170112, [2 * L])
        tmp_r = at("tmp_r", 178432, [9 * CHW])
        stage = [at(f"stage{i}", 190976 + i * 2784, [2, CHW], F32R) for i in (0, 1)]
        x_last = at("x_last", 197760, [D])
        stk = [at(f"stk{i}", off, [2, 3, L], F32R) for i, off in ((0, 41344), (1, 0))]
        probs_a = [at(f"probs_a{i}", 83200 + i * 4192, [LS]) for i in range(3)]
        probs_b = [at(f"probs_b{i}", off, [LS]) for i, off in ((0, 83200 + 3 * 4192), (1, 197760))]
        aT_hi = at("aT_hi", 170112, [NT, 3 * P], F32R)
        aT_lo = at("aT_lo", 183936, [NT, 3 * P], F32R)
        w_out_r = [at(f"w_out_r{i}", off, [SLOT]) for i, off in ((0, 24960), (1, 66304))]
        out_r = at("out_r", 133248, [9 * D])

        def slot(s):
            return ring[:, s * SLOT:(s + 1) * SLOT]

        def cut(region, at, n, **how):
            part = region[:, at:at + n]
            return part.rearrange("p (a b) -> p a b", **how) if how else part

        def xt(t):
            return px_r[:, t * D:(t + 1) * D] if t < NT - 1 else x_last[:, :]

        hT = mix_r[:, :].rearrange("p (k t) -> p k t", k=KD)
        w_in_sb = [slot(s).rearrange("p (k n) -> p k n", k=KD) for s in range(4)]
        cosT, sinT = trig_r[:, 0:L], trig_r[:, L:2 * L]
        sq = [tmp_r[:, i * CHW:(i + 1) * CHW] for i in (0, 1)]
        qg = [tmp_r[:, i * CHW:(i + 1) * CHW] for i in (2, 3, 4)]
        rt = [tmp_r[:, i * CHW:(i + 1) * CHW] for i in (5, 6)]
        ta, tb = (tmp_r[:, i * CHW:(i + 1) * CHW] for i in (7, 8))
        pbuf = cut(px_r, 0, GROUPS * LP, a=GROUPS)
        lev = [px_r[:, (GROUPS + i) * LP:(GROUPS + i + 1) * LP] for i in (0, 1)]
        mixT = hT
        w_out_sb = [w[:, :].rearrange("p (k n) -> p k n", k=KD) for w in w_out_r]
        hx = [cut(out_r, i * D, D) for i in (0, 1)]
        h2 = [cut(out_r, (2 + i) * D, D) for i in (0, 1)]
        hn = [cut(out_r, (4 + i) * D, D) for i in (0, 1)]
        hnT = [cut(out_r, (6 + i) * D, D, a=KD) for i in (0, 1)]
        g2 = out_r[:, 8 * D:9 * D]
        affT = trig_r[0:E, D:D + L]
        lgT = tmp_r[0:E, 0:NT * P]
        lg = cut(tmp_r, NT * P, NT * E, a=NT)
        mv, mif, mi = (tmp_r[0:E, at:at + 8 * ROUNDS] for at in (1500, 1700, 1900))
        mi = mi.bitcast(U32)
        raw = [at(f"raw{i}", i * 4 * SLOT, [SLOT]) for i in range(RAW)]
        w_hi = [at(f"w_hi{i}", (RAW + i) * 4 * SLOT, [SLOT], F32R) for i in range(CUT)]
        w_lo = [at(f"w_lo{i}", (RAW + CUT) * 4 * SLOT + i * 2 * SLOT, [SLOT], BF16) for i in range(CUT)]
        place = [(RAW + CUT) * 4 * SLOT + CUT * 2 * SLOT]

        def next_at(name, shape, dt=F32):
            here = place[0]
            place[0] += -(-int(np.prod(shape)) * (2 if dt == BF16 else 4) // 32) * 32
            return at(name, here, shape, dt)

        x_hl = next_at("x_hl", [KD, 2 * CAP], F32R)
        x_bf = next_at("x_bf", [KD, CAP], BF16)
        a_hl = next_at("a_hl", [FT, 2 * CAP], F32R)
        a_bf = next_at("a_bf", [FT, CAP], BF16)
        low_sum = [next_at(f"low_sum{i}", [2, CAP]) for i in (0, 1)]
        gu = [next_at(f"gu{i}", [2, 2, CAP]) for i in (0, 1)]
        silu = [next_at(f"silu{i}", [2, CAP]) for i in (0, 1)]
        act_f = [next_at(f"act_f{i}", [2, CAP]) for i in (0, 1)]
        ypart = [next_at(f"ypart{i}", [CAP]) for i in (0, 1)]
        yT = next_at("yT", [KD, CAP])
        xg_r, xgx_r, y_r, yx_r = (next_at(n, [D]) for n in ("xg", "xgx", "y", "yx"))
        xg, xgx, y_sb, yx_sb = xg_r[:, :], xgx_r[0:CAPX, :], y_r[:, :], yx_r[0:CAPX, :]
        assert place[0] <= SMALL
        nc_rest = [SMALL]

        def sb(name, shape, dt=F32):
            here = nc_rest[0]
            nc_rest[0] += -(-int(np.prod(shape[1:])) * 4 // 32) * 32
            return nc.alloc_sbuf_tensor_at(name, shape, dt, offset=base + here)

        cst = sb("cst", [P, C_COS])
        ident = cst[:, C_ID:C_ID + P]
        blk_mean = cst[:, C_BLK:C_BLK + P]
        swap = cst[:, C_SWAP:C_SWAP + P]
        dv_mean = cst[:, C_ONE:C_ONE + P]
        edge = cst[:, C_EDGE:C_COS].rearrange("p (g c) -> p g c", g=GROUPS)
        poolw = sb("poolw", [P, GROUPS, P])
        wr = sb("wr", [P, KD, E])
        g1 = sb("g1", [P, KD])
        gq = sb("gq", [P, 2])
        sg = sb("sg", [P, 2])
        psc = sb("psc", [P, GROUPS])
        lamv = sb("lamv", [P, 4, DH])
        lamj = sb("lamj", [P, DH])
        lam = sb("lam", [P, 5])
        eps = sb("eps", [P, 1])
        st = sb("st", [P, 4, NT])
        st2 = sb("st2", [P, 4, NT])
        mx = sb("mx", [P, 2, 2])
        nb = sb("nb", [P, 2, 2])
        zs = sb("zs", [P, 2, 4, 2])
        rl = sb("rl", [P, 2])
        sm = sb("sm", [P, 3, NT])
        idx = sb("idx", [P, 2, E], I32)
        gat = sb("gat", [P, 2, E])
        gidx = sb("gidx", [P, 2], I32)
        sidx = sb("sidx", [P, 2], I32)
        gcur = sb("gcur", [P, 2])

        PS = ctx.enter_context(nc.psum_tensor("PS", [P, 8, 512], F32))

        def two_banks(b, rows=P):
            return PS[0:rows, b:b + 2, :].rearrange("p b n -> p (b n)")

        s_cst, s_trig, s_par, s_lam, s_g2 = (sem(n) for n in ("s_cst", "s_trig", "s_par", "s_lam", "s_g2"))
        s_x = [sem(f"s_x{t}") for t in range(NT)]
        s_win = [sem(f"s_win{j}") for j in range(4)]
        s_wout = [sem("s_wout0"), sem("s_wout1")]
        s_stage = [sem("s_stage0"), sem("s_stage1")]
        s_stk = [sem("s_stk0"), sem("s_stk1")]
        v_lo_ready = sem("v_lo_ready")
        eps_set, pad_set = sem("eps_set"), sem("pad_set")
        ssq, var_ready, std_ready, xs_ready, xtr, hT_ready = (
            sem(n) for n in ("ssq", "var_ready", "std_ready", "xs_ready", "xtr", "hT_ready"))
        proj_done, proj_taken, ms_done, sw_done, rt_ready, qk_ready, sq_ready = (
            sem(n) for n in ("proj_done", "proj_taken", "ms_done", "sw_done", "rt_ready", "qk_ready",
                             "sq_ready"))
        dve_chain, pool_chain, pads_set, win_ready, pool_d = (
            sem(n) for n in ("dve_chain", "pool_chain", "pads_set", "win_ready", "pool_d"))
        lam_dot, lam_exp, lam_ready = sem("lam_dot"), sem("lam_exp"), sem("lam_ready")
        scores, nb_ready, exp_done, diff_ready, tr_done, tr_hi, tr_lo = (
            sem(n) for n in ("scores", "nb_ready", "exp_done", "diff_ready", "tr_done", "tr_hi", "tr_lo"))
        pv_third, pool_done, b7_taken = sem("pv_third"), sem("pool_done"), sem("b7_taken")
        osq, oms, ort, o_ready = sem("osq"), sem("oms"), sem("ort"), sem("o_ready")
        s_hx = [sem("s_hx0"), sem("s_hx1")]
        wo_done, h2_ready, ssq2, var2, std2, hn_ready, hn_tr, hnT_ready, rout_done, lgT_ready = (
            sem(n) for n in ("wo_done", "h2_ready", "ssq2", "var2", "std2", "hn_ready", "hn_tr",
                             "hnT_ready", "rout_done", "lgT_ready"))
        s_sums, s_table = [sem("s_sums0"), sem("s_sums1")], [sem("s_table0"), sem("s_table1")]
        lg_tr, lg_sub, lg_exp, aff_ready, aff_tr, ids_ready, ids_tr, route_ready = (
            sem(n) for n in ("lg_tr", "lg_sub", "lg_exp", "aff_ready", "aff_tr", "ids_ready",
                             "ids_tr", "route_ready"))
        s_w = [[sem(f"s_w{i}{h}") for h in (0, 1)] for i in range(RAW)]
        gidx_set, s_gath, s_gathx, xg_tr, xh_ready, xl_ready = (
            sem(n) for n in ("gidx_set", "s_gath", "s_gathx", "xg_tr", "xh_ready", "xl_ready"))
        hi_ready, lo_ready, tile_done, part_ready, gu_ready, silu_ready, ahi_ready = (
            sem(n) for n in ("hi_ready", "lo_ready", "tile_done", "part_ready", "gu_ready", "silu_ready",
                             "ahi_ready"))
        a_pool, a_mul, a_dve, ypart_ready, y_ready, y_tr, y_taken, gcur_set = (
            sem(n) for n in ("a_pool", "a_mul", "a_dve", "ypart_ready", "y_ready", "y_tr", "y_taken", "gcur_set"))
        sidx_set, s_scat, s_scatx, s_out = (sem(n) for n in ("sidx_set", "s_scat", "s_scatx", "s_out"))

        STEPS = HEADS * NT
        TURNS = STEPS + 3
        TRIOS = STEPS // 3
        pool_turns = {3 * (n + 1): (2 * n, 2 * n + 1) for n in range(3 * GROUPS // 2)}
        b7_use = {}
        for s in range(TURNS):
            for n in pool_turns.get(s, ()):
                b7_use["pool", n] = len(b7_use)
            if s % 3 == 1 and s >= 4:
                b7_use["pv", (s - 4) // 3] = len(b7_use)
        assert len(b7_use) == TRIOS + 3 * GROUPS

        block = ctx.enter_context(nc.Block())

        @block.sync
        def _(sp):
            sp.dma_start(cst[:], consts[:, 0:C_COS]).then_inc(s_cst, 16)
            for t in range(NT):
                if t == 0:
                    sp.dma_start(xt(0)[0:META, :], meta_tokens).then_inc(s_x[0], 16)
                    sp.dma_start(xt(0)[META:P, :], x[0, 0:P - META, :]).then_inc(s_x[0], 16)
                else:
                    a = P * t - META
                    sp.dma_start(xt(t)[0:ROWS[t], :], x[0, a:a + ROWS[t], :]).then_inc(s_x[t], 16)
            with nc.allow_non_contiguous_dma(reason="small parameters"):
                sp.dma_start(g1[:], ln1_g.rearrange("o (k p) -> p (o k)", p=P)).then_inc(s_par, 16)
                for m in range(2):
                    at = slice(DH * m, DH * m + DH)
                    sp.dma_start(gq[at, 0:1], q_norm_g.rearrange("o p -> p o")).then_inc(s_par, 16)
                    sp.dma_start(gq[at, 1:2], k_norm_g.rearrange("o p -> p o")).then_inc(s_par, 16)
                sp.dma_start(sg[:, 0:1], subln_g.rearrange("o p -> p o")).then_inc(s_par, 16)
                sp.dma_start(psc[:], pool_scale.rearrange("o (g p) -> p (o g)", p=P)).then_inc(s_par, 16)
            for j in (2, 3, 0, 1):
                sp.dma_start(w_in_sb[j], w_in[0].rearrange("(k p) n -> p k n", p=P)[:, :, 512 * j:512 * j + 512]
                             ).then_inc(s_win[j], 16)
                if j == 2:
                    sp.dma_start(trig_r[:], consts[:, C_COS:C_END]).then_inc(s_trig, 16)
                if j == 3:
                    with nc.allow_non_contiguous_dma(reason="small parameters"):
                        for n, v in enumerate((lambda_q1, lambda_k1, lambda_q2, lambda_k2)):
                            sp.dma_start(lamv[:, n, :], v[0, :].partition_broadcast(P)).then_inc(s_lam, 16)
                        sp.dma_start(poolw[:], pool_w[0].rearrange("g c d -> c g d")).then_inc(s_par, 16)
                        sp.dma_start(wr[:], w_router[0].rearrange("(k p) e -> p k e", p=P)).then_inc(s_par, 16)

            def load_w_out(half):
                sp.dma_start(w_out_sb[half], w_out[0].rearrange("(k p) n -> p k n", p=P)[:, :, 512 * half:512 * half + 512]
                             ).then_inc(s_wout[half], 16)

            for i in range(6 * HEADS):
                n, c = i // 3, i % 3
                sp.wait_ge(qk_ready, i + 1)
                sp.dma_start(parts[n, :, :, OFF[c]:OFF[c] + WID[c]].rearrange("a p t -> p a t"),
                             stage[i % 2][:, :, 0:WID[c]].bitcast(F32)).then_inc(s_stage[i % 2], 16)
            sp.wait_ge(proj_done, ITEMS)
            load_w_out(0)
            sp.wait_ge(pool_done, 3 * GROUPS)
            load_w_out(1)

            def load(e, c):
                one, s = bass.ds(e, 1), c % RAW
                for h in range(2):
                    if c < CG:
                        w = (w_gate, w_up)[h][0].rearrange("e (k p) f -> e p k f", p=P)
                        src = w[one, :, :, 256 * c:256 * c + 256]
                    else:
                        w = w_down[0].rearrange("e (k p) n -> e p k n", p=P)
                        src = w[one, :, 8 * h:8 * h + 8, 256 * (c - CG):256 * (c - CG) + 256]
                    sp.dma_start(raw[s][:, 2048 * h:2048 * h + 2048].rearrange("p (k n) -> p k n", k=8),
                                 src.rearrange("e p k n -> p (e k) n")).then_inc(s_w[s][h], 16)

            def load_expert(e, cs=range(CH)):
                for c in cs:
                    sp.wait_ge(lo_ready, TILES * e + 2 * (c - RAW) + 2)
                    load(e, c)

            sp.wait_ge(scores, 6 * NT)
            load(0, 3)
            sp.wait_ge(scores, 8 * NT)
            load(0, 0)
            sp.wait_ge(pv_third, 3 * TRIOS)
            sp.dma_start(g2, ln2_g[0, :].partition_broadcast(P)).then_inc(s_g2, 16)

            def load_hx(t):
                b = t % 2
                if t >= 2:
                    sp.wait_ge(h2_ready, t - 1)
                if t == 0:
                    sp.dma_start(hx[0][0:META, :], meta_tokens).then_inc(s_hx[0], 16)
                    sp.dma_start(hx[0][META:P, :], x[0, 0:P - META, :]).then_inc(s_hx[0], 16)
                else:
                    a = P * t - META
                    sp.dma_start(hx[b][0:ROWS[t], :], x[0, a:a + ROWS[t], :]).then_inc(s_hx[b], 16)

            load_hx(0)
            load_hx(1)
            for t in range(NT):
                R = ROWS[t]
                if t + 2 < NT:
                    load_hx(t + 2)
                sp.wait_ge(h2_ready, t + 1)
                sp.dma_start(sums[P * t:P * t + R, :], h2[t % 2][0:R, :]).then_inc(s_sums[t % 2], 16)
                sp.wait_ge(hn_ready, t + 1)
                sp.dma_start(table[P * t:P * t + R, :], hn[t % 2][0:R, :]).then_inc(s_table[t % 2], 16)
            sp.wait_ge(wo_done, NT)
            load(0, 1)
            load(0, 2)
            load_expert(0, range(RAW, CH))
            with sp.Fori(1, E) as e:
                load_expert(e)
            sp.wait_ge(s_scat, 16 * E)
            sp.wait_ge(s_scatx, 16 * E)
            sp.dma_start(out[0], sums[META:L, :]).then_inc(s_out, 16)
            sp.wait_ge(s_out, 16)

        @block.gpsimd
        def _(pool):
            steps = [0]

            def link(ins):
                steps[0] += 1
                ins.then_inc(pool_chain, 1)
                pool.wait_ge(pool_chain, steps[0])

            pool.memset(eps[:], EPS).then_inc(eps_set, 1)
            pool.wait_ge(xtr, NT)
            for g in range(GROUPS):
                pool.memset(pbuf[:, g, 0:PADW], 0.0).then_inc(pads_set, 1)
                pool.memset(pbuf[:, g, PADW + L:LP], 0.0).then_inc(pads_set, 1)
            pool.wait_ge(pads_set, 2 * GROUPS)
            n = 0
            for g in range(GROUPS):
                pool.wait_ge(proj_taken, G0 + 3 * (g + 1))
                src = pbuf[:, g, :]
                for lv in range(g + 1):
                    reach = 2 ** g - 2 ** lv if lv else 2 ** g - 1
                    lo, hi = PADW - reach, PADW + L + reach
                    a, b = (1, 0) if lv == 0 else (2 ** (lv - 1), 2 ** (lv - 1))
                    if lv == 0 and g:
                        pool.wait_ge(pool_d, g)
                    dst = lev[n % 2]
                    ins = pool.tensor_tensor(dst[:, lo:hi], src[:, lo - a:hi - a], src[:, lo + b:hi + b], ALU.add)
                    if lv < g:
                        link(ins)
                    src = dst
                    n += 1
                ins.then_inc(win_ready, 1)

            def load_heads(h):
                for i in (0, 1):
                    pool.wait_ge(s_stage[i], 16 * 3 * (h + 1))
                for half in range(2):
                    at = slice(DH * half, DH * half + DH)
                    for m in range(2):
                        pool.dma_start(stk[h % 2][at, m, 0:2, :],
                                     parts[2 * h, :, DH * m:DH * m + DH, :].rearrange("a p t -> p a t")).then_inc(s_stk[h % 2], 16)
                    pool.dma_start(stk[h % 2][at, :, 2, :],
                                 parts[2 * h + 1, half].rearrange("(m p) t -> p m t", m=2)).then_inc(s_stk[h % 2], 16)

            load_heads(0)
            pool.wait_ge(proj_done, ITEMS)
            load_heads(1)
            pool.wait_ge(scores, 2 * NT)
            load_heads(2)
            pool.wait_ge(scores, 4 * NT)
            load_heads(3)

            def gather(e):
                pool.tensor_copy(gidx[:, 0:1], idx[:, 0, bass.ds(e, 1)]).then_inc(gidx_set, 1)
                pool.tensor_copy(gidx[0:CAPX, 1:2], idx[0:CAPX, 1, bass.ds(e, 1)]).then_inc(gidx_set, 1)
                pool.wait_ge(gidx_set, 2)
                pool.indirect_dma_start(xg, None, table, bass.IndirectOffsetOnAxis(ap=gidx[:, 0:1], axis=0)
                                        ).then_inc(s_gath, 16)
                pool.indirect_dma_start(xgx, None, table, bass.IndirectOffsetOnAxis(ap=gidx[0:CAPX, 1:2], axis=0)
                                        ).then_inc(s_gathx, 16)
                pool.sem_clear(gidx_set)

            def scatter(e, first):
                if not first:
                    pool.wait_ge(s_scat, 16 * e)
                    pool.wait_ge(s_scatx, 16 * e)
                pool.wait_ge(y_taken, 2 * e + 2)
                pool.tensor_copy(sidx[:, 0:1], idx[:, 0, bass.ds(e, 1)]).then_inc(sidx_set, 1)
                pool.tensor_copy(sidx[0:CAPX, 1:2], idx[0:CAPX, 1, bass.ds(e, 1)]).then_inc(sidx_set, 1)
                pool.wait_ge(sidx_set, 2)
                pool.indirect_dma_start(sums, bass.IndirectOffsetOnAxis(ap=sidx[:, 0:1], axis=0), y_sb, None,
                                        compute_op=ALU.add).then_inc(s_scat, 16)
                pool.indirect_dma_start(sums, bass.IndirectOffsetOnAxis(ap=sidx[0:CAPX, 1:2], axis=0), yx_sb, None,
                                        compute_op=ALU.add).then_inc(s_scatx, 16)
                pool.sem_clear(sidx_set)

            for s in (*s_table, *s_sums):
                pool.wait_ge(s, 16 * (NT // 2 + (s in (s_table[0], s_sums[0]))))
            pool.wait_ge(route_ready, 4)
            def hidden(e, c, first=False):
                if c == 1 and not first:
                    pool.wait_ge(a_dve, e)
                pool.wait_ge(silu_ready, CG * e + c + 1)
                up = gu[c % 2][:, :, 1, :]
                pool.tensor_tensor(act_f[c % 2][:], silu[c % 2][:], up, ALU.mult).then_inc(a_pool, 1)
                pool.tensor_tensor(a_bf[:, 2 * c:2 * c + 2, :], silu[c % 2][:], up, ALU.mult).then_inc(a_pool, 1)
                pool.wait_ge(ahi_ready, CG * e + c + 1)
                pool.tensor_tensor(a_hl[:, 2 * c:2 * c + 2, CAP:2 * CAP], act_f[c % 2][:],
                                   a_hl[:, 2 * c:2 * c + 2, 0:CAP].bitcast(F32), ALU.subtract).then_inc(a_pool, 1)

            def expert(e, n=2, last=False):
                if not last:
                    if n:
                        pool.wait_ge(xg_tr, 3 * e + 3)
                    else:
                        pool.wait_ge(xg_tr, 3)
                    gather(e + 1)
                for c in range(CG - 2):
                    hidden(e, c, first=n == 0)
                if n:
                    scatter(e - 1, n == 1)
                hidden(e, CG - 2)

            gather(0)
            expert(0, 0)
            expert(1, 1)
            with pool.Fori(2, E - 1) as e:
                expert(e)
            expert(E - 1, last=True)
            scatter(E - 1, False)
            pool.wait_ge(s_scat, 16 * E)
            pool.wait_ge(s_scatx, 16 * E)

        @block.scalar
        def _(act):
            act.wait_ge(eps_set, 1)
            def root1(t):
                R = ROWS[t]
                act.wait_ge(var_ready, t + 1)
                act.activation(st[0:R, 2, t:t + 1], st[0:R, 1, t:t + 1], ACT.Sqrt).then_inc(std_ready, 1)

            for t in range(NT):
                R = ROWS[t]
                act.wait_ge(s_x[t], 32 if t == 0 else 16)
                act.activation(two_banks(4 + 2 * (t % 2), R), xt(t)[0:R, :], ACT.Square,
                               accum_out=st[0:R, 0, t:t + 1]).then_inc(ssq, 1)
                if t:
                    root1(t - 1)
            root1(NT - 1)

            def rope_root(i):
                act.wait_ge(ms_done, i + 1)
                if i >= 2:
                    act.wait_ge(qk_ready, i - 1)
                W = WID[i % 3]
                act.activation(rt[i % 2][:, 0:W], PS[:, 4 + i % 2, 0:W], ACT.Sqrt, bias=eps[:, 0:1]).then_inc(rt_ready, 1)

            act.wait_ge(s_par, 16 * 9)
            for t in range(NT):
                act.wait_ge(proj_done, t + 1)
                act.activation(v_hi[0:KEYS[t], t, :], PS[0:KEYS[t], t % 4, :], ACT.Copy).then_inc(proj_taken, 1)
            for n in range(3 * GROUPS):
                i, g, c = G0 + n, n // 3, n % 3
                act.wait_ge(proj_done, i + 1)
                act.activation(pbuf[:, g, PADW + OFF[c]:PADW + OFF[c] + WID[c]], PS[:, i % 4, 0:WID[c]], ACT.Copy
                               ).then_inc(proj_taken, 1)
            for i in range(6 * HEADS):
                n, W, bank = i // 3, WID[i % 3], (Q0 + i) % 4
                act.wait_ge(proj_done, Q0 + i + 1)
                if i >= 2:
                    act.wait_ge(ms_done, i - 1)
                act.activation(sq[i % 2][:, 0:W], PS[:, bank, 0:W], ACT.Square).then_inc(sq_ready, 1)
                if i >= 3:
                    act.wait_ge(qk_ready, i - 2)
                    act.wait_ge(sw_done, i - 2)
                act.activation(qg[i % 3][:, 0:W], PS[:, bank, 0:W], ACT.Identity, scale=gq[:, n % 2:n % 2 + 1]
                               ).then_inc(proj_taken, 1)
                if i:
                    rope_root(i - 1)
            rope_root(23)
            act.wait_ge(lam_dot, 2)
            act.activation(lam[:, 2:4], lam[:, 0:2], ACT.Exp).then_inc(lam_exp, 1)

            def exps(s, m):
                R = ROWS[s % NT]
                act.wait_ge(nb_ready, 2 * s + m + 1)
                if m == 0 and s >= 3:
                    act.wait_ge(tr_done, 3 * (s - 2))
                if m == 0 and s >= 2:
                    act.wait_ge(diff_ready, s - 1)
                p = probs_a[s % 3] if m == 0 else probs_b[s % 2]
                act.activation(p[0:R, :].rearrange("p (c t) -> p c t", c=3), PS[0:R, 3 * m:3 * m + 3, 0:CHW], ACT.Exp,
                               bias=nb[0:R, s % 2, m:m + 1], scale=SCALE, accum_out=zs[0:R, s % 2, 0, m:m + 1]
                               ).then_inc(exp_done, 1)

            def take_hi(s, b):
                R, col = ROWS[s % NT], (s % 3) * P
                act.wait_ge(tr_done, 3 * s + b + 1)
                if s % 3 == 0 and s:
                    act.wait_ge(pv_third, s - 3 + b + 1)
                act.activation(aT_hi[:, 3 * b:3 * b + 3, col:col + R],
                               PS[:, 6, 0:3 * P].rearrange("p (n r) -> p n r", n=3)[:, :, 0:R], ACT.Copy).then_inc(tr_hi, 1)

            def take_pv(j):
                h, at = j // 3, 3 * P * (j % 3)
                N = sum(ROWS[3 * (j % 3):3 * (j % 3) + 3])
                act.wait_ge(pv_third, 3 * j + 3)
                act.activation(mixT[:, h, at:at + N], PS[:, 7, 0:N], ACT.Copy).then_inc(b7_taken, 1)

            def take_pool(n):
                g, c = n // 3, n % 3
                act.wait_ge(pool_done, n + 1)
                act.activation(mixT[:, HEADS + g, OFF[c]:OFF[c] + WID[c]], PS[:, 7, 0:WID[c]], ACT.Identity,
                               scale=psc[:, g:g + 1]).then_inc(b7_taken, 1)

            for i in (0, 1):
                act.wait_ge(s_stage[i], 16 * 3 * HEADS)
            for s in range(TURNS):
                turn = 0 <= s - 2 < STEPS
                if turn:
                    take_hi(s - 2, 0)
                if s < STEPS:
                    exps(s, 0)
                if s in pool_turns:
                    take_pool(pool_turns[s][0])
                if turn:
                    take_hi(s - 2, 1)
                if s < STEPS:
                    exps(s, 1)
                if turn:
                    take_hi(s - 2, 2)
                if s in pool_turns:
                    take_pool(pool_turns[s][1])
                if s % 3 == 2 and s >= 5:
                    take_pv((s - 5) // 3)

            def o_root(j):
                act.wait_ge(oms, j + 1)
                if j >= 2:
                    act.wait_ge(o_ready, j - 1)
                W = WID[j % 3]
                act.activation(rt[j % 2][:, 0:W], PS[:, j % 2, 0:W], ACT.Sqrt, bias=eps[:, 0:1]).then_inc(ort, 1)

            act.wait_ge(b7_taken, len(b7_use))
            for j in range(12):
                h, c = j // 3, j % 3
                if j >= 2:
                    act.wait_ge(oms, j - 1)
                act.activation(sq[j % 2][:, 0:WID[c]], mixT[:, h, OFF[c]:OFF[c] + WID[c]], ACT.Square).then_inc(osq, 1)
                if j:
                    o_root(j - 1)
            o_root(11)

            def take_hn(t):
                R = ROWS[t]
                act.wait_ge(hn_tr, t + 1)
                if t >= 2:
                    act.wait_ge(rout_done, t - 1)
                act.activation(hnT[t % 2][:, :, 0:R], two_banks(4).rearrange("p (k r) -> p k r", k=KD)[:, :, 0:R],
                               ACT.Copy).then_inc(hnT_ready, 1)
                act.wait_ge(rout_done, t + 1)
                act.activation(lgT[:, P * t:P * t + R], PS[0:E, 6, 0:R], ACT.Copy).then_inc(lgT_ready, 1)

            for t in range(NT):
                R, b = ROWS[t], t % 2
                act.wait_ge(h2_ready, t + 1)
                if t >= 2:
                    act.wait_ge(s_table[b], 16 * (t // 2))
                    act.wait_ge(hn_tr, t - 1)
                act.activation(hn[b][0:R, :], h2[b][0:R, :], ACT.Square, accum_out=st2[0:R, 0, t:t + 1]).then_inc(ssq2, 1)
                act.wait_ge(var2, t + 1)
                act.activation(st2[0:R, 2, t:t + 1], st2[0:R, 1, t:t + 1], ACT.Sqrt).then_inc(std2, 1)
                if t:
                    take_hn(t - 1)
            take_hn(NT - 1)
            act.wait_ge(lg_sub, 1)
            act.activation(lg, lg, ACT.Exp).then_inc(lg_exp, 1)

            def cut_hi(e, c, h, first=False):
                if not first:
                    act.wait_ge(tile_done, TILES * e + 2 * (c - CUT) + 2)
                act.wait_ge(s_w[c % RAW][h], 16 * (CH // RAW * e + c // RAW + 1))
                act.activation(w_hi[c % CUT][:, 2048 * h:2048 * h + 2048], raw[c % RAW][:, 2048 * h:2048 * h + 2048],
                               ACT.Copy).then_inc(hi_ready, 1)

            def take_part(e, n):
                act.wait_ge(tile_done, TILES * e + n + 1)
                act.activation(low_sum[n % 2][:], PS[:, 2 * (n % 2):2 * (n % 2) + 2, CAP:2 * CAP], ACT.Copy
                               ).then_inc(part_ready, 1)

            def silus(e, c, first=False):
                if c == 0 and not first:
                    act.wait_ge(a_pool, 3 * (CG - 1) * e)
                elif c == 1 and not first:
                    act.wait_ge(a_dve, e)
                elif c >= 2:
                    act.wait_ge(a_pool, 3 * (CG - 1) * e + 3 * (c - 2) + 3)
                act.wait_ge(gu_ready, 2 * CG * e + 2 * c + 2)
                act.activation(silu[c % 2][:], gu[c % 2][:, :, 0, :], ACT.Silu).then_inc(silu_ready, 1)

            def hidden_hi(e, c):
                if c < CG - 1:
                    act.wait_ge(a_pool, 3 * (CG - 1) * e + 3 * c + 1)
                else:
                    act.wait_ge(a_mul, e + 1)
                act.activation(a_hl[:, 2 * c:2 * c + 2, 0:CAP], act_f[c % 2][:], ACT.Copy).then_inc(ahi_ready, 1)

            def take_ypart(e, t):
                act.wait_ge(tile_done, TILES * e + 2 * CG + t + 1)
                act.activation(ypart[t % 2][:], PS[:, 4 + t % 2, CAP:2 * CAP], ACT.Copy).then_inc(ypart_ready, 1)

            def take_x(e, b):
                n = min(3, KD - 3 * b)
                act.wait_ge(xg_tr, 3 * e + b + 1)
                act.activation(x_hl[:, 3 * b:3 * b + n, 0:CAP],
                               PS[:, 6 + b % 2, 0:n * CAP].rearrange("p (k c) -> p k c", k=n), ACT.Copy
                               ).then_inc(xh_ready, 1)

            def take_y(e, rest, first=False):
                act.wait_ge(y_tr, 2 * e + rest + 1)
                act.wait_ge(gcur_set, 2 * e + 2)
                if not rest:
                    if not first:
                        act.wait_ge(s_scat, 16 * e)
                        act.wait_ge(s_scatx, 16 * e)
                    act.activation(y_sb, two_banks(6), ACT.Identity, scale=gcur[:, 0:1]).then_inc(y_taken, 1)
                else:
                    act.activation(yx_sb, two_banks(6, CAPX), ACT.Identity, scale=gcur[0:CAPX, 1:2]).then_inc(y_taken, 1)

            def expert(e, n=2, last=False):
                for c in range(CH):
                    ahead = not (last and c + 2 >= CH)
                    early = n == 0 and c + 2 < CUT
                    if ahead:
                        cut_hi(e, c + 2, 0, first=early)
                    if c == CG:
                        silus(e, CG - 1, first=n == 0)
                        hidden_hi(e, CG - 1)
                    take_part(e, 2 * c) if c < CG else take_ypart(e, 2 * (c - CG))
                    if 1 <= c < CG:
                        silus(e, c - 1, first=n == 0)
                    if ahead:
                        cut_hi(e, c + 2, 1, first=early)
                    if 1 <= c < CG:
                        hidden_hi(e, c - 1)
                    take_part(e, 2 * c + 1) if c < CG else take_ypart(e, 2 * (c - CG) + 1)
                    if n and c in (2, 4):
                        take_y(e - 1, c == 4, first=n == 1)
                    if not last and c == CG + 1:
                        take_x(e + 1, 0)
                        take_x(e + 1, 1)
                    if not last and c == CG + 2:
                        take_x(e + 1, 2)

            act.wait_ge(wo_done, NT)
            for c in range(2):
                for h in range(2):
                    cut_hi(0, c, h, first=True)
            for b in range(3):
                take_x(0, b)
            expert(0, 0)
            expert(1, 1)
            with act.Fori(2, E - 1) as e:
                expert(e)
            expert(E - 1, last=True)
            take_y(E - 1, 0)
            take_y(E - 1, 1)

        @block.vector
        def _(dve):
            steps = [0]

            def link(ins):
                steps[0] += 1
                ins.then_inc(dve_chain, 1)
                dve.wait_ge(dve_chain, steps[0])

            def scale_rows(t):
                R = ROWS[t]
                dve.wait_ge(std_ready, t + 1)
                link(dve.reciprocal(st[0:R, 3, t:t + 1], st[0:R, 2, t:t + 1]))
                dve.tensor_scalar(xt(t)[0:R, :], xt(t)[0:R, :], st[0:R, 3, t:t + 1], None, ALU.mult).then_inc(xs_ready, 1)

            def take_xt(t):
                R = ROWS[t]
                dve.wait_ge(xtr, t + 1)
                for b in range(2):
                    gain = g1[:, 4 * b:4 * b + 4].unsqueeze(2).broadcast_to([P, 4, R])
                    dve.tensor_tensor(hT[:, 4 * b:4 * b + 4, P * t:P * t + R],
                                      PS[:, 2 * (t % 2) + b, :].rearrange("p (k r) -> p k r", k=4)[:, :, 0:R],
                                      gain, ALU.mult).then_inc(hT_ready, 1)

            for t in range(NT + 2):
                if t < NT:
                    R = ROWS[t]
                    dve.wait_ge(ssq, t + 1)
                    dve.tensor_scalar(st[0:R, 1, t:t + 1], st[0:R, 0, t:t + 1], 1.0 / D, EPS, ALU.mult, ALU.add
                                      ).then_inc(var_ready, 1)
                if 1 <= t <= NT:
                    scale_rows(t - 1)
                if t == 2:
                    dve.wait_ge(s_par, 16 * 9)
                if t >= 2:
                    take_xt(t - 2)

            for t in range(NT):
                R = KEYS[t]
                dve.wait_ge(proj_taken, t + 1)
                dve.tensor_tensor(v_lo[0:R, t, :], PS[0:R, t % 4, :], v_hi[0:R, t, :].bitcast(F32), ALU.subtract
                                  ).then_inc(v_lo_ready, 1)

            dve.wait_ge(s_lam, 64)
            for m in range(2):
                ins = dve.tensor_tensor_reduce(lamj[:], lamv[:, 2 * m, :], lamv[:, 2 * m + 1, :], 1.0, 0.0,
                                               ALU.mult, ALU.add, lam[:, m:m + 1])
                ins.then_inc(lam_dot, 1)
                dve.wait_ge(lam_dot, m + 1)
            dve.tensor_scalar(sg[:, 1:2], sg[:, 0:1], 1.0 - LAM_INIT, None, ALU.mult)

            def pool_diff(g):
                w = WINDOWS[g]
                s = lev[(sum(range(g + 2)) - 1) % 2]
                dve.wait_ge(win_ready, g + 1)
                for a, b in ((PADW, 0), (PADW + L - 8, 8)):
                    link(dve.tensor_tensor(s[:, a:a + 8], s[:, a:a + 8], edge[:, g, b:b + 8], ALU.mult))
                dve.scalar_tensor_tensor(out=pbuf[:, g, PADW:PADW + L], in0=s[:, PADW:PADW + L], scalar=1.0 / w,
                                         in1=pbuf[:, g, PADW:PADW + L], op0=ALU.mult, op1=ALU.subtract
                                         ).then_inc(pool_d, 1)

            dve.wait_ge(s_trig, 16)
            for i in range(6 * HEADS):
                W = WID[i % 3]
                at = slice(OFF[i % 3], OFF[i % 3] + W)
                hi, lo = (stage[i % 2][:, n, 0:W] for n in (0, 1))
                dve.wait_ge(rt_ready, i + 1)
                link(dve.reciprocal(rt[i % 2][:, 0:W], rt[i % 2][:, 0:W]))
                dve.tensor_tensor(ta[:, 0:W], qg[i % 3][:, 0:W], cosT[:, at], ALU.mult)
                dve.wait_ge(sw_done, i + 1)
                link(dve.tensor_tensor(tb[:, 0:W], PS[:, 6 + i % 2, 0:W], sinT[:, at], ALU.mult))
                link(dve.tensor_tensor(ta[:, 0:W], ta[:, 0:W], tb[:, 0:W], ALU.add))
                if i >= 2:
                    dve.wait_ge(s_stage[i % 2], 16 * (i // 2))
                link(dve.tensor_tensor(hi, ta[:, 0:W], rt[i % 2][:, 0:W], ALU.mult))
                link(dve.tensor_tensor(tb[:, 0:W], ta[:, 0:W], rt[i % 2][:, 0:W], ALU.mult))
                dve.tensor_tensor(lo, tb[:, 0:W], hi.bitcast(F32), ALU.subtract).then_inc(qk_ready, 1)
                if i % 5 == 4 and i // 5 < GROUPS:
                    pool_diff(i // 5)

            dve.wait_ge(lam_exp, 1)
            link(dve.tensor_tensor(lam[:, 4:5], lam[:, 2:3], lam[:, 3:4], ALU.subtract))
            link(dve.tensor_scalar(lam[:, 4:5], lam[:, 4:5], LAM_INIT, None, ALU.add))

            def maxes(s, m):
                R, b = ROWS[s % NT], s % 2
                dve.wait_ge(scores, 2 * s + m + 1)
                link(dve.tensor_reduce(mx[0:R, b, m:m + 1], PS[0:R, 3 * m:3 * m + 3, 0:CHW], AX.XY, ALU.max))
                dve.tensor_scalar(nb[0:R, b, m:m + 1], mx[0:R, b, m:m + 1], -SCALE, None, ALU.mult).then_inc(nb_ready, 1)

            def sums_of(s):
                R, b = ROWS[s % NT], s % 2
                dve.wait_ge(exp_done, 2 * s + 2)
                for m, p in enumerate((probs_a[s % 3], probs_b[b])):
                    twice = p[0:R, :].rearrange("p (c t) -> p c t", c=3)[:, 1:3, 0:2]
                    ins = dve.tensor_reduce(zs[0:R, b, 1, m:m + 1], twice, AX.XY, ALU.add)
                    link(ins)
                link(dve.tensor_tensor(zs[0:R, b, 2, :], zs[0:R, b, 0, :], zs[0:R, b, 1, :], ALU.subtract))
                link(dve.reciprocal(zs[0:R, b, 3, :], zs[0:R, b, 2, :]))
                link(dve.tensor_tensor(rl[0:R, b:b + 1], zs[0:R, b, 3, 1:2], lam[0:R, 4:5], ALU.mult))
                link(dve.tensor_scalar(probs_b[b][0:R, :], probs_b[b][0:R, :], rl[0:R, b:b + 1], None, ALU.mult))

            def difference(s):
                R, b = ROWS[s % NT], s % 2
                dve.scalar_tensor_tensor(out=probs_a[s % 3][0:R, :], in0=probs_a[s % 3][0:R, :],
                                         scalar=zs[0:R, b, 3, 0:1], in1=probs_b[b][0:R, :],
                                         op0=ALU.mult, op1=ALU.subtract).then_inc(diff_ready, 1)

            def take_lo(s, b):
                R, col = ROWS[s % NT], (s % 3) * P
                dve.wait_ge(tr_hi, 3 * s + b + 1)
                dve.tensor_tensor(aT_lo[:, 3 * b:3 * b + 3, col:col + R],
                                  PS[:, 6, 0:3 * P].rearrange("p (n r) -> p n r", n=3)[:, :, 0:R],
                                  aT_hi[:, 3 * b:3 * b + 3, col:col + R].bitcast(F32), ALU.subtract).then_inc(tr_lo, 1)

            for s in range(TURNS):
                turn = 0 <= s - 2 < STEPS
                if s < STEPS:
                    maxes(s, 0)
                if turn:
                    take_lo(s - 2, 0)
                if 0 <= s - 1 < STEPS:
                    sums_of(s - 1)
                if s < STEPS:
                    maxes(s, 1)
                if turn:
                    take_lo(s - 2, 1)
                if 0 <= s - 1 < STEPS:
                    difference(s - 1)
                if turn:
                    take_lo(s - 2, 2)

            for j in range(12):
                h, c = j // 3, j % 3
                W = WID[c]
                part = mixT[:, h, OFF[c]:OFF[c] + W]
                dve.wait_ge(ort, j + 1)
                link(dve.reciprocal(rt[j % 2][:, 0:W], rt[j % 2][:, 0:W]))
                dve.scalar_tensor_tensor(out=part, in0=part, scalar=sg[:, 1:2], in1=rt[j % 2][:, 0:W],
                                         op0=ALU.mult, op1=ALU.mult).then_inc(o_ready, 1)

            dve.memset(lgT[:, L:NT * P], 0.0).then_inc(pad_set, 1)
            dve.wait_ge(s_g2, 16)
            for t in range(NT):
                R, b = ROWS[t], t % 2
                dve.wait_ge(wo_done, t + 1)
                dve.wait_ge(s_hx[b], 16 * (t // 2 + 1 + (b == 0)))
                if t >= 2:
                    dve.wait_ge(s_sums[b], 16 * (t // 2))
                dve.tensor_tensor(h2[b][0:R, :], two_banks(2 * b, R), hx[b][0:R, :], ALU.add).then_inc(h2_ready, 1)
                dve.wait_ge(ssq2, t + 1)
                dve.tensor_scalar(st2[0:R, 1, t:t + 1], st2[0:R, 0, t:t + 1], 1.0 / D, EPS, ALU.mult, ALU.add
                                  ).then_inc(var2, 1)
                dve.wait_ge(std2, t + 1)
                link(dve.reciprocal(st2[0:R, 3, t:t + 1], st2[0:R, 2, t:t + 1]))
                dve.scalar_tensor_tensor(out=hn[b][0:R, :], in0=h2[b][0:R, :], scalar=st2[0:R, 3, t:t + 1],
                                         in1=g2[0:R, :], op0=ALU.mult, op1=ALU.mult).then_inc(hn_ready, 1)

            dve.wait_ge(lg_tr, 1)
            lp = PS[:, 7, 0:NT * E].rearrange("p (t e) -> p t e", t=NT)
            link(dve.tensor_reduce(sm[:, 0, :], lp, AX.X, ALU.max))
            dve.tensor_tensor(lg, lp, sm[:, 0, :].unsqueeze(2).broadcast_to([P, NT, E]), ALU.subtract).then_inc(lg_sub, 1)
            dve.wait_ge(lg_exp, 1)
            link(dve.tensor_reduce(sm[:, 1, :], lg, AX.X, ALU.add))
            link(dve.reciprocal(sm[:, 2, :], sm[:, 1, :]))
            dve.tensor_tensor(lg, lg, sm[:, 2, :].unsqueeze(2).broadcast_to([P, NT, E]), ALU.mult).then_inc(aff_ready, 1)
            dve.wait_ge(aff_tr, 1)
            link(dve.tensor_copy(affT, PS[0:E, 0:3, :].rearrange("p b n -> p (b n)")[:, 0:L]))
            for r in range(ROUNDS):
                best = mv[:, 8 * r:8 * r + 8]
                link(dve.max(best, affT))
                link(dve.max_index(mi[:, 8 * r:8 * r + 8], best, affT))
                if r < ROUNDS - 1:
                    link(dve.match_replace(affT, best, affT, -1.0))
            dve.tensor_copy(mif, mi).then_inc(ids_ready, 1)
            dve.wait_ge(ids_tr, 1)
            for n, (dst, rows) in enumerate(((idx[:, 0, :], P), (gat[:, 0, :], P), (idx[0:CAPX, 1, :], CAPX),
                                             (gat[0:CAPX, 1, :], CAPX))):
                dve.tensor_copy(dst, PS[0:rows, 4, n * E:(n + 1) * E]).then_inc(route_ready, 1)

            def cut_lo(e, c, h):
                cols = slice(2048 * h, 2048 * h + 2048)
                dve.wait_ge(hi_ready, TILES * e + 2 * c + h + 1)
                dve.tensor_tensor(w_lo[c % CUT][:, cols], raw[c % RAW][:, cols], w_hi[c % CUT][:, cols].bitcast(F32),
                                  ALU.subtract).then_inc(lo_ready, 1)

            def sum_gu(e, n, first=False):
                c = n // 2
                if n == 0 and not first:
                    dve.wait_ge(a_pool, 3 * (CG - 1) * e)
                elif n == 2 and not first:
                    dve.wait_ge(a_dve, e)
                elif n % 2 == 0 and n >= 4:
                    dve.wait_ge(a_pool, 3 * (CG - 1) * e + 3 * (c - 2) + 3)
                dve.wait_ge(part_ready, 2 * CG * e + n + 1)
                dve.tensor_tensor(gu[c % 2][:, n % 2, :, :], PS[:, 2 * (n % 2):2 * (n % 2) + 2, 0:CAP], low_sum[n % 2][:],
                                  ALU.add).then_inc(gu_ready, 1)

            def last_hidden(e):
                c = CG - 1
                dve.wait_ge(a_pool, 3 * (CG - 1) * e + 3 * (c - 2) + 3)
                dve.wait_ge(silu_ready, CG * e + c + 1)
                up = gu[c % 2][:, :, 1, :]
                dve.tensor_tensor(act_f[c % 2][:], silu[c % 2][:], up, ALU.mult).then_inc(a_mul, 1)
                dve.tensor_tensor(a_bf[:, 2 * c:2 * c + 2, :], silu[c % 2][:], up, ALU.mult)
                dve.wait_ge(ahi_ready, CG * e + c + 1)
                dve.tensor_tensor(a_hl[:, 2 * c:2 * c + 2, CAP:2 * CAP], act_f[c % 2][:],
                                  a_hl[:, 2 * c:2 * c + 2, 0:CAP].bitcast(F32), ALU.subtract).then_inc(a_dve, 1)

            def sum_y(e, t, first=False):
                if t == 0 and not first:
                    dve.wait_ge(y_tr, 2 * e)
                dve.wait_ge(ypart_ready, KD * e + t + 1)
                dve.tensor_tensor(yT[:, t, :], PS[:, 4 + t % 2, 0:CAP], ypart[t % 2][:], ALU.add).then_inc(y_ready, 1)

            def take_x(e, b):
                n = min(3, KD - 3 * b)
                ks = slice(3 * b, 3 * b + n)
                src = PS[:, 6 + b % 2, 0:n * CAP].rearrange("p (k c) -> p k c", k=n)
                dve.wait_ge(xh_ready, 3 * e + b + 1)
                dve.tensor_tensor(x_hl[:, ks, CAP:2 * CAP], src, x_hl[:, ks, 0:CAP].bitcast(F32), ALU.subtract
                                  ).then_inc(xl_ready, 1)
                dve.tensor_copy(x_bf[:, ks, :], src).then_inc(xl_ready, 1)

            def set_gates(e, first=False):
                if not first:
                    dve.wait_ge(y_taken, 2 * e)
                dve.tensor_copy(gcur[:, 0:1], gat[:, 0, bass.ds(e, 1)]).then_inc(gcur_set, 1)
                dve.tensor_copy(gcur[0:CAPX, 1:2], gat[0:CAPX, 1, bass.ds(e, 1)]).then_inc(gcur_set, 1)

            def expert(e, n=2, last=False):
                for c in range(CH):
                    ahead = not (last and c + 2 >= CH)
                    if c == CG:
                        last_hidden(e)
                    if ahead:
                        cut_lo(e, c + 2, 0)
                    sum_gu(e, 2 * c, n == 0) if c < CG else sum_y(e, 2 * (c - CG), n == 0)
                    if ahead:
                        cut_lo(e, c + 2, 1)
                    sum_gu(e, 2 * c + 1, n == 0) if c < CG else sum_y(e, 2 * (c - CG) + 1, n == 0)
                    if n and c == 0:
                        set_gates(e - 1, n == 1)
                    if not last and c == CG + 1:
                        take_x(e + 1, 0)
                        take_x(e + 1, 1)
                    if not last and c == CG + 2:
                        take_x(e + 1, 2)

            for c in range(2):
                for h in range(2):
                    cut_lo(0, c, h)
            for b in range(3):
                take_x(0, b)
            expert(0, 0)
            expert(1, 1)
            with dve.Fori(2, E - 1) as e:
                expert(e)
            expert(E - 1, last=True)
            set_gates(E - 1)

        @block.tensor
        def _(pe):
            pe.wait_ge(s_cst, 16)
            for t in range(NT):
                R = ROWS[t]
                pe.wait_ge(xs_ready, t + 1)
                if t >= 2:
                    pe.wait_ge(hT_ready, 2 * (t - 1))
                for k in range(KD):
                    ins = pe.transpose(PS[:, 2 * (t % 2) + k // 4, (k % 4) * P:(k % 4) * P + R],
                                       xt(t)[0:R, k * P:(k + 1) * P], ident[0:R, 0:R])
                ins.then_inc(xtr, 1)

            def stats(i):
                W = WID[i % 3]
                pe.wait_ge(sq_ready, i + 1)
                if i >= 2:
                    pe.wait_ge(rt_ready, i - 1)
                pe.matmul(PS[:, 4 + i % 2, 0:W], blk_mean, sq[i % 2][:, 0:W], start=True, stop=True).then_inc(ms_done, 1)
                pe.wait_ge(proj_taken, Q0 + i + 1)
                if i >= 2:
                    pe.wait_ge(qk_ready, i - 1)
                pe.matmul(PS[:, 6 + i % 2, 0:W], swap, qg[i % 3][:, 0:W], start=True, stop=True).then_inc(sw_done, 1)

            def bank_free(i):
                if i >= 4:
                    pe.wait_ge(proj_taken, i - 3)
                    if i - 4 < NT:
                        pe.wait_ge(v_lo_ready, i - 3)

            pe.wait_ge(hT_ready, 2 * NT)
            pe.wait_ge(s_win[2], 16)
            for t in range(NT):
                R = KEYS[t]
                bank_free(t)
                for k in range(KD):
                    ins = pe.matmul(PS[0:R, t % 4, :], hT[:, k, KEY0[t]:KEY0[t] + R], w_in_sb[2][:, k, :],
                                    start=k == 0, stop=k == KD - 1)
                ins.then_inc(proj_done, 1)
            pe.wait_ge(s_win[3], 16)
            pe.wait_ge(pads_set, 2 * GROUPS)
            for n in range(3 * GROUPS):
                i, g, c = G0 + n, n // 3, n % 3
                bank_free(i)
                for k in range(KD):
                    ins = pe.matmul(PS[:, i % 4, 0:WID[c]], w_in_sb[3][:, k, P * g:P * g + P],
                                    hT[:, k, OFF[c]:OFF[c] + WID[c]], start=k == 0, stop=k == KD - 1)
                ins.then_inc(proj_done, 1)
            for i in range(6 * HEADS):
                n, c = i // 3, i % 3
                if i in (0, 3):
                    pe.wait_ge(s_win[n % 2], 16)
                bank_free(Q0 + i)
                for k in range(KD):
                    ins = pe.matmul(PS[:, (Q0 + i) % 4, 0:WID[c]], w_in_sb[n % 2][:, k, P * (n // 2):P * (n // 2) + P],
                                    hT[:, k, OFF[c]:OFF[c] + WID[c]], start=k == 0, stop=k == KD - 1)
                ins.then_inc(proj_done, 1)
                if i:
                    stats(i - 1)
            stats(6 * HEADS - 1)

            def score(s, m):
                h, q = s // NT, s % NT
                R, b = ROWS[q], (s // NT) % 2
                if q == 0 and m == 0:
                    pe.wait_ge(s_stk[b], 16 * 6 * (h // 2 + 1))
                if s:
                    pe.wait_ge(exp_done, 2 * (s - 1) + m + 1)
                for c in range(3):
                    for n in range(2):
                        ins = pe.matmul(PS[0:R, 3 * m + c, 0:CHW], stk[b][:, m, n, P * q:P * q + R],
                                        stk[b][:, m, 2, CHS * c:CHS * c + CHW], start=n == 0, stop=n == 1)
                ins.then_inc(scores, 1)

            def transposes(s, b):
                R = ROWS[s % NT]
                if b == 0:
                    pe.wait_ge(diff_ready, s + 1)
                if s or b:
                    pe.wait_ge(tr_lo, 3 * s + b)
                for kt in range(3 * b, 3 * b + 3):
                    n = min(P, LS - KPOS[kt])
                    ins = pe.transpose(PS[0:n, 6, (kt % 3) * P:(kt % 3) * P + R],
                                       probs_a[s % 3][0:R, KPOS[kt]:KPOS[kt] + n], ident[0:R, 0:R])
                ins.then_inc(tr_done, 1)

            def bank7_free(use):
                if b7_use[use]:
                    pe.wait_ge(b7_taken, b7_use[use])

            def pv(j, b):
                h, N = j // 3, sum(ROWS[3 * (j % 3):3 * (j % 3) + 3])
                if b == 0:
                    bank7_free(("pv", j))
                pe.wait_ge(tr_lo, 3 * (3 * j + 2) + b + 1)
                for kt in range(3 * b, 3 * b + 3):
                    KR = KEYS[kt]
                    for n, (v, a) in enumerate(((v_hi, aT_hi), (v_hi, aT_lo), (v_lo, aT_hi))):
                        ins = pe.matmul(PS[:, 7, 0:N], v[0:KR, kt, DV * h:DV * h + DV], a[0:KR, kt, 0:N],
                                        start=kt == 0 and n == 0, stop=kt == NT - 1 and n == 2)
                ins.then_inc(pv_third, 1)

            def pool_product(n):
                g, c = n // 3, n % 3
                bank7_free(("pool", n))
                pe.wait_ge(pool_d, g + 1)
                pe.matmul(PS[:, 7, 0:WID[c]], poolw[:, g, :], pbuf[:, g, PADW + OFF[c]:PADW + OFF[c] + WID[c]],
                          start=True, stop=True).then_inc(pool_done, 1)

            pe.wait_ge(proj_taken, ITEMS)
            pe.wait_ge(qk_ready, 6 * HEADS)
            score(0, 0)
            score(0, 1)
            for s in range(TURNS):
                turn = 0 <= s - 2 < STEPS
                if turn:
                    transposes(s - 2, 0)
                if s % 3 == 2 and s >= 5:
                    pv((s - 5) // 3, 1)
                if s in pool_turns:
                    pool_product(pool_turns[s][0])
                if turn:
                    transposes(s - 2, 1)
                if s % 3 == 2 and s >= 5:
                    pv((s - 5) // 3, 2)
                if s % 3 == 1 and s >= 4:
                    pv((s - 4) // 3, 0)
                if s + 1 < STEPS:
                    score(s + 1, 0)
                if turn:
                    transposes(s - 2, 2)
                if s in pool_turns:
                    pool_product(pool_turns[s][1])
                if s + 1 < STEPS:
                    score(s + 1, 1)

            for j in range(12):
                W = WID[j % 3]
                pe.wait_ge(osq, j + 1)
                if j >= 2:
                    pe.wait_ge(ort, j - 1)
                pe.matmul(PS[:, j % 2, 0:W], dv_mean, sq[j % 2][:, 0:W], start=True, stop=True).then_inc(oms, 1)

            def router(t):
                R = ROWS[t]
                pe.wait_ge(hn_ready, t + 1)
                if t:
                    pe.wait_ge(hnT_ready, t)
                for k in range(KD):
                    ins = pe.transpose(PS[:, 4 + k // 4, (k % 4) * P:(k % 4) * P + R],
                                       hn[t % 2][0:R, k * P:(k + 1) * P], ident[0:R, 0:R])
                ins.then_inc(hn_tr, 1)
                pe.wait_ge(hnT_ready, t + 1)
                if t:
                    pe.wait_ge(lgT_ready, t)
                for k in range(KD):
                    ins = pe.matmul(PS[0:E, 6, 0:R], wr[:, k, :], hnT[t % 2][:, k, 0:R], start=k == 0, stop=k == KD - 1)
                ins.then_inc(rout_done, 1)

            for half in range(2):
                pe.wait_ge(s_wout[half], 16)
            pe.wait_ge(o_ready, 12)
            for t in range(NT):
                R = ROWS[t]
                if t >= 2:
                    pe.wait_ge(h2_ready, t - 1)
                for half in range(2):
                    for k in range(KD):
                        ins = pe.matmul(PS[0:R, 2 * (t % 2) + half, :], mixT[:, k, P * t:P * t + R],
                                        w_out_sb[half][:, k, :], start=k == 0, stop=k == KD - 1)
                ins.then_inc(wo_done, 1)
                if t:
                    router(t - 1)
            router(NT - 1)
            pe.wait_ge(lgT_ready, NT)
            pe.wait_ge(pad_set, 1)
            for t in range(NT):
                ins = pe.transpose(PS[:, 7, t * E:(t + 1) * E], lgT[:, P * t:P * t + P], ident[0:E, 0:E])
            ins.then_inc(lg_tr, 1)
            pe.wait_ge(h2_ready, NT)
            pe.wait_ge(aff_ready, 1)
            for t in range(NT):
                ins = pe.transpose(PS[0:E, t // 4, (t % 4) * P:(t % 4) * P + P], lg[:, t, :], ident)
            ins.then_inc(aff_tr, 1)
            pe.wait_ge(ids_ready, 1)
            for n, (src, at, rows) in enumerate(((mif, 0, P), (mv, 0, P), (mif, P, CAPX), (mv, P, CAPX))):
                ins = pe.transpose(PS[0:rows, 4, n * E:(n + 1) * E], src[:, at:at + rows], ident[0:E, 0:E])
            ins.then_inc(ids_tr, 1)

            def x_transposes(e, b, first=False):
                if b == 0:
                    pe.wait_ge(s_gath, 16 * e + 16)
                    pe.wait_ge(s_gathx, 16 * e + 16)
                    if not first:
                        pe.wait_ge(y_taken, 2 * e - 2)
                if b == 2:
                    pe.wait_ge(xl_ready, 6 * e + 2)
                for k in range(3 * b, min(3 * b + 3, KD)):
                    to = (k % 3) * CAP
                    pe.transpose(PS[:, 6 + b % 2, to:to + P], xg[:, k * P:(k + 1) * P], ident)
                    ins = pe.transpose(PS[:, 6 + b % 2, to + P:to + CAP], xgx[:, k * P:(k + 1) * P],
                                       ident[0:CAPX, 0:CAPX])
                ins.then_inc(xg_tr, 1)

            def gate_up(e, n, early=False):
                c, f = n // 2, n % 2
                if n == 0:
                    pe.wait_ge(xl_ready, 6 * e + 6)
                if f == 0:
                    pe.wait_ge(lo_ready, TILES * e + 2 * c + 2)
                if not early:
                    pe.wait_ge(gu_ready, 2 * CG * e + n - 1)
                for h in range(2):
                    bank = 2 * f + h
                    hi, lo = (w[c % CUT][:, 2048 * h:2048 * h + 2048].rearrange("p (k n) -> p k n", k=KD)
                              for w in (w_hi, w_lo))
                    for k in range(KD):
                        pe.matmul(PS[:, bank, 0:2 * CAP], hi[:, k, f * P:(f + 1) * P], x_hl[:, k, :],
                                  start=k == 0, stop=False, skip_group_check=True)
                    for k in range(KD):
                        ins = pe.matmul(PS[:, bank, 0:CAP], lo[:, k, f * P:(f + 1) * P], x_bf[:, k, :],
                                        start=False, stop=k == KD - 1, skip_group_check=True)
                ins.then_inc(tile_done, 1)

            def down(e, t, ks, early=False):
                c, f0 = CG + t // 2, (t % 2) * P
                if ks[0] == 0:
                    if t % 2 == 0:
                        pe.wait_ge(lo_ready, TILES * e + 2 * c + 2)
                    if t == 0:
                        pe.wait_ge(a_pool, 3 * (CG - 1) * e + 3 * (CG - 1))
                    if not early:
                        pe.wait_ge(y_ready, KD * e + t - 1)
                elif t == 0:
                    pe.wait_ge(a_dve, e + 1)
                hi, lo = (w[c % CUT][:, :].rearrange("p (k n) -> p k n", k=FT) for w in (w_hi, w_lo))
                for k in ks:
                    pe.matmul(PS[:, 4 + t % 2, 0:2 * CAP], hi[:, k, f0:f0 + P], a_hl[:, k, :],
                              start=k == 0, stop=False, skip_group_check=True)
                for k in ks:
                    ins = pe.matmul(PS[:, 4 + t % 2, 0:CAP], lo[:, k, f0:f0 + P], a_bf[:, k, :],
                                    start=False, stop=k == FT - 1, skip_group_check=True)
                if ks[-1] == FT - 1:
                    ins.then_inc(tile_done, 1)

            def y_transposes(e, rest, last=False):
                if rest:
                    pe.wait_ge(y_taken, 2 * e + 1)
                else:
                    pe.wait_ge(y_ready, KD * e + KD)
                    if not last:
                        pe.wait_ge(xl_ready, 6 * e + 12)
                for d in range(KD):
                    src = yT[:, d, P:CAP] if rest else yT[:, d, 0:P]
                    ins = pe.transpose(PS[0:CAPX if rest else P, 6 + d // 4, (d % 4) * P:(d % 4) * P + P], src, ident)
                ins.then_inc(y_tr, 1)

            def expert(e, first=False, last=False):
                for n in range(2 * CG):
                    gate_up(e, n, early=first and n < 2)
                    if not first and n in (3, 7):
                        y_transposes(e - 1, n == 7)
                for ks in (range(FT - 2), range(FT - 2, FT)):
                    for t in range(2):
                        down(e, t, ks, early=first)
                for t in range(1, KD):
                    if t > 1:
                        down(e, t, range(FT))
                    if not last and t == 1:
                        x_transposes(e + 1, 0, first)
                        x_transposes(e + 1, 1)
                    if not last and t == 3:
                        x_transposes(e + 1, 2)

            pe.wait_ge(route_ready, 4)
            for b in range(3):
                x_transposes(0, b, True)
            expert(0, first=True)
            with pe.Fori(1, E - 1) as e:
                expert(e)
            expert(E - 1, last=True)
            y_transposes(E - 1, 0, last=True)
            y_transposes(E - 1, 1)


_INS = ["x", "meta_tokens", "ln1_g", "w_in", "q_norm_g", "k_norm_g", "lambda_q1", "lambda_k1", "lambda_q2",
        "lambda_k2", "subln_g", "pool_w", "pool_scale", "w_out", "ln2_g", "w_router", "w_gate", "w_up", "w_down"]


def kernel(**inputs):
    import numpy as _np
    import concourse.bacc as _bacc
    from concourse import mybir as _mybir
    from concourse.bass_utils import run_bass_kernel_spmd as _run

    nc = _bacc.Bacc("TRN2", target_bir_lowering=False, num_devices=1)
    arrays = {f"in_{n}": _np.ascontiguousarray(inputs[n]) for n in _INS}
    arrays["in_consts"] = constants()
    args = [nc.dram_tensor(n, a.shape, _mybir.dt.from_np(a.dtype), kind="ExternalInput").ap()
            for n, a in arrays.items()]
    out = nc.dram_tensor("out_0", (1, SEQ, D), _mybir.dt.float32, kind="ExternalOutput").ap()
    block_kernel(nc, *args, out)
    r = _run(nc, [arrays], core_ids=[0])
    return r.results[0]["out_0"]
```

```python
from contextlib import ExitStack

import numpy as np
import concourse.bass as bass
from concourse import mybir

F32 = mybir.dt.float32
F32R = mybir.dt.float32r
BF16 = mybir.dt.bfloat16
U32 = mybir.dt.uint32
I32 = mybir.dt.int32
ACT = mybir.ActivationFunctionType
ALU = mybir.AluOpType
AX = mybir.AxisListType

P = 128
D = 1024
SEQ = 1024
META = 16
L = SEQ + META
KD = D // P
NT = -(-L // P)
HEADS = 4
DH = 64
DV = 2 * DH
GROUPS = 4
WINDOWS = (2, 4, 8, 16)
E = 16
FF = 2048
CAP = 2 * L // E
CAPX = CAP - P
EPS = 1e-6
LAM_INIT = 0.2
SCALE = DH ** -0.5
ROWS = [min(P, L - P * t) for t in range(NT)]
CHUNK3 = [(3 * P * c, sum(ROWS[3 * c:3 * c + 3])) for c in range(NT // 3)]
OFF = (0, 348, 694)
WID = (348, 346, 346)
CHS, CHW = 346, 348
LS = 3 * CHW
KEY0 = [OFF[c] + P * j for c in range(3) for j in range(3)]
KEYS = [(P, P, WID[c] - 2 * P)[j] for c in range(3) for j in range(3)]
KPOS = [CHW * c + OFF[c] - CHS * c + P * j for c in range(3) for j in range(3)]
PADW = 8
LP = L + 2 * PADW
ROUNDS = -(-CAP // 8)
SLOT = 8 * 512
FT = FF // P
RAW, CUT = 4, 3
CG, CD = FF // 256, D // 256
CH = CG + CD
TILES = 2 * CH
SMALL = 204160
G0 = NT
Q0 = G0 + 3 * GROUPS
ITEMS = Q0 + 6 * HEADS
BLOCKS = (ITEMS - G0) // 3
GROUP = range(GROUPS - 1, -1, -1)
W_COL = [3 * HEADS * DV + P * g for g in GROUP] + [HEADS * DV + P * h for h in range(HEADS)] + [
    P * h for h in range(HEADS)]


def qk_part(i):
    is_k = i < 3 * HEADS
    return 2 * ((i // 3) % HEADS) + is_k, int(is_k)


C_ID, C_BLK, C_ONE = 0, P, 2 * P
C_EDGE = 3 * P
C_COS = C_EDGE + GROUPS * 16
C_SIN = C_COS + L
C_END = C_SIN + L


def constants():
    c = np.zeros((P, C_END), np.float32)
    p = np.arange(P)
    c[p, C_ID + p] = 1.0
    c[:, C_BLK:C_BLK + P] = (p[:, None] // DH == p[None, :] // DH) / DH
    c[:, C_ONE:C_ONE + P] = 1.0 / DV
    t = np.arange(L)
    for g, w in enumerate(WINDOWS):
        count = np.minimum(t + w // 2, L) - np.maximum(t - w // 2, 0)
        edge = (w / count).astype(np.float32)
        c[:, C_EDGE + 16 * g:C_EDGE + 16 * g + 8] = edge[:8]
        c[:, C_EDGE + 16 * g + 8:C_EDGE + 16 * g + 16] = edge[-8:]
    half = DH // 2
    freq = np.float32(10000.0) ** (-np.arange(half, dtype=np.float32) / np.float32(half))
    ang = t.astype(np.float32)[None, :] * freq[p % half][:, None]
    c[:, C_COS:C_COS + L] = np.cos(ang)
    c[:, C_SIN:C_SIN + L] = np.sin(ang) * np.where(p % DH < half, -1.0, 1.0)[:, None]
    return c


def block_kernel(nc, x, meta_tokens, ln1_g, w_in, q_norm_g, k_norm_g, lambda_q1, lambda_k1,
                 lambda_q2, lambda_k2, subln_g, pool_w, pool_scale, w_out, ln2_g, w_router,
                 w_gate, w_up, w_down, consts, out):
    sums = nc.dram_tensor("sums", [L, D], F32, kind="Internal").ap()
    table = nc.dram_tensor("table", [L, D], F32, kind="Internal").ap()
    parts = nc.dram_tensor("parts", [2 * HEADS, 2, P, L], F32, kind="Internal").ap()

    ctx = ExitStack()
    with ctx:
        def sem(name):
            return ctx.enter_context(nc.semaphore(name))

        base = -(-nc.sbuf_base // 64) * 64

        def at(name, offset, shape, dt=F32):
            return nc.alloc_sbuf_tensor_at(name, [P] + shape, dt, offset=base + offset)

        w_raw = [at(f"w_raw{i}", i * 4 * D, [KD, P]) for i in (0, 1)]
        w_in_hi = [at(f"w_in_hi{i}", 8192 + i * 8192, [KD, P], F32R) for i in range(4)]
        w_in_lo = [at(f"w_in_lo{i}", 12288 + i * 8192, [KD, P], F32R) for i in range(4)]
        w_v_hi = at("w_v_hi", 8192, [KD, HEADS * DV], F32R)
        w_v_lo = at("w_v_lo", 24576, [KD, HEADS * DV], F32R)
        w_v = at("w_v", 170112, [KD, HEADS * DV])
        hT_hi = at("hT_hi", 99968, [KD, L], F32R)
        hT_lo6 = at("hT_lo6", 40960, [6, L], F32R)
        hT_lo2 = at("hT_lo2", 91648, [2, L], F32R)
        x_r = at("x_r", 133248, [NT * D])
        g1 = at("g1", 66304, [D])
        px_r = at("px_r", 66304, [(GROUPS + 2) * LP])
        mix_r = at("mix_r", 99968, [KD * L])
        v_hi = at("v_hi", 133248, [NT, HEADS * DV], F32R)
        v_lo = at("v_lo", 151680, [NT, HEADS * DV], F32R)
        trig_r = at("trig_r", 170112, [2 * L])
        tmp_r = at("tmp_r", 178432, [9 * CHW])
        stage = [at(f"stage{i}", 190976 + i * 2784, [2, CHW], F32R) for i in (0, 1)]
        stk = [at(f"stk{i}", off, [2, 3, L], F32R) for i, off in ((0, 0), (1, 41344))]
        probs_a = [at(f"probs_a{i}", 83200 + i * 4192, [LS]) for i in range(3)]
        probs_b = [at(f"probs_b{i}", off, [LS]) for i, off in ((0, 83200 + 3 * 4192), (1, 197760))]
        aT_hi = at("aT_hi", 170112, [NT, 3 * P], F32R)
        aT_lo = at("aT_lo", 183936, [NT, 3 * P], F32R)
        w_out_r = [at(f"w_out_r{i}", off, [SLOT]) for i, off in ((0, 24960), (1, 66304))]
        out_r = at("out_r", 133248, [9 * D])
        out_half = at("out_half", 201984, [512])
        hp_r = [at(f"hp_r{i}", off, [D]) for i, off in ((0, 197760), (1, 170112))]
        o_sq = [at(f"o_sq{i}", 41344 + 1536 * i, [3 * P]) for i in (0, 1)]
        o_rt = [at(f"o_rt{i}", 44416 + 1536 * i, [3 * P]) for i in (0, 1)]

        def cut(region, at, n, **how):
            part = region[:, at:at + n]
            return part.rearrange("p (a b) -> p a b", **how) if how else part

        def xt(t):
            return x_r[:, t * D:(t + 1) * D]

        def hT_lo(k):
            return hT_lo6[:, k, :] if k < 6 else hT_lo2[:, k - 6, :]

        cosT, sinT = trig_r[:, 0:L], trig_r[:, L:2 * L]
        sq = [tmp_r[:, i * CHW:(i + 1) * CHW] for i in (0, 1)]
        qg = [tmp_r[:, i * CHW:(i + 1) * CHW] for i in (2, 3, 4)]
        rt = [tmp_r[:, i * CHW:(i + 1) * CHW] for i in (5, 6)]
        ta = [tmp_r[:, 7 * CHW:8 * CHW], at("ta1", 200576, [CHW])[:, :]]
        tb = tmp_r[:, 8 * CHW:9 * CHW]
        whole = at("whole", 201984, [CHW])
        qs_r = [at(f"qs{i}", off, [CHW]) for i, off in ((0, 197760), (1, 199168))]
        pbuf = cut(px_r, 0, GROUPS * LP, a=GROUPS)
        lev = [px_r[:, (GROUPS + i) * LP:(GROUPS + i + 1) * LP] for i in (0, 1)]
        mixT = mix_r[:, :].rearrange("p (k t) -> p k t", k=KD)
        w_out_sb = [w[:, :].rearrange("p (k n) -> p k n", k=KD) for w in w_out_r]
        hx = [cut(out_r, i * D, D) for i in (0, 1)]
        h2 = [cut(out_r, (2 + i) * D, D) for i in (0, 1)]
        hn = [cut(out_r, (4 + i) * D, D) for i in (0, 1)]
        hnT = [cut(out_r, (6 + i) * D, D, a=KD) for i in (0, 1)]
        g2 = out_r[:, 8 * D:9 * D]
        affT = trig_r[0:E, D:D + L]
        lgT = tmp_r[0:E, 0:NT * P]
        lg = cut(tmp_r, NT * P, NT * E, a=NT)
        mv, mif, mi = (tmp_r[0:E, at:at + 8 * ROUNDS] for at in (1500, 1700, 1900))
        mi = mi.bitcast(U32)
        raw = [at(f"raw{i}", i * 4 * SLOT, [SLOT]) for i in range(RAW)]
        w_hi = [at(f"w_hi{i}", (RAW + i) * 4 * SLOT, [SLOT], F32R) for i in range(CUT)]
        w_lo = [at(f"w_lo{i}", (RAW + CUT) * 4 * SLOT + i * 2 * SLOT, [SLOT], BF16) for i in range(CUT)]
        place = [(RAW + CUT) * 4 * SLOT + CUT * 2 * SLOT]

        def next_at(name, shape, dt=F32):
            here = place[0]
            place[0] += -(-int(np.prod(shape)) * (2 if dt == BF16 else 4) // 32) * 32
            return at(name, here, shape, dt)

        x_hl = next_at("x_hl", [KD, 2 * CAP], F32R)
        x_bf = next_at("x_bf", [KD, CAP], BF16)
        a_hl = next_at("a_hl", [FT, 2 * CAP], F32R)
        a_bf = next_at("a_bf", [FT, CAP], BF16)
        low_sum = [next_at(f"low_sum{i}", [2, CAP]) for i in (0, 1)]
        gu = [next_at(f"gu{i}", [2, 2, CAP]) for i in (0, 1)]
        silu = [next_at(f"silu{i}", [2, CAP]) for i in (0, 1)]
        act_f = [next_at(f"act_f{i}", [2, CAP]) for i in (0, 1)]
        ypart = [next_at(f"ypart{i}", [CAP]) for i in (0, 1)]
        yT = next_at("yT", [KD, CAP])
        xg_r, xgx_r, y_r, yx_r = (next_at(n, [D]) for n in ("xg", "xgx", "y", "yx"))
        xg, xgx, y_sb, yx_sb = xg_r[:, :], xgx_r[0:CAPX, :], y_r[:, :], yx_r[0:CAPX, :]
        assert place[0] <= SMALL
        nc_rest = [SMALL]

        def sb(name, shape, dt=F32):
            here = nc_rest[0]
            nc_rest[0] += -(-int(np.prod(shape[1:])) * 4 // 32) * 32
            return nc.alloc_sbuf_tensor_at(name, shape, dt, offset=base + here)

        cst = sb("cst", [P, C_COS])
        ident = cst[:, C_ID:C_ID + P]
        blk_mean = cst[:, C_BLK:C_BLK + P]
        dv_mean = cst[:, C_ONE:C_ONE + P]
        edge = cst[:, C_EDGE:C_COS].rearrange("p (g c) -> p g c", g=GROUPS)
        poolw = sb("poolw", [P, GROUPS, P])
        wr = sb("wr", [P, KD, E])
        gq = sb("gq", [P, 2])
        sg = sb("sg", [P, 2])
        psc = sb("psc", [P, GROUPS])
        lamv = sb("lamv", [P, 4, DH])
        lamj = sb("lamj", [P, DH])
        lam = sb("lam", [P, 5])
        eps = sb("eps", [P, 1])
        st = sb("st", [P, 4, NT])
        st2 = sb("st2", [P, 4, NT])
        mx = sb("mx", [P, 2, 2])
        nb = sb("nb", [P, 2, 2])
        zs = sb("zs", [P, 2, 4, 2])
        rl = sb("rl", [P, 2])
        sm = sb("sm", [P, 3, NT])
        idx = sb("idx", [P, 2, E], I32)
        gat = sb("gat", [P, 2, E])
        gidx = sb("gidx", [P, 2], I32)
        sidx = sb("sidx", [P, 2], I32)
        gcur = sb("gcur", [P, 2])

        PS = ctx.enter_context(nc.psum_tensor("PS", [P, 8, 512], F32))

        def two_banks(b, rows=P):
            return PS[0:rows, b:b + 2, :].rearrange("p b n -> p (b n)")

        s_cst, s_trig, s_par, s_lam, s_g2 = (sem(n) for n in ("s_cst", "s_trig", "s_par", "s_lam", "s_g2"))
        s_x = [sem(f"s_x{t}") for t in range(NT)]
        s_g1, s_wv, s_win = sem("s_g1"), sem("s_wv"), [sem("s_win0"), sem("s_win1")]
        wv_lo_pool = sem("wv_lo_pool")
        wv_hi, wv_lo, win_hi, win_lo, hT_hi_ready = (
            sem(n) for n in ("wv_hi", "wv_lo", "win_hi", "win_lo", "hT_hi_ready"))
        s_small = sem("s_small")
        s_wout = [sem("s_wout0"), sem("s_wout1")]
        s_stage = [sem("s_stage0"), sem("s_stage1")]
        s_stk = [sem("s_stk0"), sem("s_stk1")]
        v_lo_ready = sem("v_lo_ready")
        eps_set, pad_set = sem("eps_set"), sem("pad_set")
        ssq, var_ready, std_ready, xs_ready, xtr, hT_ready = (
            sem(n) for n in ("ssq", "var_ready", "std_ready", "xs_ready", "xtr", "hT_ready"))
        proj_done, proj_taken, ms_done, sw_done, rt_ready, qk_ready, sq_ready = (
            sem(n) for n in ("proj_done", "proj_taken", "ms_done", "sw_done", "rt_ready", "qk_ready",
                             "sq_ready"))
        dve_chain, pool_chain, pads_set, win_ready, pool_d = (
            sem(n) for n in ("dve_chain", "pool_chain", "pads_set", "win_ready", "pool_d"))
        lam_dot, lam_exp = sem("lam_dot"), sem("lam_exp")
        scores, nb_ready, exp_done, diff_ready, tr_done, tr_hi, tr_lo = (
            sem(n) for n in ("scores", "nb_ready", "exp_done", "diff_ready", "tr_done", "tr_hi", "tr_lo"))
        cos_ready, hi_staged = sem("cos_ready"), sem("hi_staged")
        rl_ready, map1_ready = sem("rl_ready"), sem("map1_ready")
        pv_third, pool_done, pool_taken, half_done, b7_taken = (
            sem(n) for n in ("pv_third", "pool_done", "pool_taken", "half_done", "b7_taken"))
        osq, oms, ort, o_ready = sem("osq"), sem("oms"), sem("ort"), sem("o_ready")
        s_half, h_ready = sem("s_half"), sem("h_ready")
        s_hx, s_hp = [sem("s_hx0"), sem("s_hx1")], [sem("s_hp0"), sem("s_hp1")]
        wo_done, h2_ready, ssq2, var2, std2, hn_ready, hn_tr, hnT_ready, rout_done, lgT_ready = (
            sem(n) for n in ("wo_done", "h2_ready", "ssq2", "var2", "std2", "hn_ready", "hn_tr",
                             "hnT_ready", "rout_done", "lgT_ready"))
        s_sums, s_table = [sem("s_sums0"), sem("s_sums1")], [sem("s_table0"), sem("s_table1")]
        lg_tr, lg_sub, lg_exp, aff_ready, aff_tr, ids_ready, ids_tr, route_ready = (
            sem(n) for n in ("lg_tr", "lg_sub", "lg_exp", "aff_ready", "aff_tr", "ids_ready",
                             "ids_tr", "route_ready"))
        s_w = [[sem(f"s_w{i}{h}") for h in (0, 1)] for i in range(RAW)]
        gidx_set, s_gath, s_gathx, xg_tr, xh_ready, xl_ready = (
            sem(n) for n in ("gidx_set", "s_gath", "s_gathx", "xg_tr", "xh_ready", "xl_ready"))
        hi_ready, lo_ready, tile_done, part_ready, gu_ready, silu_ready, ahi_ready = (
            sem(n) for n in ("hi_ready", "lo_ready", "tile_done", "part_ready", "gu_ready", "silu_ready",
                             "ahi_ready"))
        a_pool, a_mul, a_dve, ypart_ready, y_ready, y_tr, y_taken, gcur_set = (
            sem(n) for n in ("a_pool", "a_mul", "a_dve", "ypart_ready", "y_ready", "y_tr", "y_taken", "gcur_set"))
        sidx_set, s_scat, s_scatx, s_out = (sem(n) for n in ("sidx_set", "s_scat", "s_scatx", "s_out"))

        STEPS = HEADS * NT
        TURNS = STEPS + 3
        TRIOS = STEPS // 3
        half_turns = {s: n for n, s in enumerate([s for s in range(3, TURNS) if s % 3 < 2][:2 * NT])}
        b7_use = {}
        for s in range(TURNS):
            if s in half_turns:
                b7_use["half", half_turns[s]] = len(b7_use)
            if s % 3 == 1 and s >= 4:
                b7_use["pv", (s - 4) // 3] = len(b7_use)
        assert len(b7_use) == TRIOS + 2 * NT

        early_subln = {STEPS: (0, 1), STEPS + 1: (2, 3), STEPS + 2: (4, 5)}
        LATE = 7

        def o_bank(j):
            return j % 6 if j < LATE else 7

        block = ctx.enter_context(nc.Block())

        @block.sync
        def _(sp):
            sp.dma_start(cst[:], consts[:, 0:C_COS]).then_inc(s_cst, 16)
            for t in range(NT):
                if t == 1:
                    sp.dma_start(g1[:], ln1_g[0, :].partition_broadcast(P)).then_inc(s_g1, 16)
                if t == 0:
                    sp.dma_start(xt(0)[0:META, :], meta_tokens).then_inc(s_x[0], 16)
                    sp.dma_start(xt(0)[META:P, :], x[0, 0:P - META, :]).then_inc(s_x[0], 16)
                else:
                    a = P * t - META
                    sp.dma_start(xt(t)[0:ROWS[t], :], x[0, a:a + ROWS[t], :]).then_inc(s_x[t], 16)
            with nc.allow_non_contiguous_dma(reason="small parameters"):
                for m in range(2):
                    at = slice(DH * m, DH * m + DH)
                    sp.dma_start(gq[at, 0:1], q_norm_g.rearrange("o p -> p o")).then_inc(s_par, 16)
                    sp.dma_start(gq[at, 1:2], k_norm_g.rearrange("o p -> p o")).then_inc(s_par, 16)
                sp.dma_start(sg[:, 0:1], subln_g.rearrange("o p -> p o")).then_inc(s_par, 16)
                sp.dma_start(psc[:], pool_scale.rearrange("o (g p) -> p (o g)", p=P)).then_inc(s_par, 16)
            w_cols = w_in[0].rearrange("(k p) n -> p k n", p=P)
            sp.dma_start(w_v[:], w_cols[:, :, 2 * HEADS * DV:3 * HEADS * DV]).then_inc(s_wv, 16)

            def load_block(b):
                sp.dma_start(w_raw[b % 2][:], w_cols[:, :, W_COL[b]:W_COL[b] + P]).then_inc(s_win[b % 2], 16)

            load_block(0)
            load_block(1)
            with nc.allow_non_contiguous_dma(reason="small parameters"):
                for n, v in enumerate((lambda_q1, lambda_k1, lambda_q2, lambda_k2)):
                    sp.dma_start(lamv[:, n, :], v[0, :].partition_broadcast(P)).then_inc(s_lam, 16)
                sp.dma_start(poolw[:], pool_w[0].rearrange("g c d -> c g d")).then_inc(s_small, 16)
                sp.dma_start(wr[:], w_router[0].rearrange("(k p) e -> p k e", p=P)).then_inc(s_small, 16)
            sp.wait_ge(wv_lo_pool, 2)
            sp.wait_ge(wv_lo, 2)
            sp.dma_start(trig_r[:], consts[:, C_COS:C_END]).then_inc(s_trig, 16)

            def load_w_out(half):
                sp.dma_start(w_out_sb[half], w_out[0].rearrange("(k p) n -> p k n", p=P)[:, :, 512 * half:512 * half + 512]
                             ).then_inc(s_wout[half], 16)

            for b in range(2, GROUPS + 3):
                sp.wait_ge(win_lo, b - 1)
                load_block(b)
            for i in range(6 * HEADS):
                n, c = qk_part(i)[0], i % 3
                b = GROUPS + 3 + i // 3
                if i % 3 == 0 and b < BLOCKS:
                    sp.wait_ge(win_lo, b - 1)
                    load_block(b)
                sp.wait_ge(qk_ready, i + 1)
                sp.dma_start(parts[n, :, :, OFF[c]:OFF[c] + WID[c]].rearrange("a p t -> p a t"),
                             stage[i % 2][:, :, 0:WID[c]].bitcast(F32)).then_inc(s_stage[i % 2], 16)
            sp.wait_ge(proj_done, ITEMS)
            sp.wait_ge(s_stk[0], 16 * 6)
            load_w_out(0)
            sp.wait_ge(pool_done, 3 * GROUPS)
            load_w_out(1)
            for n in range(2 * NT):
                t, half = n // 2, n % 2
                sp.wait_ge(b7_taken, b7_use["half", n] + 1)
                sp.dma_start(sums[P * t:P * t + ROWS[t], 512 * half:512 * half + 512], out_half[0:ROWS[t], :]
                             ).then_inc(s_half, 16)

            def load(e, c):
                one, s = bass.ds(e, 1), c % RAW
                for h in range(2):
                    if c < CG:
                        w = (w_gate, w_up)[h][0].rearrange("e (k p) f -> e p k f", p=P)
                        src = w[one, :, :, 256 * c:256 * c + 256]
                    else:
                        w = w_down[0].rearrange("e (k p) n -> e p k n", p=P)
                        src = w[one, :, 8 * h:8 * h + 8, 256 * (c - CG):256 * (c - CG) + 256]
                    sp.dma_start(raw[s][:, 2048 * h:2048 * h + 2048].rearrange("p (k n) -> p k n", k=8),
                                 src.rearrange("e p k n -> p (e k) n")).then_inc(s_w[s][h], 16)

            def load_expert(e, cs=range(CH)):
                for c in cs:
                    sp.wait_ge(lo_ready, TILES * e + 2 * (c - RAW) + 2)
                    load(e, c)

            sp.wait_ge(scores, 6 * NT)
            load(0, 0)
            sp.wait_ge(scores, 8 * NT)
            load(0, 3)
            sp.wait_ge(pv_third, 3 * TRIOS)
            sp.dma_start(g2, ln2_g[0, :].partition_broadcast(P)).then_inc(s_g2, 16)

            def load_hx(t):
                b = t % 2
                if t >= 2:
                    sp.wait_ge(h2_ready, t - 1)
                if t == 0:
                    sp.dma_start(hx[0][0:META, :], meta_tokens).then_inc(s_hx[0], 16)
                    sp.dma_start(hx[0][META:P, :], x[0, 0:P - META, :]).then_inc(s_hx[0], 16)
                else:
                    a = P * t - META
                    sp.dma_start(hx[b][0:ROWS[t], :], x[0, a:a + ROWS[t], :]).then_inc(s_hx[b], 16)

            def load_hp(t):
                if t >= 2:
                    sp.wait_ge(h_ready, t - 1)
                sp.dma_start(hp_r[t % 2][0:ROWS[t], :], sums[P * t:P * t + ROWS[t], :]).then_inc(s_hp[t % 2], 16)

            sp.wait_ge(s_half, 16 * 2 * NT)
            for t in (0, 1):
                load_hx(t)
                load_hp(t)
            for t in range(NT):
                R = ROWS[t]
                if t + 2 < NT:
                    load_hx(t + 2)
                    load_hp(t + 2)
                sp.wait_ge(h2_ready, t + 1)
                sp.dma_start(sums[P * t:P * t + R, :], h2[t % 2][0:R, :]).then_inc(s_sums[t % 2], 16)
                sp.wait_ge(hn_ready, t + 1)
                sp.dma_start(table[P * t:P * t + R, :], hn[t % 2][0:R, :]).then_inc(s_table[t % 2], 16)
            sp.wait_ge(wo_done, NT)
            load(0, 1)
            load(0, 2)
            load_expert(0, range(RAW, CH))
            with sp.Fori(1, E) as e:
                load_expert(e)
            sp.wait_ge(s_scat, 16 * E)
            sp.wait_ge(s_scatx, 16 * E)
            sp.dma_start(out[0], sums[META:L, :]).then_inc(s_out, 16)
            sp.wait_ge(s_out, 16)

        @block.gpsimd
        def _(pool):
            steps = [0]

            def link(ins):
                steps[0] += 1
                ins.then_inc(pool_chain, 1)
                pool.wait_ge(pool_chain, steps[0])

            pool.memset(eps[:], EPS).then_inc(eps_set, 1)
            for n in range(2):
                pool.wait_ge(wv_hi, n + 1)
                pool.tensor_tensor(w_v_lo[:, 2 * n:2 * n + 2, :], w_v[:, 2 * n:2 * n + 2, :],
                                   w_v_hi[:, 2 * n:2 * n + 2, :].bitcast(F32), ALU.subtract).then_inc(wv_lo_pool, 1)
            pool.wait_ge(xs_ready, NT)
            for g in range(GROUPS):
                pool.memset(pbuf[:, g, 0:PADW], 0.0).then_inc(pads_set, 1)
                pool.memset(pbuf[:, g, PADW + L:LP], 0.0).then_inc(pads_set, 1)
            pool.wait_ge(pads_set, 2 * GROUPS)
            def windows(j):
                g = GROUP[j]
                pool.wait_ge(proj_taken, G0 + 3 * (j + 1))
                if j:
                    pool.wait_ge(pool_d, j)
                src = pbuf[:, g, :]
                for lv in range(g + 1):
                    reach = 2 ** g - 2 ** lv if lv else 2 ** g - 1
                    lo, hi = PADW - reach, PADW + L + reach
                    a, b = (1, 0) if lv == 0 else (2 ** (lv - 1), 2 ** (lv - 1))
                    dst = lev[lv % 2]
                    ins = pool.tensor_tensor(dst[:, lo:hi], src[:, lo - a:hi - a], src[:, lo + b:hi + b], ALU.add)
                    if lv < g:
                        link(ins)
                    src = dst
                ins.then_inc(win_ready, 1)

            def load_q(h, m, half):
                pool.dma_start(stk[h % 2][DH * half:DH * half + DH, m, 0:2, :],
                               parts[2 * h, :, DH * m:DH * m + DH, :].rearrange("a p t -> p a t")).then_inc(s_stk[h % 2], 16)

            def load_k(h, half):
                pool.dma_start(stk[h % 2][DH * half:DH * half + DH, :, 2, :],
                               parts[2 * h + 1, half].rearrange("(m p) t -> p m t", m=2)).then_inc(s_stk[h % 2], 16)

            def wait_parts(h):
                for i in (0, 1):
                    pool.wait_ge(s_stage[i], 16 * ((3 * HEADS + 3 * (h + 1) + 1 - i) // 2))

            def load_heads(h):
                wait_parts(h)
                for half in range(2):
                    load_q(h, 0, half)
                    load_q(h, 1, half)
                    load_k(h, half)

            def cosines(i):
                W, at = WID[i % 3], slice(OFF[i % 3], OFF[i % 3] + WID[i % 3])
                pool.wait_ge(proj_taken, Q0 + i + 1)
                if i >= 2:
                    pool.wait_ge(qk_ready, i - 1)
                pool.tensor_tensor(ta[i % 2][:, 0:W], qg[i % 3][:, 0:W], cosT[:, at], ALU.mult).then_inc(cos_ready, 1)

            for j in range(GROUPS):
                windows(j)
            pool.wait_ge(s_trig, 16)
            cosines(0)
            for i in range(6 * HEADS):
                W = WID[i % 3]
                if i + 1 < 6 * HEADS:
                    cosines(i + 1)
                pool.wait_ge(hi_staged, i + 1)
                if i:
                    pool.wait_ge(qk_ready, i)
                link(pool.tensor_tensor(whole[:, 0:W], ta[i % 2][:, 0:W], rt[i % 2][:, 0:W], ALU.mult))
                pool.tensor_tensor(stage[i % 2][:, 1, 0:W], whole[:, 0:W], stage[i % 2][:, 0, 0:W].bitcast(F32),
                                   ALU.subtract).then_inc(qk_ready, 1)
                if i == 16:
                    wait_parts(0)
                    pool.wait_ge(win_lo, BLOCKS)
                    pool.wait_ge(proj_done, ITEMS - 9)
                if i == 18:
                    pool.wait_ge(proj_done, ITEMS - 6)
                if 16 <= i < 20:
                    load_q(0, (i - 16) // 2, i % 2)
                if i == 20:
                    pool.wait_ge(proj_done, ITEMS - 3)
                    load_k(0, 0)
                    load_k(0, 1)
            pool.wait_ge(proj_done, ITEMS)
            load_heads(1)
            pool.wait_ge(scores, 2 * NT)
            load_heads(2)
            pool.wait_ge(scores, 4 * NT)
            load_heads(3)

            def gather(e):
                pool.tensor_copy(gidx[:, 0:1], idx[:, 0, bass.ds(e, 1)]).then_inc(gidx_set, 1)
                pool.tensor_copy(gidx[0:CAPX, 1:2], idx[0:CAPX, 1, bass.ds(e, 1)]).then_inc(gidx_set, 1)
                pool.wait_ge(gidx_set, 2)
                pool.indirect_dma_start(xg, None, table, bass.IndirectOffsetOnAxis(ap=gidx[:, 0:1], axis=0)
                                        ).then_inc(s_gath, 16)
                pool.indirect_dma_start(xgx, None, table, bass.IndirectOffsetOnAxis(ap=gidx[0:CAPX, 1:2], axis=0)
                                        ).then_inc(s_gathx, 16)
                pool.sem_clear(gidx_set)

            def scatter(e, first):
                if not first:
                    pool.wait_ge(s_scat, 16 * e)
                    pool.wait_ge(s_scatx, 16 * e)
                pool.wait_ge(y_taken, 2 * e + 2)
                pool.tensor_copy(sidx[:, 0:1], idx[:, 0, bass.ds(e, 1)]).then_inc(sidx_set, 1)
                pool.tensor_copy(sidx[0:CAPX, 1:2], idx[0:CAPX, 1, bass.ds(e, 1)]).then_inc(sidx_set, 1)
                pool.wait_ge(sidx_set, 2)
                pool.indirect_dma_start(sums, bass.IndirectOffsetOnAxis(ap=sidx[:, 0:1], axis=0), y_sb, None,
                                        compute_op=ALU.add).then_inc(s_scat, 16)
                pool.indirect_dma_start(sums, bass.IndirectOffsetOnAxis(ap=sidx[0:CAPX, 1:2], axis=0), yx_sb, None,
                                        compute_op=ALU.add).then_inc(s_scatx, 16)
                pool.sem_clear(sidx_set)

            for t in range(NT):
                R, b = ROWS[t], t % 2
                pool.wait_ge(s_hx[b], 16 * (t // 2 + 1 + (b == 0)))
                pool.wait_ge(s_hp[b], 16 * (t // 2 + 1))
                pool.tensor_tensor(hx[b][0:R, :], hx[b][0:R, :], hp_r[b][0:R, :], ALU.add).then_inc(h_ready, 1)
            for s in (*s_table, *s_sums):
                pool.wait_ge(s, 16 * (NT // 2 + (s in (s_table[0], s_sums[0]))))
            pool.wait_ge(route_ready, 4)
            def hidden(e, c, first=False):
                if c == 1 and not first:
                    pool.wait_ge(a_dve, e)
                pool.wait_ge(silu_ready, CG * e + c + 1)
                up = gu[c % 2][:, :, 1, :]
                pool.tensor_tensor(act_f[c % 2][:], silu[c % 2][:], up, ALU.mult).then_inc(a_pool, 1)
                pool.tensor_tensor(a_bf[:, 2 * c:2 * c + 2, :], silu[c % 2][:], up, ALU.mult).then_inc(a_pool, 1)
                pool.wait_ge(ahi_ready, CG * e + c + 1)
                pool.tensor_tensor(a_hl[:, 2 * c:2 * c + 2, CAP:2 * CAP], act_f[c % 2][:],
                                   a_hl[:, 2 * c:2 * c + 2, 0:CAP].bitcast(F32), ALU.subtract).then_inc(a_pool, 1)

            def expert(e, n=2, last=False):
                if not last:
                    if n:
                        pool.wait_ge(xg_tr, 3 * e + 3)
                    else:
                        pool.wait_ge(xg_tr, 3)
                    gather(e + 1)
                for c in range(CG - 2):
                    hidden(e, c, first=n == 0)
                if n:
                    scatter(e - 1, n == 1)
                hidden(e, CG - 2)

            gather(0)
            expert(0, 0)
            expert(1, 1)
            with pool.Fori(2, E - 1) as e:
                expert(e)
            expert(E - 1, last=True)
            scatter(E - 1, False)
            pool.wait_ge(s_scat, 16 * E)
            pool.wait_ge(s_scatx, 16 * E)

        @block.scalar
        def _(act):
            act.wait_ge(eps_set, 1)
            def root1(t):
                R = ROWS[t]
                act.wait_ge(var_ready, t + 1)
                act.activation(st[0:R, 2, t:t + 1], st[0:R, 1, t:t + 1], ACT.Sqrt).then_inc(std_ready, 1)

            def take_hT_hi(t):
                R = ROWS[t]
                act.wait_ge(xtr, t + 1)
                act.activation(hT_hi[:, :, P * t:P * t + R],
                               two_banks(2 * (t % 2)).rearrange("p (k r) -> p k r", k=KD)[:, :, 0:R], ACT.Copy
                               ).then_inc(hT_hi_ready, 1)

            for t in range(NT + 2):
                if t < NT:
                    R = ROWS[t]
                    act.wait_ge(s_x[t], 32 if t == 0 else 16)
                    act.activation(two_banks(4 + 2 * (t % 2), R), xt(t)[0:R, :], ACT.Square,
                                   accum_out=st[0:R, 0, t:t + 1]).then_inc(ssq, 1)
                if 1 <= t <= NT:
                    root1(t - 1)
                if t >= 2:
                    take_hT_hi(t - 2)
                n = t - (NT - 4)
                if 0 <= n < 4:
                    act.wait_ge(s_wv, 16)
                    act.activation(w_v_hi[:, 2 * n:2 * n + 2, :], w_v[:, 2 * n:2 * n + 2, :], ACT.Copy).then_inc(wv_hi, 1)

            def cut_block_hi(b):
                act.wait_ge(s_win[b % 2], 16 * (b // 2 + 1))
                act.wait_ge(proj_done, NT if b < 4 else G0 + 3 * (b - 4) + 3)
                act.activation(w_in_hi[b % 4][:], w_raw[b % 2][:], ACT.Copy).then_inc(win_hi, 1)

            def rope_root(i):
                act.wait_ge(ms_done, i + 1)
                if i >= 2:
                    act.wait_ge(qk_ready, i - 1)
                W = WID[i % 3]
                act.activation(rt[i % 2][:, 0:W], PS[:, 4 + i % 2, 0:W], ACT.Sqrt, bias=eps[:, 0:1]).then_inc(rt_ready, 1)

            act.wait_ge(s_par, 16 * 6)
            for t in range(NT):
                act.wait_ge(proj_done, t + 1)
                act.activation(v_hi[0:KEYS[t], t, :], PS[0:KEYS[t], t % 4, :], ACT.Copy).then_inc(proj_taken, 1)
            cut_block_hi(0)
            cut_block_hi(1)
            for n in range(3 * GROUPS):
                i, g, c = G0 + n, GROUP[n // 3], n % 3
                if n % 3 == 0:
                    cut_block_hi(n // 3 + 2)
                act.wait_ge(proj_done, i + 1)
                act.activation(pbuf[:, g, PADW + OFF[c]:PADW + OFF[c] + WID[c]], PS[:, i % 4, 0:WID[c]], ACT.Copy
                               ).then_inc(proj_taken, 1)
            for i in range(6 * HEADS):
                W, bank, b = WID[i % 3], (Q0 + i) % 4, GROUPS + i // 3
                if i % 3 == 0 and b + 2 < BLOCKS:
                    cut_block_hi(b + 2)
                act.wait_ge(proj_done, Q0 + i + 1)
                if i >= 2:
                    act.wait_ge(ms_done, i - 1)
                act.activation(sq[i % 2][:, 0:W], PS[:, bank, 0:W], ACT.Square).then_inc(sq_ready, 1)
                if i >= 3:
                    act.wait_ge(qk_ready, i - 2)
                    act.wait_ge(sw_done, 4 * (i - 2))
                act.activation(qg[i % 3][:, 0:W], PS[:, bank, 0:W], ACT.Identity, scale=gq[:, qk_part(i)[1]:qk_part(i)[1] + 1]
                               ).then_inc(proj_taken, 1)
                if i:
                    rope_root(i - 1)
                if i >= 2:
                    act.wait_ge(qk_ready, i - 1)
                act.wait_ge(proj_taken, Q0 + i + 1)
                half = DH // 2
                for b in range(P // half):
                    src, dst = slice(half * b, half * b + half), slice(half * (b ^ 1), half * (b ^ 1) + half)
                    act.activation(qs_r[i % 2][dst, 0:W], qg[i % 3][src, 0:W], ACT.Copy).then_inc(sw_done, 1)
            rope_root(23)
            act.wait_ge(lam_dot, 2)
            act.activation(lam[:, 2:4], lam[:, 0:2], ACT.Exp).then_inc(lam_exp, 1)

            def exps(s, m):
                R = ROWS[s % NT]
                act.wait_ge(nb_ready, 2 * s + m + 1)
                if m == 0 and s >= 3:
                    act.wait_ge(tr_done, 3 * (s - 2))
                if m == 0 and s >= 2:
                    act.wait_ge(diff_ready, s - 1)
                p = probs_a[s % 3] if m == 0 else probs_b[s % 2]
                act.activation(p[0:R, :].rearrange("p (c t) -> p c t", c=3), PS[0:R, 3 * m:3 * m + 3, 0:CHW], ACT.Exp,
                               bias=nb[0:R, s % 2, m:m + 1], scale=SCALE, accum_out=zs[0:R, s % 2, 0, m:m + 1]
                               ).then_inc(exp_done, 1)

            def scale_map1(s):
                R, b = ROWS[s % NT], s % 2
                act.wait_ge(rl_ready, s + 1)
                act.activation(probs_b[b][0:R, :], probs_b[b][0:R, :], ACT.Copy, scale=rl[0:R, b:b + 1]
                               ).then_inc(map1_ready, 1)

            def take_hi(s, b):
                R, col = ROWS[s % NT], (s % 3) * P
                act.wait_ge(tr_done, 3 * s + b + 1)
                if s % 3 == 0 and s:
                    act.wait_ge(pv_third, s - 3 + b + 1)
                act.activation(aT_hi[:, 3 * b:3 * b + 3, col:col + R],
                               PS[:, 6, 0:3 * P].rearrange("p (n r) -> p n r", n=3)[:, :, 0:R], ACT.Copy).then_inc(tr_hi, 1)

            def take_pv(j):
                h, at = j // 3, 3 * P * (j % 3)
                N = sum(ROWS[3 * (j % 3):3 * (j % 3) + 3])
                act.wait_ge(pv_third, 3 * j + 3)
                act.activation(mixT[:, h, at:at + N], PS[:, 7, 0:N], ACT.Copy).then_inc(b7_taken, 1)

            def take_pool(n):
                g, c = n // 3, n % 3
                act.wait_ge(pool_done, n + 1)
                act.activation(mixT[:, HEADS + g, OFF[c]:OFF[c] + WID[c]], PS[:, 6 + n % 2, 0:WID[c]], ACT.Identity,
                               scale=psc[:, g:g + 1]).then_inc(pool_taken, 1)

            def take_half(n):
                R = ROWS[n // 2]
                act.wait_ge(half_done, n + 1)
                if n:
                    act.wait_ge(s_half, 16 * n)
                act.activation(out_half[0:R, :], PS[0:R, 7, :], ACT.Copy).then_inc(b7_taken, 1)

            def square_o(j):
                at, W = CHUNK3[j // HEADS]
                if j >= 2:
                    act.wait_ge(oms, j - 1)
                act.activation(o_sq[j % 2][:, 0:W], mixT[:, j % HEADS, at:at + W], ACT.Square).then_inc(osq, 1)

            def root_o(j):
                W = CHUNK3[j // HEADS][1]
                act.wait_ge(oms, j + 1)
                if j >= 2:
                    act.wait_ge(o_ready, j - 1)
                act.activation(o_rt[j % 2][:, 0:W], PS[:, o_bank(j), 0:W], ACT.Sqrt, bias=eps[:, 0:1]).then_inc(ort, 1)

            for n in range(4):
                take_pool(n)
            for s in range(TURNS):
                turn = 0 <= s - 2 < STEPS
                for j in early_subln.get(s - 1, ()):
                    root_o(j)
                for j in early_subln.get(s, ()):
                    if j == 0:
                        act.wait_ge(b7_taken, b7_use["pv", 3 * (HEADS - 1)] + 1)
                    square_o(j)
                if s == 1:
                    act.wait_ge(qk_ready, 6 * HEADS)
                if s == 2:
                    for i in (0, 1):
                        act.wait_ge(s_stage[i], 16 * 3 * HEADS)
                if turn:
                    take_hi(s - 2, 0)
                if s < STEPS:
                    exps(s, 0)
                if turn:
                    take_hi(s - 2, 1)
                if 0 <= s - 1 < STEPS:
                    scale_map1(s - 1)
                if s < STEPS:
                    exps(s, 1)
                if s < 2:
                    for n in range(4 * s + 4, 4 * s + 8):
                        take_pool(n)
                if s in half_turns:
                    take_half(half_turns[s])
                if turn:
                    take_hi(s - 2, 2)
                if s % 3 == 2 and s >= 5:
                    take_pv((s - 5) // 3)
            for j in early_subln[STEPS + 2]:
                root_o(j)
            square_o(LATE - 1)
            root_o(LATE - 1)

            act.wait_ge(b7_taken, len(b7_use))
            def take_hn(t):
                R = ROWS[t]
                act.wait_ge(hn_tr, t + 1)
                if t >= 2:
                    act.wait_ge(rout_done, t - 1)
                act.activation(hnT[t % 2][:, :, 0:R], two_banks(4).rearrange("p (k r) -> p k r", k=KD)[:, :, 0:R],
                               ACT.Copy).then_inc(hnT_ready, 1)

            def take_logits(t):
                R = ROWS[t]
                act.wait_ge(rout_done, t + 1)
                act.activation(lgT[:, P * t:P * t + R], PS[0:E, 6, 0:R], ACT.Copy).then_inc(lgT_ready, 1)

            for t in range(NT):
                R, b = ROWS[t], t % 2
                if LATE + t < 3 * HEADS:
                    square_o(LATE + t)
                if t and LATE + t - 1 < 3 * HEADS:
                    root_o(LATE + t - 1)
                if t:
                    take_hn(t - 1)
                act.wait_ge(h2_ready, t + 1)
                if t >= 2:
                    act.wait_ge(s_table[b], 16 * (t // 2))
                    act.wait_ge(hn_tr, t - 1)
                act.activation(hn[b][0:R, :], h2[b][0:R, :], ACT.Square, accum_out=st2[0:R, 0, t:t + 1]).then_inc(ssq2, 1)
                act.wait_ge(var2, t + 1)
                act.activation(st2[0:R, 2, t:t + 1], st2[0:R, 1, t:t + 1], ACT.Sqrt).then_inc(std2, 1)
                if t:
                    take_logits(t - 1)
            take_hn(NT - 1)
            take_logits(NT - 1)
            act.wait_ge(lg_sub, 1)
            act.activation(lg, lg, ACT.Exp).then_inc(lg_exp, 1)

            def cut_hi(e, c, h, first=False):
                if not first:
                    act.wait_ge(tile_done, TILES * e + 2 * (c - CUT) + 2)
                act.wait_ge(s_w[c % RAW][h], 16 * (CH // RAW * e + c // RAW + 1))
                act.activation(w_hi[c % CUT][:, 2048 * h:2048 * h + 2048], raw[c % RAW][:, 2048 * h:2048 * h + 2048],
                               ACT.Copy).then_inc(hi_ready, 1)

            def take_part(e, n):
                act.wait_ge(tile_done, TILES * e + n + 1)
                act.activation(low_sum[n % 2][:], PS[:, 2 * (n % 2):2 * (n % 2) + 2, CAP:2 * CAP], ACT.Copy
                               ).then_inc(part_ready, 1)

            def silus(e, c, first=False):
                if c == 0 and not first:
                    act.wait_ge(a_pool, 3 * (CG - 1) * e)
                elif c == 1 and not first:
                    act.wait_ge(a_dve, e)
                elif c >= 2:
                    act.wait_ge(a_pool, 3 * (CG - 1) * e + 3 * (c - 2) + 3)
                act.wait_ge(gu_ready, 2 * CG * e + 2 * c + 2)
                act.activation(silu[c % 2][:], gu[c % 2][:, :, 0, :], ACT.Silu).then_inc(silu_ready, 1)

            def hidden_hi(e, c):
                if c < CG - 1:
                    act.wait_ge(a_pool, 3 * (CG - 1) * e + 3 * c + 1)
                else:
                    act.wait_ge(a_mul, e + 1)
                act.activation(a_hl[:, 2 * c:2 * c + 2, 0:CAP], act_f[c % 2][:], ACT.Copy).then_inc(ahi_ready, 1)

            def take_ypart(e, t):
                act.wait_ge(tile_done, TILES * e + 2 * CG + t + 1)
                act.activation(ypart[t % 2][:], PS[:, 4 + t % 2, CAP:2 * CAP], ACT.Copy).then_inc(ypart_ready, 1)

            def take_x(e, b):
                n = min(3, KD - 3 * b)
                act.wait_ge(xg_tr, 3 * e + b + 1)
                act.activation(x_hl[:, 3 * b:3 * b + n, 0:CAP],
                               PS[:, 6 + b % 2, 0:n * CAP].rearrange("p (k c) -> p k c", k=n), ACT.Copy
                               ).then_inc(xh_ready, 1)

            def take_y(e, rest, first=False):
                act.wait_ge(y_tr, 2 * e + rest + 1)
                act.wait_ge(gcur_set, 2 * e + 2)
                if not rest:
                    if not first:
                        act.wait_ge(s_scat, 16 * e)
                        act.wait_ge(s_scatx, 16 * e)
                    act.activation(y_sb, two_banks(6), ACT.Identity, scale=gcur[:, 0:1]).then_inc(y_taken, 1)
                else:
                    act.activation(yx_sb, two_banks(6, CAPX), ACT.Identity, scale=gcur[0:CAPX, 1:2]).then_inc(y_taken, 1)

            def expert(e, n=2, last=False):
                for c in range(CH):
                    ahead = not (last and c + 2 >= CH)
                    early = n == 0 and c + 2 < CUT
                    if ahead:
                        cut_hi(e, c + 2, 0, first=early)
                    if c == CG:
                        silus(e, CG - 1, first=n == 0)
                        hidden_hi(e, CG - 1)
                    take_part(e, 2 * c) if c < CG else take_ypart(e, 2 * (c - CG))
                    if 1 <= c < CG:
                        silus(e, c - 1, first=n == 0)
                    if ahead:
                        cut_hi(e, c + 2, 1, first=early)
                    if 1 <= c < CG:
                        hidden_hi(e, c - 1)
                    take_part(e, 2 * c + 1) if c < CG else take_ypart(e, 2 * (c - CG) + 1)
                    if n and c in (2, 4):
                        take_y(e - 1, c == 4, first=n == 1)
                    if not last and c == CG + 1:
                        take_x(e + 1, 0)
                        take_x(e + 1, 1)
                    if not last and c == CG + 2:
                        take_x(e + 1, 2)

            act.wait_ge(wo_done, NT)
            for c in range(2):
                for h in range(2):
                    cut_hi(0, c, h, first=True)
            for b in range(3):
                take_x(0, b)
            expert(0, 0)
            expert(1, 1)
            with act.Fori(2, E - 1) as e:
                expert(e)
            expert(E - 1, last=True)
            take_y(E - 1, 0)
            take_y(E - 1, 1)

        @block.vector
        def _(dve):
            steps = [0]

            def count(ins):
                steps[0] += 1
                ins.then_inc(dve_chain, 1)
                return steps[0]

            def link(ins):
                dve.wait_ge(dve_chain, count(ins))

            def scale_rows(t):
                R = ROWS[t]
                dve.wait_ge(std_ready, t + 1)
                link(dve.reciprocal(st[0:R, 3, t:t + 1], st[0:R, 2, t:t + 1]))
                dve.scalar_tensor_tensor(out=xt(t)[0:R, :], in0=xt(t)[0:R, :], scalar=st[0:R, 3, t:t + 1],
                                         in1=g1[0:R, :], op0=ALU.mult, op1=ALU.mult).then_inc(xs_ready, 1)

            def take_hT_lo(t):
                R = ROWS[t]
                cols = slice(P * t, P * t + R)
                src = two_banks(2 * (t % 2)).rearrange("p (k r) -> p k r", k=KD)[:, :, 0:R]
                dve.wait_ge(hT_hi_ready, t + 1)
                dve.tensor_tensor(hT_lo6[:, :, cols], src[:, 0:6, :], hT_hi[:, 0:6, cols].bitcast(F32), ALU.subtract
                                  ).then_inc(hT_ready, 1)
                dve.tensor_tensor(hT_lo2[:, :, cols], src[:, 6:8, :], hT_hi[:, 6:8, cols].bitcast(F32), ALU.subtract
                                  ).then_inc(hT_ready, 1)

            for t in range(NT + 2):
                if t < NT:
                    R = ROWS[t]
                    dve.wait_ge(ssq, t + 1)
                    dve.tensor_scalar(st[0:R, 1, t:t + 1], st[0:R, 0, t:t + 1], 1.0 / D, EPS, ALU.mult, ALU.add
                                      ).then_inc(var_ready, 1)
                if 1 <= t <= NT:
                    scale_rows(t - 1)
                if t == 0:
                    dve.wait_ge(s_g1, 16)
                if t >= 2:
                    take_hT_lo(t - 2)
                n = t - NT + 2
                if t >= NT:
                    dve.wait_ge(wv_hi, n + 1)
                    dve.tensor_tensor(w_v_lo[:, 2 * n:2 * n + 2, :], w_v[:, 2 * n:2 * n + 2, :],
                                      w_v_hi[:, 2 * n:2 * n + 2, :].bitcast(F32), ALU.subtract).then_inc(wv_lo, 1)

            def cut_block_lo(b):
                dve.wait_ge(win_hi, b + 1)
                dve.tensor_tensor(w_in_lo[b % 4][:], w_raw[b % 2][:], w_in_hi[b % 4][:].bitcast(F32), ALU.subtract
                                  ).then_inc(win_lo, 1)

            for t in range(NT):
                R = KEYS[t]
                dve.wait_ge(proj_taken, t + 1)
                dve.tensor_tensor(v_lo[0:R, t, :], PS[0:R, t % 4, :], v_hi[0:R, t, :].bitcast(F32), ALU.subtract
                                  ).then_inc(v_lo_ready, 1)

            def pool_diff(j):
                g = GROUP[j]
                w, last = WINDOWS[g], lev[g % 2]
                dve.wait_ge(win_ready, j + 1)
                for a, b in ((PADW, 0), (PADW + L - 8, 8)):
                    link(dve.tensor_tensor(last[:, a:a + 8], last[:, a:a + 8], edge[:, g, b:b + 8], ALU.mult))
                dve.scalar_tensor_tensor(out=pbuf[:, g, PADW:PADW + L], in0=last[:, PADW:PADW + L], scalar=1.0 / w,
                                         in1=pbuf[:, g, PADW:PADW + L], op0=ALU.mult, op1=ALU.subtract
                                         ).then_inc(pool_d, 1)

            cut_block_lo(0)
            cut_block_lo(1)
            cut_block_lo(2)
            for j in range(GROUPS):
                if j + 3 < GROUPS + 2:
                    cut_block_lo(j + 3)
                pool_diff(j)

            dve.wait_ge(s_par, 16 * 6)
            dve.wait_ge(s_lam, 64)
            for m in range(2):
                ins = dve.tensor_tensor_reduce(lamj[:], lamv[:, 2 * m, :], lamv[:, 2 * m + 1, :], 1.0, 0.0,
                                               ALU.mult, ALU.add, lam[:, m:m + 1])
                ins.then_inc(lam_dot, 1)
                dve.wait_ge(lam_dot, m + 1)
            dve.tensor_scalar(sg[:, 1:2], sg[:, 0:1], 1.0 - LAM_INIT, None, ALU.mult)

            dve.wait_ge(s_trig, 16)
            for i in range(6 * HEADS):
                W = WID[i % 3]
                at = slice(OFF[i % 3], OFF[i % 3] + W)
                if i % 3 == 0 and GROUPS + i // 3 + 2 < BLOCKS:
                    cut_block_lo(GROUPS + i // 3 + 2)
                dve.wait_ge(sw_done, 4 * i + 4)
                dve.wait_ge(cos_ready, i + 1)
                if i:
                    dve.wait_ge(hi_staged, i)
                link(dve.tensor_tensor(tb[:, 0:W], qs_r[i % 2][:, 0:W], sinT[:, at], ALU.mult))
                dve.wait_ge(rt_ready, i + 1)
                count(dve.tensor_tensor(ta[i % 2][:, 0:W], ta[i % 2][:, 0:W], tb[:, 0:W], ALU.add))
                link(dve.reciprocal(rt[i % 2][:, 0:W], rt[i % 2][:, 0:W]))
                if i >= 2:
                    dve.wait_ge(s_stage[i % 2], 16 * (i // 2))
                dve.tensor_tensor(stage[i % 2][:, 0, 0:W], ta[i % 2][:, 0:W], rt[i % 2][:, 0:W], ALU.mult
                                  ).then_inc(hi_staged, 1)

            dve.wait_ge(lam_exp, 1)
            link(dve.tensor_tensor(lam[:, 4:5], lam[:, 2:3], lam[:, 3:4], ALU.subtract))
            link(dve.tensor_scalar(lam[:, 4:5], lam[:, 4:5], LAM_INIT, None, ALU.add))

            def row_max(s, m):
                R = ROWS[s % NT]
                dve.wait_ge(scores, 2 * s + m + 1)
                return count(dve.tensor_reduce(mx[0:R, s % 2, m:m + 1], PS[0:R, 3 * m:3 * m + 3, 0:CHW], AX.XY, ALU.max))

            def exp_bias(s, m, max_done):
                R, b = ROWS[s % NT], s % 2
                dve.wait_ge(dve_chain, max_done)
                dve.tensor_scalar(nb[0:R, b, m:m + 1], mx[0:R, b, m:m + 1], -SCALE, None, ALU.mult).then_inc(nb_ready, 1)

            def twice_counted(s):
                R, b = ROWS[s % NT], s % 2
                dve.wait_ge(exp_done, 2 * s + 2)
                for m, p in enumerate((probs_a[s % 3], probs_b[b])):
                    twice = p[0:R, :].rearrange("p (c t) -> p c t", c=3)[:, 1:3, 0:2]
                    done = count(dve.tensor_reduce(zs[0:R, b, 1, m:m + 1], twice, AX.XY, ALU.add))
                return done

            def row_sums(s, twice_done):
                R, b = ROWS[s % NT], s % 2
                dve.wait_ge(dve_chain, twice_done)
                link(dve.tensor_tensor(zs[0:R, b, 2, :], zs[0:R, b, 0, :], zs[0:R, b, 1, :], ALU.subtract))
                return count(dve.reciprocal(zs[0:R, b, 3, :], zs[0:R, b, 2, :]))

            def map1_factor(s, recip_done):
                R, b = ROWS[s % NT], s % 2
                dve.wait_ge(dve_chain, recip_done)
                dve.tensor_tensor(rl[0:R, b:b + 1], zs[0:R, b, 3, 1:2], lam[0:R, 4:5], ALU.mult).then_inc(rl_ready, 1)

            def difference(s):
                R, b = ROWS[s % NT], s % 2
                dve.wait_ge(map1_ready, s + 1)
                dve.scalar_tensor_tensor(out=probs_a[s % 3][0:R, :], in0=probs_a[s % 3][0:R, :],
                                         scalar=zs[0:R, b, 3, 0:1], in1=probs_b[b][0:R, :],
                                         op0=ALU.mult, op1=ALU.subtract).then_inc(diff_ready, 1)

            def take_lo(s, b):
                R, col = ROWS[s % NT], (s % 3) * P
                dve.wait_ge(tr_hi, 3 * s + b + 1)
                dve.tensor_tensor(aT_lo[:, 3 * b:3 * b + 3, col:col + R],
                                  PS[:, 6, 0:3 * P].rearrange("p (n r) -> p n r", n=3)[:, :, 0:R],
                                  aT_hi[:, 3 * b:3 * b + 3, col:col + R].bitcast(F32), ALU.subtract).then_inc(tr_lo, 1)

            def scale_o(j):
                at, W = CHUNK3[j // HEADS]
                o = mixT[:, j % HEADS, at:at + W]
                dve.wait_ge(ort, j + 1)
                link(dve.reciprocal(o_rt[j % 2][:, 0:W], o_rt[j % 2][:, 0:W]))
                dve.scalar_tensor_tensor(out=o, in0=o, scalar=sg[:, 1:2], in1=o_rt[j % 2][:, 0:W],
                                         op0=ALU.mult, op1=ALU.mult).then_inc(o_ready, 1)

            for s in range(TURNS):
                new, last, turn = s < STEPS, 0 <= s - 1 < STEPS, 0 <= s - 2 < STEPS
                if new:
                    max_done = row_max(s, 0)
                if last:
                    twice_done = twice_counted(s - 1)
                if new:
                    exp_bias(s, 0, max_done)
                if last:
                    recip_done = row_sums(s - 1, twice_done)
                if s == STEPS + 1:
                    scale_o(0)
                if turn:
                    take_lo(s - 2, 0)
                if last:
                    map1_factor(s - 1, recip_done)
                if new:
                    exp_bias(s, 1, row_max(s, 1))
                if turn:
                    take_lo(s - 2, 1)
                if last:
                    difference(s - 1)
                if turn:
                    take_lo(s - 2, 2)
                for j in early_subln.get(s - 1, ()):
                    if j:
                        scale_o(j)
            for j in (*early_subln[STEPS + 2], LATE - 1):
                scale_o(j)

            dve.memset(lgT[:, L:NT * P], 0.0).then_inc(pad_set, 1)
            dve.wait_ge(s_g2, 16)
            for t in range(NT):
                R, b = ROWS[t], t % 2
                if t and LATE + t - 1 < 3 * HEADS:
                    scale_o(LATE + t - 1)
                dve.wait_ge(wo_done, t + 1)
                dve.wait_ge(h_ready, t + 1)
                if t >= 2:
                    dve.wait_ge(s_sums[b], 16 * (t // 2))
                dve.tensor_tensor(h2[b][0:R, :], two_banks(2 * b, R), hx[b][0:R, :], ALU.add).then_inc(h2_ready, 1)
                dve.wait_ge(ssq2, t + 1)
                dve.tensor_scalar(st2[0:R, 1, t:t + 1], st2[0:R, 0, t:t + 1], 1.0 / D, EPS, ALU.mult, ALU.add
                                  ).then_inc(var2, 1)
                dve.wait_ge(std2, t + 1)
                link(dve.reciprocal(st2[0:R, 3, t:t + 1], st2[0:R, 2, t:t + 1]))
                dve.scalar_tensor_tensor(out=hn[b][0:R, :], in0=h2[b][0:R, :], scalar=st2[0:R, 3, t:t + 1],
                                         in1=g2[0:R, :], op0=ALU.mult, op1=ALU.mult).then_inc(hn_ready, 1)

            dve.wait_ge(lg_tr, 1)
            lp = PS[:, 7, 0:NT * E].rearrange("p (t e) -> p t e", t=NT)
            link(dve.tensor_reduce(sm[:, 0, :], lp, AX.X, ALU.max))
            dve.tensor_tensor(lg, lp, sm[:, 0, :].unsqueeze(2).broadcast_to([P, NT, E]), ALU.subtract).then_inc(lg_sub, 1)
            dve.wait_ge(lg_exp, 1)
            link(dve.tensor_reduce(sm[:, 1, :], lg, AX.X, ALU.add))
            link(dve.reciprocal(sm[:, 2, :], sm[:, 1, :]))
            dve.tensor_tensor(lg, lg, sm[:, 2, :].unsqueeze(2).broadcast_to([P, NT, E]), ALU.mult).then_inc(aff_ready, 1)
            dve.wait_ge(aff_tr, 1)
            link(dve.tensor_copy(affT, PS[0:E, 0:3, :].rearrange("p b n -> p (b n)")[:, 0:L]))
            for r in range(ROUNDS):
                best = mv[:, 8 * r:8 * r + 8]
                link(dve.max(best, affT))
                link(dve.max_index(mi[:, 8 * r:8 * r + 8], best, affT))
                if r < ROUNDS - 1:
                    link(dve.match_replace(affT, best, affT, -1.0))
            dve.tensor_copy(mif, mi).then_inc(ids_ready, 1)
            dve.wait_ge(ids_tr, 1)
            for n, (dst, rows) in enumerate(((idx[:, 0, :], P), (gat[:, 0, :], P), (idx[0:CAPX, 1, :], CAPX),
                                             (gat[0:CAPX, 1, :], CAPX))):
                dve.tensor_copy(dst, PS[0:rows, 4, n * E:(n + 1) * E]).then_inc(route_ready, 1)

            def cut_lo(e, c, h):
                cols = slice(2048 * h, 2048 * h + 2048)
                dve.wait_ge(hi_ready, TILES * e + 2 * c + h + 1)
                dve.tensor_tensor(w_lo[c % CUT][:, cols], raw[c % RAW][:, cols], w_hi[c % CUT][:, cols].bitcast(F32),
                                  ALU.subtract).then_inc(lo_ready, 1)

            def sum_gu(e, n, first=False):
                c = n // 2
                if n == 0 and not first:
                    dve.wait_ge(a_pool, 3 * (CG - 1) * e)
                elif n == 2 and not first:
                    dve.wait_ge(a_dve, e)
                elif n % 2 == 0 and n >= 4:
                    dve.wait_ge(a_pool, 3 * (CG - 1) * e + 3 * (c - 2) + 3)
                dve.wait_ge(part_ready, 2 * CG * e + n + 1)
                dve.tensor_tensor(gu[c % 2][:, n % 2, :, :], PS[:, 2 * (n % 2):2 * (n % 2) + 2, 0:CAP], low_sum[n % 2][:],
                                  ALU.add).then_inc(gu_ready, 1)

            def last_hidden(e):
                c = CG - 1
                dve.wait_ge(a_pool, 3 * (CG - 1) * e + 3 * (c - 2) + 3)
                dve.wait_ge(silu_ready, CG * e + c + 1)
                up = gu[c % 2][:, :, 1, :]
                dve.tensor_tensor(act_f[c % 2][:], silu[c % 2][:], up, ALU.mult).then_inc(a_mul, 1)
                dve.tensor_tensor(a_bf[:, 2 * c:2 * c + 2, :], silu[c % 2][:], up, ALU.mult)
                dve.wait_ge(ahi_ready, CG * e + c + 1)
                dve.tensor_tensor(a_hl[:, 2 * c:2 * c + 2, CAP:2 * CAP], act_f[c % 2][:],
                                  a_hl[:, 2 * c:2 * c + 2, 0:CAP].bitcast(F32), ALU.subtract).then_inc(a_dve, 1)

            def sum_y(e, t, first=False):
                if t == 0 and not first:
                    dve.wait_ge(y_tr, 2 * e)
                dve.wait_ge(ypart_ready, KD * e + t + 1)
                dve.tensor_tensor(yT[:, t, :], PS[:, 4 + t % 2, 0:CAP], ypart[t % 2][:], ALU.add).then_inc(y_ready, 1)

            def take_x(e, b):
                n = min(3, KD - 3 * b)
                ks = slice(3 * b, 3 * b + n)
                src = PS[:, 6 + b % 2, 0:n * CAP].rearrange("p (k c) -> p k c", k=n)
                dve.wait_ge(xh_ready, 3 * e + b + 1)
                dve.tensor_tensor(x_hl[:, ks, CAP:2 * CAP], src, x_hl[:, ks, 0:CAP].bitcast(F32), ALU.subtract
                                  ).then_inc(xl_ready, 1)
                dve.tensor_copy(x_bf[:, ks, :], src).then_inc(xl_ready, 1)

            def set_gates(e, first=False):
                if not first:
                    dve.wait_ge(y_taken, 2 * e)
                dve.tensor_copy(gcur[:, 0:1], gat[:, 0, bass.ds(e, 1)]).then_inc(gcur_set, 1)
                dve.tensor_copy(gcur[0:CAPX, 1:2], gat[0:CAPX, 1, bass.ds(e, 1)]).then_inc(gcur_set, 1)

            def expert(e, n=2, last=False):
                for c in range(CH):
                    ahead = not (last and c + 2 >= CH)
                    if c == CG:
                        last_hidden(e)
                    if ahead:
                        cut_lo(e, c + 2, 0)
                    sum_gu(e, 2 * c, n == 0) if c < CG else sum_y(e, 2 * (c - CG), n == 0)
                    if ahead:
                        cut_lo(e, c + 2, 1)
                    sum_gu(e, 2 * c + 1, n == 0) if c < CG else sum_y(e, 2 * (c - CG) + 1, n == 0)
                    if n and c == 0:
                        set_gates(e - 1, n == 1)
                    if not last and c == CG + 1:
                        take_x(e + 1, 0)
                        take_x(e + 1, 1)
                    if not last and c == CG + 2:
                        take_x(e + 1, 2)

            for c in range(2):
                for h in range(2):
                    cut_lo(0, c, h)
            for b in range(3):
                take_x(0, b)
            expert(0, 0)
            expert(1, 1)
            with dve.Fori(2, E - 1) as e:
                expert(e)
            expert(E - 1, last=True)
            set_gates(E - 1)

        @block.tensor
        def _(pe):
            pe.wait_ge(s_cst, 16)
            for t in range(NT):
                R = ROWS[t]
                pe.wait_ge(xs_ready, t + 1)
                if t >= 2:
                    pe.wait_ge(hT_ready, 2 * (t - 1))
                for k in range(KD):
                    ins = pe.transpose(PS[:, 2 * (t % 2) + k // 4, (k % 4) * P:(k % 4) * P + R],
                                       xt(t)[0:R, k * P:(k + 1) * P], ident[0:R, 0:R])
                ins.then_inc(xtr, 1)

            def stats(i):
                W = WID[i % 3]
                pe.wait_ge(sq_ready, i + 1)
                if i >= 2:
                    pe.wait_ge(rt_ready, i - 1)
                pe.matmul(PS[:, 4 + i % 2, 0:W], blk_mean, sq[i % 2][:, 0:W], start=True, stop=True).then_inc(ms_done, 1)

            def bank_free(i):
                if i >= 4:
                    pe.wait_ge(proj_taken, i - 3)
                    if i - 4 < NT:
                        pe.wait_ge(v_lo_ready, i - 3)

            pe.wait_ge(hT_ready, 2 * NT)
            for t in range(NT):
                R = KEYS[t]
                toks = slice(KEY0[t], KEY0[t] + R)
                bank_free(t)
                for k in range(KD):
                    if t == 0 and k in (0, 4):
                        pe.wait_ge(wv_lo if k else wv_lo_pool, 2)
                    for n, (h, w) in enumerate(((hT_hi[:, k, toks], w_v_hi), (hT_hi[:, k, toks], w_v_lo),
                                                (hT_lo(k)[:, toks], w_v_hi))):
                        ins = pe.matmul(PS[0:R, t % 4, :], h, w[:, k, :], start=k == 0 and n == 0,
                                        stop=k == KD - 1 and n == 2)
                ins.then_inc(proj_done, 1)

            def block_item(i):
                b, c = (i - G0) // 3, (i - G0) % 3
                toks = slice(OFF[c], OFF[c] + WID[c])
                if c == 0:
                    pe.wait_ge(win_lo, b + 1)
                bank_free(i)
                for k in range(KD):
                    hi, lo = w_in_hi[b % 4][:, k, :], w_in_lo[b % 4][:, k, :]
                    for n, (w, h) in enumerate(((hi, hT_hi[:, k, toks]), (hi, hT_lo(k)[:, toks]),
                                                (lo, hT_hi[:, k, toks]))):
                        ins = pe.matmul(PS[:, i % 4, 0:WID[c]], w, h, start=k == 0 and n == 0,
                                        stop=k == KD - 1 and n == 2)
                ins.then_inc(proj_done, 1)

            pe.wait_ge(pads_set, 2 * GROUPS)
            for i in range(G0, Q0):
                block_item(i)
            for i in range(6 * HEADS):
                block_item(Q0 + i)
                if i:
                    stats(i - 1)
            stats(6 * HEADS - 1)

            def score(s, m):
                h, q = s // NT, s % NT
                R, b = ROWS[q], (s // NT) % 2
                if q == 0 and m == 0:
                    pe.wait_ge(s_stk[b], 16 * 6 * (h // 2 + 1))
                if s:
                    pe.wait_ge(exp_done, 2 * (s - 1) + m + 1)
                for c in range(3):
                    for n in range(2):
                        ins = pe.matmul(PS[0:R, 3 * m + c, 0:CHW], stk[b][:, m, n, P * q:P * q + R],
                                        stk[b][:, m, 2, CHS * c:CHS * c + CHW], start=n == 0, stop=n == 1)
                ins.then_inc(scores, 1)

            def transposes(s, b):
                R = ROWS[s % NT]
                if b == 0:
                    pe.wait_ge(diff_ready, s + 1)
                if s or b:
                    pe.wait_ge(tr_lo, 3 * s + b)
                for kt in range(3 * b, 3 * b + 3):
                    n = min(P, LS - KPOS[kt])
                    ins = pe.transpose(PS[0:n, 6, (kt % 3) * P:(kt % 3) * P + R],
                                       probs_a[s % 3][0:R, KPOS[kt]:KPOS[kt] + n], ident[0:R, 0:R])
                ins.then_inc(tr_done, 1)

            def bank7_free(use):
                if b7_use[use]:
                    pe.wait_ge(b7_taken, b7_use[use])

            def pv(j, b):
                h, N = j // 3, sum(ROWS[3 * (j % 3):3 * (j % 3) + 3])
                if b == 0:
                    bank7_free(("pv", j))
                pe.wait_ge(tr_lo, 3 * (3 * j + 2) + b + 1)
                for kt in range(3 * b, 3 * b + 3):
                    KR = KEYS[kt]
                    for n, (v, a) in enumerate(((v_hi, aT_hi), (v_hi, aT_lo), (v_lo, aT_hi))):
                        ins = pe.matmul(PS[:, 7, 0:N], v[0:KR, kt, DV * h:DV * h + DV], a[0:KR, kt, 0:N],
                                        start=kt == 0 and n == 0, stop=kt == NT - 1 and n == 2)
                ins.then_inc(pv_third, 1)

            def pool_product(n):
                g, c = n // 3, n % 3
                if n >= 2:
                    pe.wait_ge(pool_taken, n - 1)
                pe.wait_ge(pool_d, GROUPS)
                pe.matmul(PS[:, 6 + n % 2, 0:WID[c]], poolw[:, g, :], pbuf[:, g, PADW + OFF[c]:PADW + OFF[c] + WID[c]],
                          start=True, stop=True).then_inc(pool_done, 1)

            def half_product(n, ks):
                t, half = n // 2, n % 2
                if ks[0] == HEADS:
                    bank7_free(("half", n))
                    if n < 2:
                        pe.wait_ge(s_wout[half], 16)
                for k in ks:
                    ins = pe.matmul(PS[0:ROWS[t], 7, :], mixT[:, k, P * t:P * t + ROWS[t]], w_out_sb[half][:, k, :],
                                    start=k == HEADS, stop=k == KD - 1)
                if ks[-1] == KD - 1:
                    ins.then_inc(half_done, 1)

            def mean_o(j):
                W = CHUNK3[j // HEADS][1]
                pe.wait_ge(osq, j + 1)
                if j == 6 or j > LATE:
                    pe.wait_ge(ort, j)
                pe.matmul(PS[:, o_bank(j), 0:W], dv_mean, o_sq[j % 2][:, 0:W], start=True, stop=True).then_inc(oms, 1)

            pe.wait_ge(s_small, 32)
            pe.wait_ge(proj_taken, ITEMS)
            pe.wait_ge(rt_ready, 6 * HEADS)
            score(0, 0)
            score(0, 1)
            for n in range(4):
                pool_product(n)
            for s in range(TURNS):
                turn = 0 <= s - 2 < STEPS
                if s == 2:
                    pe.wait_ge(pool_taken, 3 * GROUPS)
                if turn:
                    transposes(s - 2, 0)
                if s % 3 == 2 and s >= 5:
                    pv((s - 5) // 3, 1)
                if s in half_turns:
                    half_product(half_turns[s], (4, 5))
                if turn:
                    transposes(s - 2, 1)
                if s % 3 == 2 and s >= 5:
                    pv((s - 5) // 3, 2)
                if s in half_turns:
                    half_product(half_turns[s], (6, 7))
                if turn:
                    transposes(s - 2, 2)
                if s + 1 < STEPS:
                    score(s + 1, 0)
                    score(s + 1, 1)
                if s < 2:
                    for n in range(4 * s + 4, 4 * s + 8):
                        pool_product(n)
                if s % 3 == 1 and s >= 4:
                    pv((s - 4) // 3, 0)
                for j in early_subln.get(s, ()):
                    if j == 0:
                        pe.wait_ge(exp_done, 2 * STEPS)
                    mean_o(j)
            mean_o(LATE - 1)
            pe.wait_ge(b7_taken, len(b7_use))

            def hn_transposes(t):
                R = ROWS[t]
                pe.wait_ge(hn_ready, t + 1)
                if t:
                    pe.wait_ge(hnT_ready, t)
                for k in range(KD):
                    ins = pe.transpose(PS[:, 4 + k // 4, (k % 4) * P:(k % 4) * P + R],
                                       hn[t % 2][0:R, k * P:(k + 1) * P], ident[0:R, 0:R])
                ins.then_inc(hn_tr, 1)

            def router(t):
                R = ROWS[t]
                pe.wait_ge(hnT_ready, t + 1)
                if t:
                    pe.wait_ge(lgT_ready, t)
                for k in range(KD):
                    ins = pe.matmul(PS[0:E, 6, 0:R], wr[:, k, :], hnT[t % 2][:, k, 0:R], start=k == 0, stop=k == KD - 1)
                ins.then_inc(rout_done, 1)

            for t in range(NT):
                R = ROWS[t]
                pe.wait_ge(o_ready, HEADS * (t // 3 + 1))
                if t == 0:
                    pe.wait_ge(ort, LATE)
                if t >= 2:
                    pe.wait_ge(h2_ready, t - 1)
                for half in range(2):
                    for k in range(HEADS):
                        ins = pe.matmul(PS[0:R, 2 * (t % 2) + half, :], mixT[:, k, P * t:P * t + R],
                                        w_out_sb[half][:, k, :], start=k == 0, stop=k == HEADS - 1)
                    if half == 0 and t:
                        hn_transposes(t - 1)
                ins.then_inc(wo_done, 1)
                if t:
                    router(t - 1)
                if LATE + t < 3 * HEADS:
                    mean_o(LATE + t)
            hn_transposes(NT - 1)
            router(NT - 1)
            pe.wait_ge(lgT_ready, NT)
            pe.wait_ge(pad_set, 1)
            for t in range(NT):
                ins = pe.transpose(PS[:, 7, t * E:(t + 1) * E], lgT[:, P * t:P * t + P], ident[0:E, 0:E])
            ins.then_inc(lg_tr, 1)
            pe.wait_ge(h2_ready, NT)
            pe.wait_ge(aff_ready, 1)
            for t in range(NT):
                ins = pe.transpose(PS[0:E, t // 4, (t % 4) * P:(t % 4) * P + P], lg[:, t, :], ident)
            ins.then_inc(aff_tr, 1)
            pe.wait_ge(ids_ready, 1)
            for n, (src, at, rows) in enumerate(((mif, 0, P), (mv, 0, P), (mif, P, CAPX), (mv, P, CAPX))):
                ins = pe.transpose(PS[0:rows, 4, n * E:(n + 1) * E], src[:, at:at + rows], ident[0:E, 0:E])
            ins.then_inc(ids_tr, 1)

            def x_transposes(e, b, first=False):
                if b == 0:
                    pe.wait_ge(s_gath, 16 * e + 16)
                    pe.wait_ge(s_gathx, 16 * e + 16)
                    if not first:
                        pe.wait_ge(y_taken, 2 * e - 2)
                if b == 2:
                    pe.wait_ge(xl_ready, 6 * e + 2)
                for k in range(3 * b, min(3 * b + 3, KD)):
                    to = (k % 3) * CAP
                    pe.transpose(PS[:, 6 + b % 2, to:to + P], xg[:, k * P:(k + 1) * P], ident)
                    ins = pe.transpose(PS[:, 6 + b % 2, to + P:to + CAP], xgx[:, k * P:(k + 1) * P],
                                       ident[0:CAPX, 0:CAPX])
                ins.then_inc(xg_tr, 1)

            def gate_up(e, n, early=False):
                c, f = n // 2, n % 2
                if n == 0:
                    pe.wait_ge(xl_ready, 6 * e + 6)
                if f == 0:
                    pe.wait_ge(lo_ready, TILES * e + 2 * c + 2)
                if not early:
                    pe.wait_ge(gu_ready, 2 * CG * e + n - 1)
                for h in range(2):
                    bank = 2 * f + h
                    hi, lo = (w[c % CUT][:, 2048 * h:2048 * h + 2048].rearrange("p (k n) -> p k n", k=KD)
                              for w in (w_hi, w_lo))
                    for k in range(KD):
                        pe.matmul(PS[:, bank, 0:2 * CAP], hi[:, k, f * P:(f + 1) * P], x_hl[:, k, :],
                                  start=k == 0, stop=False, skip_group_check=True)
                    for k in range(KD):
                        ins = pe.matmul(PS[:, bank, 0:CAP], lo[:, k, f * P:(f + 1) * P], x_bf[:, k, :],
                                        start=False, stop=k == KD - 1, skip_group_check=True)
                ins.then_inc(tile_done, 1)

            def down(e, t, ks, early=False):
                c, f0 = CG + t // 2, (t % 2) * P
                if ks[0] == 0:
                    if t % 2 == 0:
                        pe.wait_ge(lo_ready, TILES * e + 2 * c + 2)
                    if t == 0:
                        pe.wait_ge(a_pool, 3 * (CG - 1) * e + 3 * (CG - 1))
                    if not early:
                        pe.wait_ge(y_ready, KD * e + t - 1)
                elif t == 0:
                    pe.wait_ge(a_dve, e + 1)
                hi, lo = (w[c % CUT][:, :].rearrange("p (k n) -> p k n", k=FT) for w in (w_hi, w_lo))
                for k in ks:
                    pe.matmul(PS[:, 4 + t % 2, 0:2 * CAP], hi[:, k, f0:f0 + P], a_hl[:, k, :],
                              start=k == 0, stop=False, skip_group_check=True)
                for k in ks:
                    ins = pe.matmul(PS[:, 4 + t % 2, 0:CAP], lo[:, k, f0:f0 + P], a_bf[:, k, :],
                                    start=False, stop=k == FT - 1, skip_group_check=True)
                if ks[-1] == FT - 1:
                    ins.then_inc(tile_done, 1)

            def y_transposes(e, rest, last=False):
                if rest:
                    pe.wait_ge(y_taken, 2 * e + 1)
                else:
                    pe.wait_ge(y_ready, KD * e + KD)
                    if not last:
                        pe.wait_ge(xl_ready, 6 * e + 12)
                for d in range(KD):
                    src = yT[:, d, P:CAP] if rest else yT[:, d, 0:P]
                    ins = pe.transpose(PS[0:CAPX if rest else P, 6 + d // 4, (d % 4) * P:(d % 4) * P + P], src, ident)
                ins.then_inc(y_tr, 1)

            def expert(e, first=False, last=False):
                for n in range(2 * CG):
                    gate_up(e, n, early=first and n < 2)
                    if not first and n in (3, 7):
                        y_transposes(e - 1, n == 7)
                for ks in (range(FT - 2), range(FT - 2, FT)):
                    for t in range(2):
                        down(e, t, ks, early=first)
                for t in range(1, KD):
                    if t > 1:
                        down(e, t, range(FT))
                    if not last and t == 1:
                        x_transposes(e + 1, 0, first)
                        x_transposes(e + 1, 1)
                    if not last and t == 3:
                        x_transposes(e + 1, 2)

            pe.wait_ge(route_ready, 4)
            for b in range(3):
                x_transposes(0, b, True)
            expert(0, first=True)
            with pe.Fori(1, E - 1) as e:
                expert(e)
            expert(E - 1, last=True)
            y_transposes(E - 1, 0, last=True)
            y_transposes(E - 1, 1)


_INS = ["x", "meta_tokens", "ln1_g", "w_in", "q_norm_g", "k_norm_g", "lambda_q1", "lambda_k1", "lambda_q2",
        "lambda_k2", "subln_g", "pool_w", "pool_scale", "w_out", "ln2_g", "w_router", "w_gate", "w_up", "w_down"]


def kernel(**inputs):
    import numpy as _np
    import concourse.bacc as _bacc
    from concourse import mybir as _mybir
    from concourse.bass_utils import run_bass_kernel_spmd as _run

    nc = _bacc.Bacc("TRN2", target_bir_lowering=False, num_devices=1)
    arrays = {f"in_{n}": _np.ascontiguousarray(inputs[n]) for n in _INS}
    arrays["in_consts"] = constants()
    args = [nc.dram_tensor(n, a.shape, _mybir.dt.from_np(a.dtype), kind="ExternalInput").ap()
            for n, a in arrays.items()]
    out = nc.dram_tensor("out_0", (1, SEQ, D), _mybir.dt.float32, kind="ExternalOutput").ap()
    block_kernel(nc, *args, out)
    r = _run(nc, [arrays], core_ids=[0])
    return r.results[0]["out_0"]
```
